# Optimizing a Trainium2 kernel written in Bass

```python
import math
import jax, jax.numpy as jnp
from jax import lax
import numpy as np

D_MODEL = 1024
BATCH = 1
SEQ = 256
DEPTH = 2
DEC_BATCH = 8
DEC_SEQ = 1
PAST_LEN = 2048
PAGE_SIZE = 128

N_META = 16
D_A = D_MODEL // 2
S5_GROUP = 16
S5_GROUPS = D_A // S5_GROUP
S5_STATE = 64
DT_MIN = 1e-3
DT_MAX = 1e-1
D_B = D_MODEL // 2
RW_HEAD = 64
RW_HEADS = D_B // RW_HEAD
LORA_W = 64
LORA_A = 64
LORA_G = 128
GN_EPS = 64e-5
P_RW = 3 * D_B + LORA_W + LORA_A + LORA_G
P_IN = D_A + P_RW + 2 * D_MODEL
D_FF = 2816
N_EXPERTS = 8
TOP_K = 2
D_EXPERT = 3584
N_DENSE = (DEPTH + 1) // 2
N_MOE = DEPTH // 2
RMS_EPS = 1e-6

kernel_name = 'hybrid_gated_s5_rwkv7_moe_step'

def rmsnorm(x, g):
    xf = x.astype(jnp.float32)
    y = xf * lax.rsqrt(jnp.mean(xf * xf, axis=-1, keepdims=True) + RMS_EPS)
    return (y * g.astype(jnp.float32)).astype(x.dtype)

def swiglu(h, w1, w3, w2):
    return (jax.nn.silu(h @ w1) * (h @ w3)) @ w2

def moe_ffn(h, w_router, w1, w3, w2):
    logits = (h @ w_router).astype(jnp.float32)
    top_v, top_i = lax.top_k(logits, TOP_K)
    gates = jax.nn.softmax(top_v, axis=-1)
    combine = jnp.sum(jax.nn.one_hot(top_i, N_EXPERTS, dtype=jnp.float32) * gates[..., None], axis=-2)
    combine = combine.astype(h.dtype)
    out = jnp.zeros_like(h)
    for e in range(N_EXPERTS):
        out = out + combine[..., e:e + 1] * swiglu(h, w1[e], w3[e], w2[e])
    return out

def _cplx_affine_combine(e1, e2):
    a1r, a1i, b1r, b1i = e1
    a2r, a2i, b2r, b2i = e2
    return (a1r * a2r - a1i * a2i,
            a1r * a2i + a1i * a2r,
            a2r * b1r - a2i * b1i + b2r,
            a2r * b1i + a2i * b1r + b2i)

def s5_branch(u, x0_re, x0_im, lam_re, lam_im, log_dt, b_re, b_im, c_re, c_im, d_skip, w_glu1, w_glu2):
    f32 = jnp.float32
    bsz, t_len, _ = u.shape
    uf = u.astype(f32).reshape(bsz, t_len, S5_GROUPS, S5_GROUP)
    lr = lam_re.astype(f32)
    li = lam_im.astype(f32)
    dt = jnp.exp(log_dt.astype(f32))[:, None]
    mag = jnp.exp(lr * dt)
    ab_re = mag * jnp.cos(li * dt)
    ab_im = mag * jnp.sin(li * dt)
    den = lr * lr + li * li
    q_re = ((ab_re - 1.0) * lr + ab_im * li) / den
    q_im = (ab_im * lr - (ab_re - 1.0) * li) / den
    bu_re = jnp.einsum('btgc,gpc->btgp', uf, b_re.astype(f32))
    bu_im = jnp.einsum('btgc,gpc->btgp', uf, b_im.astype(f32))
    bb_re = q_re * bu_re - q_im * bu_im
    bb_im = q_re * bu_im + q_im * bu_re
    x0r = x0_re.astype(f32)
    x0i = x0_im.astype(f32)
    bb_re = bb_re.at[:, 0].add(ab_re * x0r - ab_im * x0i)
    bb_im = bb_im.at[:, 0].add(ab_re * x0i + ab_im * x0r)
    a_re = jnp.broadcast_to(ab_re, (1, t_len) + ab_re.shape)
    a_im = jnp.broadcast_to(ab_im, (1, t_len) + ab_im.shape)
    _, _, xs_re, xs_im = lax.associative_scan(_cplx_affine_combine, (a_re, a_im, bb_re, bb_im), axis=1)
    y = (jnp.einsum('btgp,gcp->btgc', xs_re, c_re.astype(f32))
         - jnp.einsum('btgp,gcp->btgc', xs_im, c_im.astype(f32))
         + d_skip.astype(f32).reshape(S5_GROUPS, S5_GROUP) * uf)
    y = jax.nn.gelu(y.reshape(bsz, t_len, D_A)).astype(u.dtype)
    out = (y @ w_glu1) * jax.nn.sigmoid(y @ w_glu2)
    return out, xs_re[:, -1], xs_im[:, -1]

def rwkv7_branch(p, shift0, s0, mu, w0, w_up, a0, a_up, g_up, k_k, k_a, r_k, gn_g, gn_b, w_bo):
    f32 = jnp.float32
    bsz, t_len, _ = p.shape
    prev = jnp.concatenate([shift0[:, None].astype(p.dtype), p[:, :-1]], axis=1)
    z = (p + (prev - p) * mu).astype(f32)
    o1, o2, o3 = D_B, 2 * D_B, 3 * D_B
    o4 = o3 + LORA_W
    o5 = o4 + LORA_A
    r = z[..., :o1]
    k = z[..., o1:o2]
    v = z[..., o2:o3]
    zw = z[..., o3:o4]
    za = z[..., o4:o5]
    zg = z[..., o5:]
    w_log = -jax.nn.softplus(-(w0 + jnp.tanh(zw) @ w_up)) - 0.5
    decay = jnp.exp(-jnp.exp(w_log))
    a = jax.nn.sigmoid(a0 + za @ a_up)
    g = jax.nn.sigmoid(zg) @ g_up

    def heads(t):
        return t.reshape(bsz, t_len, RW_HEADS, RW_HEAD)

    kk = heads(k * k_k)
    kk = kk / jnp.maximum(jnp.linalg.norm(kk, axis=-1, keepdims=True), 1e-12)
    k = k * (1.0 + (a - 1.0) * k_a)
    rh, kh, vh, wh, ah = heads(r), heads(k), heads(v), heads(decay), heads(a)

    def tm(t):
        return jnp.swapaxes(t, 0, 1)

    def step(s, inp):
        r_t, w_t, k_t, v_t, kk_t, a_t = inp
        sa = jnp.einsum('bhvk,bhk->bhv', s, -kk_t)
        s = (s * w_t[:, :, None, :]
             + sa[..., None] * (kk_t * a_t)[:, :, None, :]
             + v_t[..., None] * k_t[:, :, None, :])
        return s, jnp.einsum('bhvk,bhk->bhv', s, r_t)

    s_fin, o = lax.scan(step, s0.astype(f32), (tm(rh), tm(wh), tm(kh), tm(vh), tm(kk), tm(ah)))
    o = tm(o)
    mean = jnp.mean(o, axis=-1, keepdims=True)
    var = jnp.mean(jnp.square(o - mean), axis=-1, keepdims=True)
    o = ((o - mean) * lax.rsqrt(var + GN_EPS)).reshape(bsz, t_len, D_B) * gn_g + gn_b
    bonus = (jnp.sum(rh * kh * r_k, axis=-1, keepdims=True) * vh).reshape(bsz, t_len, D_B)
    out = ((o + bonus) * g).astype(p.dtype) @ w_bo
    return out, s_fin, p[:, -1].astype(f32)

def trunk(x, s5_re0, s5_im0, rw_s0, rw_sh0, W):
    new_re, new_im, new_s, new_sh = [], [], [], []
    o_a = D_A
    o_b = D_A + P_RW
    o_c = o_b + D_MODEL
    for l in range(DEPTH):
        h = rmsnorm(x, W['norm_mix'][l])
        proj = h @ W['w_in'][l]
        ya, xr, xi = s5_branch(proj[..., :o_a], s5_re0[l], s5_im0[l],
                               W['s5_lam_re'][l], W['s5_lam_im'][l], W['s5_log_dt'][l],
                               W['s5_b_re'][l], W['s5_b_im'][l], W['s5_c_re'][l], W['s5_c_im'][l],
                               W['s5_d'][l], W['s5_glu1'][l], W['s5_glu2'][l])
        yb, s_fin, sh = rwkv7_branch(proj[..., o_a:o_b], rw_sh0[l], rw_s0[l],
                                     W['rw_mu'][l], W['rw_w0'][l], W['rw_w_up'][l], W['rw_a0'][l],
                                     W['rw_a_up'][l], W['rw_g_up'][l], W['rw_k_k'][l], W['rw_k_a'][l],
                                     W['rw_r_k'][l], W['rw_gn_g'][l], W['rw_gn_b'][l], W['rw_w_bo'][l])
        m = (jax.nn.sigmoid(proj[..., o_b:o_c]) * ya.astype(x.dtype)
             + jax.nn.sigmoid(proj[..., o_c:]) * yb.astype(x.dtype))
        x = x + m @ W['w_out'][l]
        h2 = rmsnorm(x, W['norm_ffn'][l])
        j = l // 2
        if l % 2 == 0:
            x = x + swiglu(h2, W['ffn_w1'][j], W['ffn_w3'][j], W['ffn_w2'][j])
        else:
            x = x + moe_ffn(h2, W['moe_router'][j], W['moe_w1'][j], W['moe_w3'][j], W['moe_w2'][j])
        new_re.append(xr)
        new_im.append(xi)
        new_s.append(s_fin)
        new_sh.append(sh)
    y = rmsnorm(x, W['norm_final'])
    return (y, jnp.stack(new_re), jnp.stack(new_im), jnp.stack(new_s), jnp.stack(new_sh))

def setup_inputs(seed: int = 0) -> dict:
    key = jax.random.key(seed)
    ks = list(jax.random.split(key, 48))
    it = iter(ks)
    f32 = jnp.float32

    def nrm(shape, scale):
        return scale * jax.random.normal(next(it), shape, f32)

    def unif(shape, lo, hi):
        return jax.random.uniform(next(it), shape, f32, lo, hi)

    G, P, C, H, N = S5_GROUPS, S5_STATE, S5_GROUP, RW_HEADS, RW_HEAD
    lam_im_base = jnp.broadcast_to(math.pi * jnp.arange(P, dtype=f32), (DEPTH, G, P))
    return {
        'x_prompt': nrm((BATCH, SEQ, D_MODEL), 1.0),
        'x_sample': nrm((DEC_BATCH, DEC_SEQ, D_MODEL), 1.0),
        'state_s5_re': nrm((DEPTH, DEC_BATCH, G, P), 0.5),
        'state_s5_im': nrm((DEPTH, DEC_BATCH, G, P), 0.5),
        'state_rwkv': nrm((DEPTH, DEC_BATCH, H, N, N), 0.2),
        'state_shift': nrm((DEPTH, DEC_BATCH, P_RW), 1.0),
        'meta_tokens': nrm((N_META, D_MODEL), 1.0),
        'norm_mix': 1.0 + nrm((DEPTH, D_MODEL), 0.05),
        'w_in': nrm((DEPTH, D_MODEL, P_IN), D_MODEL ** -0.5),
        's5_lam_re': -0.5 + nrm((DEPTH, G, P), 0.01),
        's5_lam_im': lam_im_base + nrm((DEPTH, G, P), 0.01),
        's5_log_dt': unif((DEPTH, G), math.log(DT_MIN), math.log(DT_MAX)),
        's5_b_re': nrm((DEPTH, G, P, C), (2 * C) ** -0.5),
        's5_b_im': nrm((DEPTH, G, P, C), (2 * C) ** -0.5),
        's5_c_re': nrm((DEPTH, G, C, P), (2 * P) ** -0.5),
        's5_c_im': nrm((DEPTH, G, C, P), (2 * P) ** -0.5),
        's5_d': nrm((DEPTH, D_A), 1.0),
        's5_glu1': nrm((DEPTH, D_A, D_MODEL), D_A ** -0.5),
        's5_glu2': nrm((DEPTH, D_A, D_MODEL), D_A ** -0.5),
        'rw_mu': unif((DEPTH, P_RW), 0.0, 1.0),
        'rw_w0': -2.0 + nrm((DEPTH, D_B), 0.5),
        'rw_w_up': nrm((DEPTH, LORA_W, D_B), 0.1),
        'rw_a0': nrm((DEPTH, D_B), 0.1),
        'rw_a_up': nrm((DEPTH, LORA_A, D_B), 0.5 * LORA_A ** -0.5),
        'rw_g_up': nrm((DEPTH, LORA_G, D_B), LORA_G ** -0.5),
        'rw_k_k': 0.85 + nrm((DEPTH, D_B), 0.05),
        'rw_k_a': 1.0 + nrm((DEPTH, D_B), 0.05),
        'rw_r_k': nrm((DEPTH, H, N), 0.1),
        'rw_gn_g': 1.0 + nrm((DEPTH, D_B), 0.05),
        'rw_gn_b': nrm((DEPTH, D_B), 0.02),
        'rw_w_bo': nrm((DEPTH, D_B, D_MODEL), D_B ** -0.5),
        'w_out': nrm((DEPTH, D_MODEL, D_MODEL), D_MODEL ** -0.5),
        'norm_ffn': 1.0 + nrm((DEPTH, D_MODEL), 0.05),
        'ffn_w1': nrm((N_DENSE, D_MODEL, D_FF), D_MODEL ** -0.5),
        'ffn_w3': nrm((N_DENSE, D_MODEL, D_FF), D_MODEL ** -0.5),
        'ffn_w2': nrm((N_DENSE, D_FF, D_MODEL), D_FF ** -0.5),
        'moe_router': nrm((N_MOE, D_MODEL, N_EXPERTS), D_MODEL ** -0.5),
        'moe_w1': nrm((N_MOE, N_EXPERTS, D_MODEL, D_EXPERT), D_MODEL ** -0.5),
        'moe_w3': nrm((N_MOE, N_EXPERTS, D_MODEL, D_EXPERT), D_MODEL ** -0.5),
        'moe_w2': nrm((N_MOE, N_EXPERTS, D_EXPERT, D_MODEL), D_EXPERT ** -0.5),
        'norm_final': 1.0 + nrm((D_MODEL,), 0.05),
    }

def reference(x_prompt, x_sample, state_s5_re, state_s5_im, state_rwkv, state_shift,
              meta_tokens, norm_mix, w_in, s5_lam_re, s5_lam_im, s5_log_dt, s5_b_re, s5_b_im,
              s5_c_re, s5_c_im, s5_d, s5_glu1, s5_glu2, rw_mu, rw_w0, rw_w_up, rw_a0, rw_a_up,
              rw_g_up, rw_k_k, rw_k_a, rw_r_k, rw_gn_g, rw_gn_b, rw_w_bo, w_out, norm_ffn,
              ffn_w1, ffn_w3, ffn_w2, moe_router, moe_w1, moe_w3, moe_w2, norm_final):
    W = dict(norm_mix=norm_mix, w_in=w_in, s5_lam_re=s5_lam_re, s5_lam_im=s5_lam_im,
             s5_log_dt=s5_log_dt, s5_b_re=s5_b_re, s5_b_im=s5_b_im, s5_c_re=s5_c_re,
             s5_c_im=s5_c_im, s5_d=s5_d, s5_glu1=s5_glu1, s5_glu2=s5_glu2, rw_mu=rw_mu,
             rw_w0=rw_w0, rw_w_up=rw_w_up, rw_a0=rw_a0, rw_a_up=rw_a_up, rw_g_up=rw_g_up,
             rw_k_k=rw_k_k, rw_k_a=rw_k_a, rw_r_k=rw_r_k, rw_gn_g=rw_gn_g, rw_gn_b=rw_gn_b,
             rw_w_bo=rw_w_bo, w_out=w_out, norm_ffn=norm_ffn, ffn_w1=ffn_w1, ffn_w3=ffn_w3,
             ffn_w2=ffn_w2, moe_router=moe_router, moe_w1=moe_w1, moe_w3=moe_w3,
             moe_w2=moe_w2, norm_final=norm_final)
    f32 = jnp.float32
    bsz = x_prompt.shape[0]
    meta = jnp.broadcast_to(meta_tokens.astype(x_prompt.dtype)[None], (bsz, N_META, D_MODEL))
    xp = jnp.concatenate([meta, x_prompt], axis=1)
    z_re = jnp.zeros((DEPTH, bsz, S5_GROUPS, S5_STATE), f32)
    z_s = jnp.zeros((DEPTH, bsz, RW_HEADS, RW_HEAD, RW_HEAD), f32)
    z_sh = jnp.zeros((DEPTH, bsz, P_RW), f32)
    yp, p_re, p_im, p_rw, p_sh = trunk(xp, z_re, z_re, z_s, z_sh, W)
    ys, s_re, s_im, s_rw, s_sh = trunk(x_sample, state_s5_re, state_s5_im, state_rwkv, state_shift, W)
    return (yp[:, N_META:], ys, p_re, p_im, p_rw, p_sh, s_re, s_im, s_rw, s_sh)


_drawn_inputs = setup_inputs


def setup_inputs(seed=0):
    import zlib

    import numpy as np

    out = dict(_drawn_inputs(seed))
    spreads = {}
    factors = {}
    for name, (base, spread) in spreads.items():
        noise = np.random.default_rng([zlib.crc32(name.encode()), seed]).standard_normal(out[name].shape)
        drawn = base * np.exp(spread * noise) if base else spread * noise
        out[name] = __import__('jax').numpy.asarray(drawn.astype(out[name].dtype))
    for name, factor in factors.items():
        out[name] = (out[name] * factor).astype(out[name].dtype)
    return out
```

```python
import math
from contextlib import ExitStack

import numpy as np

import concourse.bass as bass
from concourse import mybir

ALU = mybir.AluOpType
ACT = mybir.ActivationFunctionType
AX = mybir.AxisListType
F32 = mybir.dt.float32
I32 = mybir.dt.int32
U32 = mybir.dt.uint32

P = 128
DEPTH = 2
D = 1024
DC = D // P
N_META = 16
TP = 272
NS = 8
T = TP + NS
G5, S5P, S5C = 32, 64, 16
DA = G5 * S5C
CA = DA // P
JT = G5 * S5P // P
LEVELS = 9
H, N = 8, 64
DB = H * N
CB = DB // P
PRW = 3 * DB + 64 + 64 + 128
CR = PRW // P
PIN = DA + PRW + 2 * D
CIN = PIN // P
DFF = 2816
CF = DFF // P
E = 8
DE = 3584
FW = 256
NG = DE // FW
CAP = 128

CH = 32
TILES = [(0, 128, [(32 * c, 32) for c in range(4)]),
         (128, 128, [(32 * c, 32) for c in range(4)]),
         (256, 24, [(0, 16)] + [(16 + b, 1) for b in range(NS)])]
MAXC = 9

SLOT = 2048
RING = 7
WIN_TILES = [2] * 15 + [1] * 4
S_WIN, S_GLU, S_WBO, S_WOUT = len(WIN_TILES), 4, 2, 4
S_MIX = S_WIN + S_GLU + S_WBO + S_WOUT
S_FUP, S_FDOWN = CF, DC * CF // 16
S_DENSE = 2 * S_MIX + S_FUP + S_FDOWN
S_EXPERT = 3 * NG
assert S_DENSE % RING == 0 and S_EXPERT % RING == 0
MIX_AT = [0, S_MIX + S_FUP + S_FDOWN]
FFN_AT = S_MIX

PV = {}
_at = 0
for _n, _w in (("norm_mix", DC), ("norm_ffn", DC), ("d", CA), ("mu", CR), ("w0", CB), ("a0", CB),
               ("k_k", CB), ("k_a", CB), ("r_k", CB), ("gn_g", CB), ("gn_b", CB)):
    PV[_n] = (_at, _w)
    _at += _w
PVW = _at

EPS_RMS, EPS_GN = 1e-6, 64e-5
TWO_PI = 2 * math.pi
C1 = 6.28125
C2 = float(np.float32(TWO_PI - C1))
C3 = TWO_PI - C1 - C2
ROUND = 12582912.0
PI_IN = 3.1415925


def expert_order():
    order = [("up", 0)]
    for g in range(NG):
        if g + 1 < NG:
            order.append(("up", g + 1))
        order.append(("down", g))
    return order


def build(nc, a, debug=None):
    with ExitStack() as ctx:
        def sb(name, shape, dt=F32):
            return ctx.enter_context(nc.sbuf_tensor(name, shape, dt))

        def sem(name):
            return ctx.enter_context(nc.semaphore(name))

        ring = sb("ring", [P, RING, SLOT])
        x = sb("x", [P, DC, T])
        arena = sb("arena", [P, 29472])
        ones = sb("ones", [P, P])
        blk = sb("blk", [P, P])
        ident = sb("ident", [P, P])
        before = sb("before", [P, P])
        iota = sb("iota", [P, P])
        masks = sb("masks", [P, 5, P])
        masks_s = sb("masks_s", [24, 5, 24])
        sel_c = sb("sel_c", [P, 2, 4])
        sel_s = sb("sel_s", [24, 2, MAXC])
        keep = sb("keep", [P, T])
        eps = sb("eps", [P, 2])
        pv = sb("pv", [P, DEPTH, PVW])
        nfin = sb("nfin", [P, DC])
        lam = sb("lam", [P, 3, DEPTH * JT])
        x0 = sb("x0", [P, DEPTH, 2, JT, NS])
        s0 = sb("s0", [P, CB, NS, N])
        shift0 = sb("shift0", [P, DEPTH, CR, NS])
        router = sb("router", [P, DC, E])
        qq = sb("qq", [P, 3, DEPTH * JT])
        apow = sb("apow", [P, LEVELS, 3, DEPTH * JT])
        axt = sb("axt", [P, 2, JT, NS])
        rstd = sb("rstd", [P, 2, T])
        wend = sb("wend", [P, CB, MAXC + 8])
        s5out = sb("s5out", [P, JT, 2, 1 + NS])
        top_i = sb("top_i", [P, 3, E], U32)
        n_int = sb("n_int", [P, 1], I32)

        pools = [ctx.enter_context(nc.psum_tensor(f"bank{i}", [P, 512], F32)) for i in range(8)]

        def ar(at, *shape):
            n = 1
            for s in shape:
                n *= s
            v = arena[:, at:at + n]
            if len(shape) == 1:
                return v
            names = "abcd"[:len(shape)]
            return v.rearrange(f"p ({' '.join(names)}) -> p {' '.join(names)}",
                               **{k: s for k, s in zip(names[1:], shape[1:])})

        gate = ar(0, 2 * DC, T)
        h = ar(4480, DC, T)
        u = ar(6720, CA, T)
        s5_b = ar(7840, CA, 2, P)
        s5_c = ar(8864, JT, 2, 32)
        lora_up = ar(9888, 2, DB)
        prow = ar(10912, CR, T + 1)
        z = ar(14848, CR, T)
        sq = ar(14848, DC, T)
        s5x = ar(18768, 2, 2, 2, T)
        y5 = ar(21008, CA, T)
        glu_s = ar(18768, 2, T)
        F0 = 20512
        small = ar(22128, 18, DEPTH * JT)
        kr = ar(F0, CB, 2, T)
        beta, chi, beta_e, chi_e, gg, bonus = (ar(F0 + CB * T * (2 + i), CB, T) for i in range(6))
        tmp = [ar(10912 + 1120 * i, CB, T) for i in range(3)] + [ar(4480 + 1120 * i, CB, T) for i in range(2)]
        o_t = z[:, 4:8, :]
        gpre, hst = ar(18208, CB, MAXC, N), ar(4480, CB, MAXC, N)
        rt, ov = ar(14848, CB, P), ar(15360, CB, P)
        U0 = 4480 + CB * MAXC * N
        un = [ar(U0 + 256 * i, 2, P) for i in range(13)]
        am, pm, a2, p2, e1, e2, xk, yk, zk, poff, akt, mbt, mkt = un
        U1 = U0 + 256 * 13
        v_tok, be_tok, ch_tok = (ar(U1 + P * i, 2, N) for i in range(3))
        v_bd, be_bd, nx_bd = (ar(U1 + 3 * P + 1152 * i, 2, MAXC, N) for i in range(3))
        act = ar(10912, CF, T)
        silu_s = ar(17072, 2, T)
        zcar = ar(14300, CB, N)
        route = ar(14560, 12, 3, E)
        h_tok = ar(7840, 3, D)
        h_e = ar(10912, DC, CAP)
        sel_p, sel_w = ar(11936, 3, CAP), ar(12320, 3, CAP)
        mix_w = ar(12704, T)
        sil_e, act_e, act_t = ar(13000, 2, FW), ar(13512, 2, FW), ar(14024, 2, 2, CAP)
        y_e = ar(17100, D)

        names = ["consts", "small_w", "s0_in", "shift_out", "s5_out", "rw_out", "y_stored", "final_out",
                 "norm_sq", "norm_ps", "norm_rt", "h_ready", "x_ready",
                 "disc_exp1", "disc_ang", "disc_exp2", "disc_done",
                 "proj_ps", "proj_out", "pad_zero",
                 "act_quad", "act_oct", "e1_out", "zcar_out", "place_moved", "bu_ps", "bu_q", "bu_used", "scan_done", "y5_ps", "y5_mix", "y5_done", "s5_last",
                 "lora_ps", "lora_in", "lora_out", "z_ready", "kk_sq", "kk_ps", "kk_norm", "cum_ready",
                 "exps_ready", "bonus_in", "bonus_ps", "fm_ready",
                 "glu_ps", "glu_sig", "glu_out",
                 "tr_ps", "tr_out", "gram_ps", "gram_out", "sq_ps", "sq_out", "quad_ps", "quad_out",
                 "oct_ps", "oct_out", "e8_ps", "e8_out", "y_ps", "y_out", "off_ps", "off_out",
                 "fix_ps", "x_out", "gh_ps", "h_out", "gh_out", "ro_ps", "ro_out", "ov_out",
                 "z_ps", "z_out", "zs_ps", "zs_out", "o_ps", "o_out", "o_mean_ps", "o_cent", "o_sq",
                 "o_var_ps", "o_std", "o_ready", "bo_ps", "bo_out", "wo_ps", "wo_out",
                 "up_ps", "up_silu", "up_out", "down_ps", "down_out",
                 "logit_ps", "logit_out", "gates_in", "gates_out", "ht_ps", "ht_out", "count_in",
                 "count_ps", "count_out", "sel_ready", "sel_used", "ga_ps", "ga_out", "mw_ps", "mw_out",
                 "eup_ps", "eup_silu", "eup_act", "et_ps", "et_out", "ey_ps", "ey_out", "em_ps", "em_out",
                 "weights_used", "dve_step", "n_ready"]
        S = {n: sem(n) for n in names}
        slot_in = [sem(f"slot_in{i}") for i in range(RING)]
        nconsts = [0]
        block = ctx.enter_context(nc.Block())

        def slot(n):
            return ring[:, n % RING, :]

        CONSTS = [(ones, "ones"), (blk, "blk"), (ident, "ident"), (before, "before"), (iota, "iota"),
                  (masks, "masks"), (masks_s, "masks_s"), (sel_c, "sel_c"), (sel_s, "sel_s"),
                  (keep, "keep"), (eps, "eps"), (pv, "pv"), (nfin, "nfin"), (lam, "lam"), (x0, "x0"),
                  (shift0, "shift0"), (router, "router"), (x, "x")]
        N_CONST = 16 * len(CONSTS)

        @block.sync
        def _(sp):
            for s in range(RING):
                sp.dma_start(ring[:, s, :], a["wstream"][s]).then_inc(slot_in[s], 16)
            with sp.Fori(1, (S_DENSE + E * S_EXPERT) // RING) as r:
                for s in range(RING):
                    sp.wait_ge(S["weights_used"], r * RING + (s - RING + 1))
                    sp.dma_start(ring[:, s, :], a["wstream"][bass.ds(r * RING + s, 1)].rearrange("o p n -> (o p) n"))\
                        .then_inc(slot_in[s], 16)
            sp.wait_ge(S["n_ready"], 1)
            npass = sp.value_load(n_int[0:1, 0:1], min_val=1, max_val=3)
            with sp.If(npass > 1):
                with sp.Fori(1, npass) as p:
                    with sp.Fori(0, E * S_EXPERT // RING) as r:
                        for s in range(RING):
                            sp.wait_ge(S["weights_used"], p * (E * S_EXPERT) + r * RING + (S_DENSE + s - RING + 1))
                            sp.dma_start(ring[:, s, :], a["wstream"][bass.ds(r * RING + (S_DENSE + s), 1)]
                                         .rearrange("o p n -> (o p) n")).then_inc(slot_in[s], 16)

        @block.gpsimd
        def _(pool):
            for t, n in CONSTS:
                pool.dma_start(t[:], a[n]).then_inc(S["consts"], 16)
            for l in range(DEPTH):
                if l:
                    pool.wait_ge(S["x_ready"], 2 * l - 1)
                pool.dma_start(s5_b, a["s5_b"][l]).then_inc(S["small_w"], 16)
                pool.dma_start(s5_c, a["s5_c"][l]).then_inc(S["small_w"], 16)
                pool.dma_start(lora_up, a["lora_up"][l]).then_inc(S["small_w"], 16)
                pool.dma_start(s0[:], a["s0"][l]).then_inc(S["s0_in"], 16)
                pool.wait_ge(S["proj_out"], CIN * l + CA + CR)
                pool.dma_start(a["o_shift"][l], prow[:, :, TP:T + 1]).then_inc(S["shift_out"], 16)
                pool.wait_ge(S["s5_last"], JT * (l + 1))
                pool.dma_start(a["o_s5"][l], s5out[:]).then_inc(S["s5_out"], 16)
                pool.wait_ge(S["zs_out"], H * (l + 1))
                pool.dma_start(a["o_rw"][l], hst).then_inc(S["rw_out"], 16)
            for n in ("shift_out", "s5_out", "rw_out"):
                pool.wait_ge(S[n], 16 * DEPTH)
            pool.wait_ge(S["final_out"], 1)
            pool.dma_start(a["y"], h).then_inc(S["y_stored"], 16)
            pool.wait_ge(S["y_stored"], 16)

        units = [(m, f) for m in range(3) for f in range(CB)]
        NU = len(units)
        EO = expert_order()

        @block.tensor
        def _(pe):
            def mm(out, lhsT, rhs, start=True, stop=True, **k):
                return nc.tensor.matmul(out, lhsT, rhs, start=start, stop=stop, **k)

            def products(out, pairs, done, release=False):
                for i, (w, r) in enumerate(pairs):
                    ins = mm(out, w, r, i == 0, i == len(pairs) - 1)
                    if i == 0 and release:
                        ins.then_inc(S["weights_used"], 1)
                if done is not None:
                    ins.then_inc(S[done], 1)

            def give_back():
                pe.nop().then_inc(S["weights_used"], 1)

            def arrived(n):
                pe.wait_ge(slot_in[n % RING], 16 * (n // RING + 1))

            def norm(i):
                pe.wait_ge(S["norm_sq"], i + 1)
                for c in range(DC):
                    last = mm(pools[0][:, 0:T], ones[:], sq[:, c, :], c == 0, c == DC - 1)
                last.then_inc(S["norm_ps"], 1)

            def proj_tile(l, n, at):
                s, j = at
                if j == 0:
                    arrived(s)
                if n >= 3:
                    pe.wait_ge(S["proj_out"], CIN * l + n - 2)
                w = slot(s).rearrange("p (j k m) -> p j k m", j=2, k=DC)
                products(pools[n % 3][:, 0:T], [(w[:, j, k, :], h[:, k, :]) for k in range(DC)], "proj_ps",
                         release=j == 0 and n > 0)

            def bu_tile(l, j):
                aa, b = j // 4, j % 4
                if j == 0:
                    pe.wait_ge(S["small_w"], 48 * (l + 1))
                    pe.wait_ge(S["proj_out"], CIN * l + CA)
                if j >= 2:
                    pe.wait_ge(S["bu_used"], JT * l + j - 1)
                for c in range(2):
                    last = mm(pools[4 + 2 * (j % 2) + c][:, 0:T], s5_b[32 * b:32 * b + 32, aa, c, :],
                              u[32 * b:32 * b + 32, aa, :])
                last.then_inc(S["bu_ps"], 1)

            def y5_tile(l, j):
                aa, b = j // 4, j % 4
                pe.wait_ge(S["scan_done"], JT * l + j + 1)
                if b == 0 and j:
                    pe.wait_ge(S["y5_mix"], CA * l + aa)
                for c in range(2):
                    last = mm(pools[3][32 * b:32 * b + 32, 0:T], s5_c[:, j, c, :], s5x[:, j % 2, 1, c, :],
                              c == 0, c == 1)
                last.then_inc(S["y5_ps"], 1)

            def glu(l):
                base = MIX_AT[l] + S_WIN
                pe.wait_ge(S["y5_done"], CA * (l + 1))
                for n in range(DC):
                    s = base + n // 2
                    if n % 2 == 0:
                        arrived(s)
                    if n >= 2:
                        pe.wait_ge(S["glu_out"], DC * l + n - 1)
                    w = slot(s).rearrange("p (j c k m) -> p j c k m", j=2, c=2, k=CA)
                    for c in range(2):
                        products(pools[2 * (n % 2) + c][:, 0:T], [(w[:, n % 2, c, k, :], y5[:, k, :]) for k in range(CA)],
                                 "glu_ps" if c else None, release=c == 0 and n % 2 == 0 and n > 0)
                pe.wait_ge(S["glu_out"], DC * (l + 1))
                give_back()

            def rwkv_features(l):
                pe.wait_ge(S["lora_in"], l + 1)
                pe.wait_ge(S["bu_used"], JT * (l + 1))
                for i in range(3):
                    for f in range(CB):
                        n = 4 * i + f
                        if n >= 4:
                            pe.wait_ge(S["lora_out"], 3 * CB * l + n - 3)
                        o = pools[4 + n % 4][:, 0:T]
                        if i < 2:
                            last = mm(o, lora_up[64 * i:64 * i + 64, 0, f * P:(f + 1) * P],
                                      z[64 * i:64 * i + 64, 12, :])
                        else:
                            last = mm(o, lora_up[:, 1, f * P:(f + 1) * P], z[:, 13, :])
                        last.then_inc(S["lora_ps"], 1)
                pe.wait_ge(S["kk_sq"], l + 1)
                pe.wait_ge(S["lora_out"], 3 * CB * (l + 1))
                for f in range(CB):
                    last = mm(pools[4 + f][:, 0:T], blk[:], tmp[0][:, f, :])
                last.then_inc(S["kk_ps"], 1)
                pe.wait_ge(S["bonus_in"], l + 1)
                for f in range(CB):
                    last = mm(pools[4 + f][:, 0:T], blk[:], bonus[:, f, :])
                last.then_inc(S["bonus_ps"], 1)

            def unit(l, m, f):
                t0, nt, chunks = TILES[m]
                n_u = NU * l + CB * m + f
                tok = slice(t0, t0 + nt)
                if m == 0 and f == 0:
                    pe.wait_ge(S["fm_ready"], l + 1)
                if n_u:
                    pe.wait_ge(S["gh_out"], n_u)
                    pe.wait_ge(S["ro_out"], n_u)
                    pe.wait_ge(S["ov_out"], n_u)
                    pe.wait_ge(S["h_out"], n_u)
                    if f == 0:
                        pe.wait_ge(S["o_out"], H * (3 * l + m))
                for i, src in enumerate((kr[:, f, 0, tok], z[:, 8 + f, tok], beta_e[:, f, tok], chi_e[:, f, tok])):
                    last = nc.tensor.transpose(pools[0][0:nt, i * P:(i + 1) * P], src, ident[:])
                last.then_inc(S["tr_ps"], 1)
                for par in range(2):
                    q = slice(64 * par, 64 * par + 64)
                    mm(pools[1 + par][0:nt, 0:nt], kr[q, f, 0, tok], beta[q, f, tok])
                    mm(pools[3 + par][0:nt, 0:2 * nt].rearrange("p (c t) -> p c t", c=2), beta[q, f, tok], kr[q, f, :, tok])
                    last = mm(pools[5 + par][0:nt, 0:2 * nt].rearrange("p (c t) -> p c t", c=2), chi[q, f, tok], kr[q, f, :, tok])
                last.then_inc(S["gram_ps"], 1)
                pe.wait_ge(S["tr_out"], n_u + 1)
                pe.wait_ge(S["gram_out"], n_u + 1)
                for par in range(2):
                    mm(pools[1][0:nt, par * P:par * P + nt], pm[0:nt, par, 0:nt], am[0:nt, par, 0:nt])
                    mm(pools[1][0:nt, (2 + par) * P:(2 + par) * P + nt], am[0:nt, par, 0:nt], pm[0:nt, par, 0:nt])
                    last = mm(pools[2][0:nt, par * N:(par + 1) * N], akt[0:nt, par, 0:nt], v_tok[0:nt, par, :])
                last.then_inc(S["sq_ps"], 1)
                pe.wait_ge(S["sq_out"], n_u + 1)
                pe.wait_ge(S["e1_out"], n_u + 1)
                for par in range(2):
                    mm(pools[3][0:nt, par * P:par * P + nt], p2[0:nt, par, 0:nt], a2[0:nt, par, 0:nt])
                    mm(pools[3][0:nt, (2 + par) * P:(2 + par) * P + nt], a2[0:nt, par, 0:nt], p2[0:nt, par, 0:nt])
                    last = mm(pools[4][0:nt, par * P:par * P + nt], a2[0:nt, par, 0:nt], e1[0:nt, par, 0:nt])
                last.then_inc(S["quad_ps"], 1)
                pe.wait_ge(S["quad_out"], n_u + 1)
                for par in range(2):
                    mm(pools[5][0:nt, par * P:par * P + nt], pm[0:nt, par, 0:nt], am[0:nt, par, 0:nt])
                    last = mm(pools[6][0:nt, par * P:par * P + nt], am[0:nt, par, 0:nt], e2[0:nt, par, 0:nt])
                last.then_inc(S["oct_ps"], 1)
                pe.wait_ge(S["oct_out"], n_u + 1)
                for par in range(2):
                    last = mm(pools[1][0:nt, par * P:par * P + nt], a2[0:nt, par, 0:nt], e1[0:nt, par, 0:nt])
                last.then_inc(S["e8_ps"], 1)
                pe.wait_ge(S["e8_out"], n_u + 1)
                for par in range(2):
                    last = mm(pools[2][0:nt, par * P:(par + 1) * P], e2[0:nt, par, 0:nt], xk[0:nt, par, :])
                last.then_inc(S["y_ps"], 1)
                pe.wait_ge(S["y_out"], n_u + 1)
                for par in range(2):
                    last = mm(pools[3][0:nt, par * P:(par + 1) * P], poff[0:nt, par, 0:nt], yk[0:nt, par, :])
                last.then_inc(S["off_ps"], 1)
                pe.wait_ge(S["off_out"], n_u + 1)
                for par in range(2):
                    last = mm(pools[4][0:nt, par * P:(par + 1) * P], e2[0:nt, par, 0:nt], zk[0:nt, par, :])
                last.then_inc(S["fix_ps"], 1)
                pe.wait_ge(S["x_out"], n_u + 1)
                ncn = len(chunks)
                for par in range(2):
                    q = slice(64 * par, 64 * par + 64)
                    c0 = 0
                    for bank_g, bank_h, w in ((5, 6, min(8, ncn)), (1, 2, ncn - 8)):
                        if w <= 0:
                            continue
                        bd = slice(c0, c0 + w)
                        def cv(t, w=w):
                            return t[q, 0:w * N].rearrange("p (c v) -> p c v", c=w)
                        mm(cv(pools[bank_g]), xk[0:nt, par, 0:N], be_bd[0:nt, par, bd, :])
                        mm(cv(pools[bank_h]), ch_tok[0:nt, par, :], v_bd[0:nt, par, bd, :], True, False)
                        last = mm(cv(pools[bank_h]), be_tok[0:nt, par, :], nx_bd[0:nt, par, bd, :], False, True)
                        c0 += w
                last.then_inc(S["gh_ps"], 1)
                for par in range(2):
                    q = slice(64 * par, 64 * par + 64)
                    mm(pools[3][q, 0:nt], xk[0:nt, par, 0:N], mbt[0:nt, par, 0:nt])
                    mm(pools[7][q, 0:nt], zk[0:nt, par, 0:N], mbt[0:nt, par, 0:nt], True, False)
                    last = mm(pools[7][q, 0:nt], v_tok[0:nt, par, :], mkt[0:nt, par, 0:nt], False, True)
                last.then_inc(S["ro_ps"], 1)

            def chain(l, m):
                t0, nt, chunks = TILES[m]
                k = NU * l + CB * (m + 1)
                pe.wait_ge(S["gh_out"], k)
                pe.wait_ge(S["h_out"], k)
                pe.wait_ge(S["ro_out"], k)
                pe.wait_ge(S["ov_out"], k)
                seq = 4 if m < 2 else 1
                if m:
                    pe.wait_ge(S["zcar_out"], 2 * l + m)
                for c in range(seq):
                    n_c = 9 * l + 4 * m + c
                    pe.wait_ge(S["z_out"], n_c + l + 1)
                    for f in range(CB):
                        for par in range(2):
                            q = slice(64 * par, 64 * par + 64)
                            src = zcar[q, f, :] if c == 0 else hst[q, f, c - 1, :]
                            last = mm(pools[par][q, f * N:(f + 1) * N], gpre[q, f, c, :], src)
                    last.then_inc(S["z_ps"], 1)
                if m == 2:
                    pe.wait_ge(S["s0_in"], 16 * (l + 1))
                    for f in range(CB):
                        for par in range(2):
                            n = 2 * f + par
                            q = slice(64 * par, 64 * par + 64)
                            if n >= 2:
                                pe.wait_ge(S["zs_out"], H * l + n - 1)
                            for b in range(NS):
                                last = mm(pools[2 + par][q, b * N:(b + 1) * N], gpre[q, f, 1 + b, :], s0[q, f, b, :])
                            last.then_inc(S["zs_ps"], 1)
                for f in range(CB):
                    for par in range(2):
                        n = 2 * f + par
                        q = slice(64 * par, 64 * par + 64)
                        k = H * (3 * l + m) + n
                        if k >= 2:
                            pe.wait_ge(S["o_out"], k - 1)
                        for c, (r0, w) in enumerate(chunks):
                            if m == 2 and c:
                                src = s0[q, f, c - 1, :]
                            else:
                                src = zcar[q, f, :] if c == 0 else hst[q, f, c - 1, :]
                            last = mm(pools[4 + par][q, r0:r0 + w], src, rt[q, f, r0:r0 + w])
                        last.then_inc(S["o_ps"], 1)

            def finish_rwkv(l):
                pe.wait_ge(S["o_out"], 3 * H * (l + 1))
                for f in range(CB):
                    last = mm(pools[f][:, 0:T], blk[:], o_t[:, f, :])
                last.then_inc(S["o_mean_ps"], 1)
                pe.wait_ge(S["o_sq"], l + 1)
                for f in range(CB):
                    last = mm(pools[4 + f][:, 0:T], blk[:], tmp[1][:, f, :])
                last.then_inc(S["o_var_ps"], 1)
                pe.wait_ge(S["o_ready"], l + 1)
                base = MIX_AT[l] + S_WIN + S_GLU
                for n in range(DC):
                    s = base + n // 4
                    if n % 4 == 0:
                        arrived(s)
                    if n >= 4:
                        pe.wait_ge(S["bo_out"], DC * l + n - 3)
                    w = slot(s).rearrange("p (j k m) -> p j k m", j=4, k=CB)
                    products(pools[n % 4][:, 0:T], [(w[:, n % 4, k, :], o_t[:, k, :]) for k in range(CB)], "bo_ps",
                             release=n == 4)
                base += S_WBO
                pe.wait_ge(S["bo_out"], DC * (l + 1))
                give_back()
                for n in range(DC):
                    s = base + n // 2
                    if n % 2 == 0:
                        arrived(s)
                    if n >= 4:
                        pe.wait_ge(S["wo_out"], DC * l + n - 3)
                    w = slot(s).rearrange("p (j k m) -> p j k m", j=2, k=DC)
                    products(pools[4 + n % 4][:, 0:T], [(w[:, n % 2, k, :], gate[:, k, :]) for k in range(DC)], "wo_ps",
                             release=n % 2 == 0 and n > 0)
                pe.wait_ge(S["wo_out"], DC * (l + 1))
                give_back()

            def mix(l):
                norm(2 * l)
                pe.wait_ge(S["h_ready"], 2 * l + 1)
                at, n = [], 0
                for s, k in enumerate(WIN_TILES):
                    at += [(MIX_AT[l] + s, j) for j in range(k)]
                for n in range(CA):
                    proj_tile(l, n, at[n])
                n = CA
                for j in range(JT):
                    bu_tile(l, j)
                    for _ in range(2):
                        if n < CIN:
                            proj_tile(l, n, at[n])
                            n += 1
                    if j >= 2:
                        y5_tile(l, j - 2)
                pe.wait_ge(S["proj_out"], CIN * (l + 1))
                give_back()
                for j in range(JT - 2, JT):
                    y5_tile(l, j)
                glu(l)
                rwkv_features(l)
                for m in range(3):
                    for f in range(CB):
                        unit(l, m, f)
                    chain(l, m)
                finish_rwkv(l)

            def ffn():
                norm(1)
                pe.wait_ge(S["h_ready"], 2)
                for n in range(CF):
                    s = FFN_AT + n
                    arrived(s)
                    if n >= 2:
                        pe.wait_ge(S["up_out"], n - 1)
                    w = slot(s).rearrange("p (c k m) -> p c k m", c=2, k=DC)
                    for c in range(2):
                        products(pools[2 * (n % 2) + c][:, 0:T], [(w[:, c, k, :], h[:, k, :]) for k in range(DC)],
                                 "up_ps" if c else None, release=c == 0 and n > 0)
                pe.wait_ge(S["up_out"], CF)
                give_back()
                for n in range(DC):
                    if n >= 4:
                        pe.wait_ge(S["down_out"], n - 3)
                    for k in range(CF):
                        b = n * CF + k
                        s = FFN_AT + S_FUP + b // 16
                        if b % 16 == 0:
                            arrived(s)
                        last = mm(pools[4 + n % 4][:, 0:T], slot(s)[:, (b % 16) * P:(b % 16 + 1) * P], act[:, k, :],
                                  k == 0, k == CF - 1)
                        if k == CF - 1:
                            last.then_inc(S["down_ps"], 1)
                        elif b % 16 == 15:
                            last.then_inc(S["weights_used"], 1)
                assert (DC * CF) % 16 == 0
                pe.wait_ge(S["down_out"], DC)
                give_back()

            def routing():
                norm(3)
                pe.wait_ge(S["h_ready"], 4)
                for m, (t0, nt, _) in enumerate(TILES):
                    for k in range(DC):
                        last = mm(pools[1][0:nt, m * E:(m + 1) * E], h[:, k, t0:t0 + nt], router[:, k, :], k == 0, k == DC - 1)
                last.then_inc(S["logit_ps"], 1)
                for m, (t0, nt, _) in enumerate(TILES):
                    for half in range(2):
                        n = 2 * m + half
                        if n >= 4:
                            pe.wait_ge(S["ht_out"], n - 3)
                        for j in range(4):
                            last = nc.tensor.transpose(pools[4 + n % 4][0:nt, j * P:(j + 1) * P],
                                                       h[:, 4 * half + j, t0:t0 + nt], ident[:])
                        last.then_inc(S["ht_ps"], 1)
                pe.wait_ge(S["count_in"], 1)
                for m, (t0, nt, _) in enumerate(TILES):
                    o = pools[2][0:nt, m * E:(m + 1) * E]
                    for mp in range(m):
                        mm(o, ones[:, 0:nt], route[:, 0, mp, :], mp == 0, False)
                    mm(o, before[0:nt, 0:nt], route[0:nt, 0, m, :], m == 0, True)
                for m, (t0, nt, _) in enumerate(TILES):
                    last = mm(pools[2][:, 3 * E:4 * E], ones[0:nt, :], route[0:nt, 0, m, :], m == 0, m == 2)
                last.then_inc(S["count_ps"], 1)

            def expert(i):
                pe.wait_ge(S["sel_ready"], i + 1)
                pe.wait_ge(S["em_out"], i * DC + 2)
                for m, (t0, nt, _) in enumerate(TILES):
                    last = nc.tensor.transpose(pools[6][:, t0:t0 + nt], sel_w[0:nt, m, :], ident[0:nt, 0:nt])
                last.then_inc(S["mw_ps"], 1)
                for half in range(2):
                    if half:
                        pe.wait_ge(S["mw_out"], i + 1)
                    for j in range(4):
                        for m, (t0, nt, _) in enumerate(TILES):
                            last = mm(pools[7 - half][:, j * P:(j + 1) * P],
                                      h_tok[0:nt, m, (4 * half + j) * P:(4 * half + j + 1) * P],
                                      sel_p[0:nt, m, :], m == 0, m == 2)
                    last.then_inc(S["ga_ps"], 1)
                pe.wait_ge(S["ga_out"], i * 2 + 2)
                pe.nop().then_inc(S["sel_used"], 1)
                n = 0
                for kind, g in EO:
                    if kind == "up":
                        pe.wait_ge(S["eup_act"], i * NG + (g + 1))
                        for c in range(2):
                            pe.wait_ge(slot_in[n % RING], (i * (S_EXPERT // RING) + (S_DENSE // RING + n // RING + 1)) * 16)
                            w = slot(n).rearrange("p (k m) -> p k m", k=DC)
                            products(pools[g % 2][:, c * FW:(c + 1) * FW], [(h_e[:, k, :], w[:, k, :]) for k in range(DC)],
                                     "eup_ps" if c else "weights_used", release=c == 0 and g == 1)
                            n += 1
                    else:
                        pe.wait_ge(S["eup_act"], i * NG + (g + 3))
                        pe.wait_ge(S["et_out"], i * NG + (g + 1))
                        for j in range(2):
                            last = nc.tensor.transpose(pools[2 + g % 2][:, j * P:(j + 1) * P], act_e[:, g % 2, j * P:(j + 1) * P], ident[:])
                            if j == 0 and g < NG - 1:
                                last.then_inc(S["weights_used"], 1)
                        last.then_inc(S["et_ps"], 1)
                        pe.wait_ge(S["et_out"], i * NG + (g + 3))
                        pe.wait_ge(slot_in[n % RING], (i * (S_EXPERT // RING) + (S_DENSE // RING + n // RING + 1)) * 16)
                        if g == 0:
                            pe.wait_ge(S["ey_out"], i + 1)
                        w = slot(n).rearrange("p (k m) -> p k m", k=2)
                        for j in range(2):
                            for half in range(2):
                                last = mm(pools[4 + half][:], act_t[:, g % 2, j, :], w[:, j, half * 512:(half + 1) * 512],
                                          g == 0 and j == 0, g == NG - 1 and j == 1)
                        last.then_inc(S["ey_ps" if g == NG - 1 else "weights_used"], 1)
                        n += 1
                pe.wait_ge(S["ey_out"], i + 2)
                give_back()
                for c in range(DC):
                    pe.wait_ge(S["em_out"], i * DC + (c + 1))
                    mm(pools[6 + c % 2][:, 0:T], y_e[:, c * P:(c + 1) * P], mix_w).then_inc(S["em_ps"], 1)

            def experts():
                pe.wait_ge(S["count_out"], 1)
                pe.wait_ge(S["ht_out"], 6)
                with pe.Fori(0, E) as e:
                    expert(e)
                pe.wait_ge(S["n_ready"], 1)
                npass = pe.value_load(n_int[0:1, 0:1], min_val=1, max_val=3)
                with pe.If(npass > 1):
                    with pe.Fori(1, npass) as p:
                        with pe.Fori(0, E) as e:
                            expert(p * E + e)

            pe.wait_ge(S["consts"], N_CONST)
            mix(0)
            ffn()
            mix(1)
            routing()
            experts()
            norm(4)

        @block.scalar
        def _(ac):

            def fn(out, in_, func, **k):
                return nc.scalar.activation(out, in_, func, **k)

            def norm(i):
                if i:
                    ac.wait_ge(S["x_ready"], i)
                fn(sq, x[:], ACT.Square).then_inc(S["norm_sq"], 1)
                ac.wait_ge(S["norm_ps"], i + 1)
                fn(rstd[:, 0, :], pools[0][:, 0:T], ACT.Sqrt, scale=1.0 / D, bias=eps[:, 0:1]).then_inc(S["norm_rt"], 1)

            def proj_out(l, n):
                ac.wait_ge(S["proj_ps"], CIN * l + n + 1)
                src = pools[n % 3][:, 0:T]
                if n < CA:
                    ins = fn(u[:, n, :], src, ACT.Identity)
                elif n < CA + CR:
                    ins = fn(prow[:, n - CA, 1:T + 1], src, ACT.Identity)
                else:
                    ins = fn(gate[:, n - CA - CR, :], src, ACT.Sigmoid)
                ins.then_inc(S["proj_out"], 1)

            def bu_out(l, j):
                ac.wait_ge(S["bu_ps"], JT * l + j + 1)
                if j >= 2:
                    ac.wait_ge(S["y5_ps"], JT * l + j - 1)
                q = qq[:, 0, JT * l + j:JT * l + j + 1]
                for c in range(2):
                    ins = fn(s5x[:, j % 2, 0, c, :], pools[4 + 2 * (j % 2) + c][:, 0:T], ACT.Identity, scale=q)
                ins.then_inc(S["bu_q"], 1)

            def mix(l):
                norm(2 * l)
                for n in range(CA):
                    proj_out(l, n)
                n = CA
                for j in range(2):
                    bu_out(l, j)
                    for _ in range(2):
                        proj_out(l, n)
                        n += 1
                for j in range(2, JT):
                    bu_out(l, j)
                    for _ in range(2):
                        if n < CIN:
                            proj_out(l, n)
                            n += 1
                for aa in range(CA):
                    ac.wait_ge(S["y5_mix"], CA * l + aa + 1)
                    fn(y5[:, aa, :], y5[:, aa, :], ACT.Gelu_apprx_tanh).then_inc(S["y5_done"], 1)
                for n in range(DC):
                    ac.wait_ge(S["glu_ps"], DC * l + n + 1)
                    if n >= 2:
                        ac.wait_ge(S["glu_out"], DC * l + n - 1)
                    fn(glu_s[:, n % 2, :], pools[2 * (n % 2) + 1][:, 0:T], ACT.Sigmoid).then_inc(S["glu_sig"], 1)
                ac.wait_ge(S["z_ready"], l + 1)
                ac.wait_ge(S["shift_out"], 16 * (l + 1))
                fn(z[0:64, 12, :], z[0:64, 12, :], ACT.Tanh)
                fn(z[:, 13, :], z[:, 13, :], ACT.Sigmoid).then_inc(S["lora_in"], 1)
                for i in range(3):
                    for f in range(CB):
                        k = 4 * i + f
                        ac.wait_ge(S["lora_ps"], 3 * CB * l + k + 1)
                        src = pools[4 + k % 4][:, 0:T]
                        if i < 2:
                            c0 = PV["w0" if i == 0 else "a0"][0]
                            ins = fn(tmp[1 + i][:, f, :], src, ACT.Sigmoid, bias=pv[:, l, c0 + f:c0 + f + 1])
                        else:
                            ins = fn(gg[:, f, :], src, ACT.Identity)
                        ins.then_inc(S["lora_out"], 1)
                ac.wait_ge(S["kk_ps"], l + 1)
                for f in range(CB):
                    ins = fn(tmp[0][:, f, :], pools[4 + f][:, 0:T], ACT.Sqrt)
                ins.then_inc(S["kk_norm"], 1)
                ac.wait_ge(S["cum_ready"], l + 1)
                fn(kr[:, :, 1, :], tmp[3], ACT.Exp)
                fn(kr[:, :, 0, :], tmp[4], ACT.Exp)
                fn(beta, tmp[3], ACT.Exp, scale=-1.0)
                fn(beta_e, chi_e, ACT.Exp).then_inc(S["exps_ready"], 1)
                for m in range(3):
                    t0, nt, chunks = TILES[m]
                    for f in range(CB):
                        n_u = NU * l + CB * m + f
                        ac.wait_ge(S["tr_ps"], n_u + 1)
                        ps = pools[0][0:nt, :].rearrange("p (i a k) -> p i a k", i=4, a=2)
                        fn(xk[0:nt, :, 0:N], ps[:, 0], ACT.Identity)
                        fn(v_tok[0:nt], ps[:, 1], ACT.Identity)
                        fn(be_tok[0:nt], ps[:, 2], ACT.Identity)
                        fn(ch_tok[0:nt], ps[:, 3], ACT.Identity).then_inc(S["tr_out"], 1)
                        ac.wait_ge(S["sq_ps"], n_u + 1)
                        sqv = pools[1][0:nt, :].rearrange("p (i t) -> p i t", i=4)
                        fn(a2[0:nt, :, 0:nt], sqv[:, 0:2, 0:nt], ACT.Identity)
                        fn(p2[0:nt, :, 0:nt], sqv[:, 2:4, 0:nt], ACT.Identity)
                        fn(xk[0:nt, :, N:P], pools[2][0:nt, 0:P].rearrange("p (a k) -> p a k", a=2), ACT.Identity)\
                            .then_inc(S["sq_out"], 1)
                        ac.wait_ge(S["quad_ps"], n_u + 1)
                        qv = pools[3][0:nt, :].rearrange("p (i t) -> p i t", i=4)
                        fn(am[0:nt, :, 0:nt], qv[:, 0:2, 0:nt], ACT.Identity)
                        fn(pm[0:nt, :, 0:nt], qv[:, 2:4, 0:nt], ACT.Identity).then_inc(S["act_quad"], 1)
                        ac.wait_ge(S["oct_ps"], n_u + 1)
                        fn(a2[0:nt, :, 0:nt], pools[5][0:nt, 0:2 * P].rearrange("p (a t) -> p a t", a=2)[:, :, 0:nt],
                           ACT.Identity).then_inc(S["act_oct"], 1)
                        ac.wait_ge(S["y_ps"], n_u + 1)
                        fn(yk[0:nt], pools[2][0:nt, 0:2 * P].rearrange("p (a t) -> p a t", a=2), ACT.Identity)\
                            .then_inc(S["y_out"], 1)
                        ac.wait_ge(S["off_ps"], n_u + 1)
                        fn(zk[0:nt], pools[3][0:nt, 0:2 * P].rearrange("p (a t) -> p a t", a=2), ACT.Identity)\
                            .then_inc(S["off_out"], 1)
                        ac.wait_ge(S["gh_ps"], n_u + 1)
                        w = min(8, len(chunks))
                        ins = fn(hst[:, f, 0:w, :], pools[6][:, 0:w * N].rearrange("p (c v) -> p c v", c=w), ACT.Identity)
                        if len(chunks) > 8:
                            ins = fn(hst[:, f, 8, :], pools[2][:, 0:N], ACT.Identity)
                        ins.then_inc(S["h_out"], 1)
                        ac.wait_ge(S["ro_ps"], n_u + 1)
                        fn(ov[:, f, 0:nt], pools[7][:, 0:nt], ACT.Identity).then_inc(S["ov_out"], 1)
                ac.wait_ge(S["o_cent"], l + 1)
                fn(tmp[1], o_t, ACT.Square).then_inc(S["o_sq"], 1)
                ac.wait_ge(S["o_var_ps"], l + 1)
                for f in range(CB):
                    ins = fn(tmp[0][:, f, :], pools[4 + f][:, 0:T], ACT.Sqrt, scale=1.0 / N, bias=eps[:, 1:2])
                ins.then_inc(S["o_std"], 1)

            def ffn():
                norm(1)
                for n in range(CF):
                    ac.wait_ge(S["up_ps"], n + 1)
                    if n >= 2:
                        ac.wait_ge(S["up_out"], n - 1)
                    fn(silu_s[:, n % 2, :], pools[2 * (n % 2)][:, 0:T], ACT.Silu).then_inc(S["up_silu"], 1)

            def routing():
                norm(3)
                for m, (t0, nt, _) in enumerate(TILES):
                    for half in range(2):
                        n = 2 * m + half
                        ac.wait_ge(S["ht_ps"], n + 1)
                        fn(h_tok[0:nt, m, 512 * half:512 * half + 512], pools[4 + n % 4][0:nt, :], ACT.Identity)\
                            .then_inc(S["ht_out"], 1)
                ac.wait_ge(S["gates_in"], 1)
                fn(route[:, 6, :, 0:2], route[:, 5, :, 0:2], ACT.Sigmoid).then_inc(S["gates_out"], 1)

            def expert(i):
                ac.wait_ge(S["mw_ps"], i + 1)
                fn(mix_w, pools[6][:, 0:T], ACT.Identity).then_inc(S["mw_out"], 1)
                for half in range(2):
                    ac.wait_ge(S["ga_ps"], i * 2 + (half + 1))
                    fn(h_e[:, 4 * half:4 * half + 4, :], pools[7 - half][:].rearrange("p (c s) -> p c s", c=4),
                       ACT.Identity).then_inc(S["ga_out"], 1)
                for kind, g in EO:
                    if kind == "up":
                        ac.wait_ge(S["eup_ps"], i * NG + (g + 1))
                        ac.wait_ge(S["eup_act"], i * NG + (g + 1))
                        fn(sil_e[:, g % 2, :], pools[g % 2][:, 0:FW], ACT.Silu).then_inc(S["eup_silu"], 1)
                    else:
                        ac.wait_ge(S["et_ps"], i * NG + (g + 1))
                        fn(act_t[:, g % 2], pools[2 + g % 2][:, 0:2 * P].rearrange("p (j s) -> p j s", j=2),
                           ACT.Identity).then_inc(S["et_out"], 1)
                ac.wait_ge(S["ey_ps"], i + 1)
                fn(y_e[:, 0:512], pools[4][:], ACT.Identity)
                fn(y_e[:, 512:1024], pools[5][:], ACT.Identity).then_inc(S["ey_out"], 1)

            def experts():
                for _ in range(2):
                    nc.scalar.nop().then_inc(S["et_out"], 1)
                nc.scalar.nop().then_inc(S["ey_out"], 1)
                with ac.Fori(0, E) as e:
                    expert(e)
                ac.wait_ge(S["n_ready"], 1)
                npass = ac.value_load(n_int[0:1, 0:1], min_val=1, max_val=3)
                with ac.If(npass > 1):
                    with ac.Fori(1, npass) as p:
                        with ac.Fori(0, E) as e:
                            expert(p * E + e)

            ac.wait_ge(S["consts"], N_CONST)
            fn(small[:, 2, :], lam[:, 2, :], ACT.Exp).then_inc(S["disc_exp1"], 1)
            ac.wait_ge(S["disc_ang"], 1)
            fn(small[:, 3, :], small[:, 4, :], ACT.Exp)
            fn(small[:, 5:7, :], small[:, 7:9, :], ACT.Sin).then_inc(S["disc_exp2"], 1)
            mix(0)
            ffn()
            mix(1)
            routing()
            experts()
            norm(4)

        @block.vector
        def _(dve):
            steps = [0]
            v = nc.vector

            def step(ins):
                steps[0] += 1
                ins.then_inc(S["dve_step"], 1)
                dve.wait_ge(S["dve_step"], steps[0])

            def col(l, name, i):
                c0 = PV[name][0]
                return pv[:, l, c0 + i:c0 + i + 1]

            def norm(i, gains, out):
                dve.wait_ge(S["norm_rt"], i + 1)
                step(v.reciprocal(rstd[:, 1, :], rstd[:, 0, :]))
                for c in range(DC):
                    ins = v.scalar_tensor_tensor(out=out[:, c, :], in0=x[:, c, :], scalar=gains[:, c:c + 1],
                                                 in1=rstd[:, 1, :], op0=ALU.mult, op1=ALU.mult)
                ins.then_inc(S["h_ready"], 1)

            def discretise():
                s = lambda i: small[:, i, :]
                lr, li = lam[:, 0, :], lam[:, 1, :]
                tt, ts = v.tensor_tensor, v.tensor_scalar
                dve.wait_ge(S["disc_exp1"], 1)
                step(tt(s(4), lr, s(2), ALU.mult))
                step(tt(s(9), li, s(2), ALU.mult))
                step(ts(s(10), s(9), 1 / TWO_PI, ROUND, ALU.mult, ALU.add))
                step(ts(s(10), s(10), ROUND, None, ALU.subtract))
                for c in (C1, C2, C3):
                    step(v.scalar_tensor_tensor(out=s(9), in0=s(10), scalar=-c, in1=s(9), op0=ALU.mult, op1=ALU.add))
                step(ts(s(7), s(9), -PI_IN, PI_IN, ALU.max, ALU.min))
                step(ts(s(10), s(9), math.pi / 2, None, ALU.add))
                step(ts(s(11), s(10), math.pi, -TWO_PI, ALU.is_gt, ALU.mult))
                step(tt(s(10), s(10), s(11), ALU.add))
                ts(s(8), s(10), -PI_IN, PI_IN, ALU.max, ALU.min).then_inc(S["disc_ang"], 1)
                dve.wait_ge(S["disc_exp2"], 1)
                ar_, ai_, na = apow[:, 0, 0, :], apow[:, 0, 1, :], apow[:, 0, 2, :]
                step(tt(ar_, s(3), s(6), ALU.mult))
                step(tt(ai_, s(3), s(5), ALU.mult))
                step(tt(s(12), lr, lr, ALU.mult))
                step(tt(s(13), li, li, ALU.mult))
                step(tt(s(12), s(12), s(13), ALU.add))
                step(v.reciprocal(s(12), s(12)))
                step(ts(s(13), ar_, 1.0, None, ALU.subtract))
                step(tt(s(14), s(13), lr, ALU.mult))
                step(tt(s(15), ai_, li, ALU.mult))
                step(tt(s(14), s(14), s(15), ALU.add))
                step(tt(qq[:, 0, :], s(14), s(12), ALU.mult))
                step(tt(s(14), ai_, lr, ALU.mult))
                step(tt(s(15), s(13), li, ALU.mult))
                step(tt(s(14), s(14), s(15), ALU.subtract))
                step(tt(qq[:, 1, :], s(14), s(12), ALU.mult))
                step(ts(qq[:, 2, :], qq[:, 1, :], -1.0, None, ALU.mult))
                step(ts(na, ai_, -1.0, None, ALU.mult))
                for k in range(1, LEVELS):
                    br, bi, bn = (apow[:, k - 1, i, :] for i in range(3))
                    step(tt(s(14), br, br, ALU.mult))
                    step(tt(s(15), bi, bi, ALU.mult))
                    step(tt(apow[:, k, 0, :], s(14), s(15), ALU.subtract))
                    step(tt(s(14), br, bi, ALU.mult))
                    step(ts(apow[:, k, 1, :], s(14), 2.0, None, ALU.mult))
                    step(ts(apow[:, k, 2, :], s(14), -2.0, None, ALU.mult))
                for l in range(DEPTH):
                    def ab(i):
                        return apow[:, 0, i, JT * l:JT * (l + 1)].unsqueeze(2).broadcast_to([P, JT, NS])
                    tt(axt[:, 0], x0[:, l, 1], ab(2), ALU.mult)
                    step(tt(axt[:, 1], x0[:, l, 0], ab(1), ALU.mult))
                    for c in range(2):
                        step(tt(x0[:, l, c], x0[:, l, c], ab(0), ALU.mult))
                    step(tt(x0[:, l], x0[:, l], axt[:], ALU.add))

            def scan_tile(l, j):
                k_ = JT * l + j
                A, B = (s5x[:, j % 2, i] for i in range(2))
                ps_r, ps_i = (pools[4 + 2 * (j % 2) + c][:, 0:T] for c in range(2))
                stt = v.scalar_tensor_tensor
                dve.wait_ge(S["bu_q"], k_ + 1)
                stt(out=A[:, 0, :], in0=ps_i, scalar=qq[:, 2, k_:k_ + 1], in1=A[:, 0, :], op0=ALU.mult, op1=ALU.add)
                ins = stt(out=A[:, 1, :], in0=ps_r, scalar=qq[:, 1, k_:k_ + 1], in1=A[:, 1, :], op0=ALU.mult, op1=ALU.add)
                ins.then_inc(S["bu_used"], 1)
                dve.wait_ge(S["bu_used"], k_ + 1)
                step(v.tensor_tensor(A[:, :, TP:T], A[:, :, TP:T], x0[:, l, :, j, :], ALU.add))
                for k in range(LEVELS):
                    n = 1 << k
                    src, dst = (A, B) if k % 2 == 0 else (B, A)
                    r_, i_, m_ = (apow[:, k, c, k_:k_ + 1] for c in range(3))
                    stt(out=dst[:, :, n:TP], in0=src[:, :, 0:TP - n], scalar=r_, in1=src[:, :, n:TP],
                        op0=ALU.mult, op1=ALU.add)
                    step(v.tensor_copy(dst[:, :, 0:n], src[:, :, 0:n]))
                    stt(out=dst[:, 0, n:TP], in0=src[:, 1, 0:TP - n], scalar=m_, in1=dst[:, 0, n:TP],
                        op0=ALU.mult, op1=ALU.add)
                    step(stt(out=dst[:, 1, n:TP], in0=src[:, 0, 0:TP - n], scalar=i_, in1=dst[:, 1, n:TP],
                             op0=ALU.mult, op1=ALU.add))
                assert LEVELS % 2 == 1
                v.tensor_copy(B[:, :, TP:T], A[:, :, TP:T]).then_inc(S["scan_done"], 1)
                dve.wait_ge(S["scan_done"], k_ + 1)
                if l and j == 0:
                    dve.wait_ge(S["s5_out"], 16 * l)
                v.tensor_copy(s5out[:, j], B[:, :, TP - 1:T]).then_inc(S["s5_last"], 1)

            def y5_add(l, aa):
                dve.wait_ge(S["y5_ps"], JT * l + 4 * aa + 4)
                v.scalar_tensor_tensor(out=y5[:, aa, :], in0=u[:, aa, :], scalar=col(l, "d", aa),
                                       in1=pools[3][:, 0:T], op0=ALU.mult, op1=ALU.add).then_inc(S["y5_mix"], 1)

            def mix(l):
                tt, ts, stt = v.tensor_tensor, v.tensor_scalar, v.scalar_tensor_tensor
                norm(2 * l, pv[:, l, PV["norm_mix"][0]:PV["norm_mix"][0] + DC], h)
                v.memset(prow[:, :, 0:1], 0.0).then_inc(S["pad_zero"], 1)
                dve.wait_ge(S["small_w"], 48 * (l + 1))
                step(ts(s5_c[:, :, 1, :], s5_c[:, :, 1, :], -1.0, None, ALU.mult))
                for j in range(JT):
                    scan_tile(l, j)
                    if j >= 4 and j % 4 == 1:
                        y5_add(l, j // 4 - 1)
                y5_add(l, CA - 1)
                dve.wait_ge(S["proj_out"], CIN * l + CA + CR)
                dve.wait_ge(S["pad_zero"], l + 1)
                tt(z[:, :, 0:TP], prow[:, :, 0:TP], prow[:, :, 1:TP + 1], ALU.subtract)
                step(tt(z[:, :, TP:T], shift0[:, l], prow[:, :, TP + 1:T + 1], ALU.subtract))
                for c in range(CR):
                    ins = stt(out=z[:, c, :], in0=z[:, c, :], scalar=col(l, "mu", c), in1=prow[:, c, 1:T + 1],
                              op0=ALU.mult, op1=ALU.add)
                ins.then_inc(S["z_ready"], 1)
                for n in range(DC):
                    dve.wait_ge(S["glu_sig"], DC * l + n + 1)
                    step(tt(gate[:, n, :], gate[:, n, :], glu_s[:, n % 2, :], ALU.mult))
                    tt(gate[:, n, :], gate[:, n, :], pools[2 * (n % 2)][:, 0:T], ALU.mult).then_inc(S["glu_out"], 1)
                dve.wait_ge(S["z_ready"], l + 1)
                dve.wait_ge(S["shift_out"], 16 * (l + 1))
                kk = chi
                for f in range(CB):
                    ins = ts(kk[:, f, :], z[:, 4 + f, :], col(l, "k_k", f), None, ALU.mult)
                step(ins)
                tt(tmp[0], kk, kk, ALU.mult).then_inc(S["kk_sq"], 1)
                dve.wait_ge(S["lora_out"], 3 * CB * (l + 1))
                step(ts(tmp[1], tmp[1], -math.exp(-0.5), None, ALU.mult))
                flat = "p a t -> p (a t)"
                for f in range(CB):
                    ins = v.tensor_tensor_scan(tmp[3][:, f, :], keep[:], tmp[1][:, f, :], 0.0, ALU.mult, ALU.add)
                step(ins)
                tt(tmp[4], tmp[3], tmp[1], ALU.subtract)
                full = TP // CH
                cv = tmp[3][:, :, 0:full * CH].rearrange("p a (c t) -> p a c t", t=CH)
                for f in range(CB):
                    tt(chi_e[:, f, 0:full * CH].rearrange("p (c t) -> p c t", t=CH),
                       cv[:, f, :, CH - 1:CH].broadcast_to([P, full, CH]), cv[:, f], ALU.subtract)
                tt(chi_e[:, :, full * CH:TP], tmp[3][:, :, TP - 1:TP].broadcast_to([P, CB, TP - full * CH]),
                   tmp[3][:, :, full * CH:TP], ALU.subtract)
                v.memset(chi_e[:, :, TP:T], 0.0).then_inc(S["cum_ready"], 1)
                dve.wait_ge(S["kk_norm"], l + 1)
                step(ts(tmp[0], tmp[0], 1e-12, None, ALU.max))
                step(v.reciprocal(tmp[0], tmp[0]))
                step(tt(kk, kk, tmp[0], ALU.mult))
                kp = z[:, 4:8, :]
                for f in range(CB):
                    ins = ts(tmp[0][:, f, :], tmp[2][:, f, :], 1.0, col(l, "k_a", f), ALU.subtract, ALU.mult)
                step(ins)
                step(stt(out=kp.rearrange(flat), in0=tmp[0].rearrange(flat), scalar=1.0, in1=kp.rearrange(flat),
                         op0=ALU.add, op1=ALU.mult))
                for f in range(CB):
                    ins = stt(out=bonus[:, f, :], in0=z[:, f, :], scalar=col(l, "r_k", f), in1=kp[:, f, :],
                              op0=ALU.mult, op1=ALU.mult)
                ins.then_inc(S["bonus_in"], 1)
                step(tt(tmp[2], tmp[2], kk, ALU.mult))
                dve.wait_ge(S["exps_ready"], l + 1)
                for f in range(CB):
                    v.tensor_copy(wend[:, f, 0:full], kr[:, f, 1, CH - 1:full * CH:CH])
                v.tensor_copy(wend[:, :, full:full + 1 + NS], kr[:, :, 1, TP - 1:T])
                step(tt(kr[:, :, 0, :], kr[:, :, 0, :], kk, ALU.mult))
                step(tt(kr[:, :, 1, :], kr[:, :, 1, :], z[:, 0:4, :], ALU.mult))
                tt(chi, beta, kp, ALU.mult)
                step(tt(chi_e, beta_e, kp, ALU.mult))
                tt(beta, beta, tmp[2], ALU.mult)
                tt(beta_e, beta_e, tmp[2], ALU.mult)
                v.memset(zcar, 0.0).then_inc(S["z_out"], 1)
                dve.wait_ge(S["bonus_ps"], l + 1)
                for f in range(CB):
                    ins = tt(bonus[:, f, :], z[:, 8 + f, :], pools[4 + f][:, 0:T], ALU.mult)
                ins.then_inc(S["fm_ready"], 1)
                dve.wait_ge(S["fm_ready"], l + 1)
                for m in range(3):
                    for f in range(CB):
                        unit(l, m, f)
                    chain(l, m)
                dve.wait_ge(S["o_mean_ps"], l + 1)
                for f in range(CB):
                    ins = stt(out=o_t[:, f, :], in0=pools[f][:, 0:T], scalar=-1.0 / N, in1=o_t[:, f, :],
                              op0=ALU.mult, op1=ALU.add)
                ins.then_inc(S["o_cent"], 1)
                dve.wait_ge(S["o_std"], l + 1)
                dve.wait_ge(S["o_cent"], l + 1)
                step(v.reciprocal(tmp[0], tmp[0]))
                step(tt(o_t, o_t, tmp[0], ALU.mult))
                for f in range(CB):
                    ins = ts(o_t[:, f, :], o_t[:, f, :], col(l, "gn_g", f), col(l, "gn_b", f), ALU.mult, ALU.add)
                step(ins)
                step(tt(o_t, o_t, bonus, ALU.add))
                tt(o_t, o_t, gg, ALU.mult).then_inc(S["o_ready"], 1)
                for n in range(DC):
                    dve.wait_ge(S["bo_ps"], DC * l + n + 1)
                    step(tt(gate[:, DC + n, :], gate[:, DC + n, :], pools[n % 4][:, 0:T], ALU.mult))
                    tt(gate[:, n, :], gate[:, n, :], gate[:, DC + n, :], ALU.add).then_inc(S["bo_out"], 1)
                for n in range(DC):
                    dve.wait_ge(S["wo_ps"], DC * l + n + 1)
                    tt(x[:, n, :], x[:, n, :], pools[4 + n % 4][:, 0:T], ALU.add).then_inc(S["wo_out"], 1)
                dve.wait_ge(S["wo_out"], DC * (l + 1))
                v.nop().then_inc(S["x_ready"], 1)

            def unit(l, m, f):
                tt, ts, stt = v.tensor_tensor, v.tensor_scalar, v.scalar_tensor_tensor
                t0, nt, chunks = TILES[m]
                ncn = len(chunks)
                n_u = NU * l + CB * m + f
                mk = masks[:] if m < 2 else masks_s[:]
                sc = sel_c[:] if m < 2 else sel_s[:]
                dve.wait_ge(S["gram_ps"], n_u + 1)
                for par in range(2):
                    tt(am[0:nt, par, 0:nt], pools[1 + par][0:nt, 0:nt], mk[:, 0], ALU.mult)
                    g3 = pools[3 + par][0:nt, 0:2 * nt].rearrange("p (c t) -> p c t", c=2)
                    g5 = pools[5 + par][0:nt, 0:2 * nt].rearrange("p (c t) -> p c t", c=2)
                    tt(pm[0:nt, par, 0:nt], g3[:, 0], mk[:, 1], ALU.mult)
                    tt(poff[0:nt, par, 0:nt], g3[:, 0], mk[:, 2], ALU.mult)
                    tt(mbt[0:nt, par, 0:nt], g3[:, 1], mk[:, 4], ALU.mult)
                    tt(akt[0:nt, par, 0:nt], g5[:, 0], mk[:, 3], ALU.mult)
                    ins = tt(mkt[0:nt, par, 0:nt], g5[:, 1], mk[:, 4], ALU.mult)
                ins.then_inc(S["gram_out"], 1)
                dve.wait_ge(S["gram_out"], n_u + 1)
                for par in range(2):
                    ins = tt(e1[0:nt, par, 0:nt], ident[0:nt, 0:nt], pm[0:nt, par, 0:nt], ALU.subtract)
                ins.then_inc(S["e1_out"], 1)
                dve.wait_ge(S["tr_out"], n_u + 1)

                def chunked(out, src, sign):
                    for par in range(2):
                        tt(out[0:nt, par, 0:ncn, :], src[0:nt, par, :].unsqueeze(1).broadcast_to([nt, ncn, N]),
                           sc[:, sign].unsqueeze(2).broadcast_to([nt, ncn, N]), ALU.mult)

                chunked(v_bd, v_tok, 0)
                chunked(be_bd, be_tok, 0)
                dve.wait_ge(S["quad_ps"], n_u + 1)
                dve.wait_ge(S["act_quad"], n_u + 1)
                tt(e2[0:nt, :, 0:nt], e1[0:nt, :, 0:nt],
                   pools[4][0:nt, 0:2 * P].rearrange("p (a t) -> p a t", a=2)[:, :, 0:nt], ALU.add).then_inc(S["quad_out"], 1)
                dve.wait_ge(S["quad_out"], n_u + 1)
                dve.wait_ge(S["oct_ps"], n_u + 1)
                dve.wait_ge(S["act_oct"], n_u + 1)
                tt(e1[0:nt, :, 0:nt], e2[0:nt, :, 0:nt],
                   pools[6][0:nt, 0:2 * P].rearrange("p (a t) -> p a t", a=2)[:, :, 0:nt], ALU.add).then_inc(S["oct_out"], 1)
                dve.wait_ge(S["oct_out"], n_u + 1)
                dve.wait_ge(S["e8_ps"], n_u + 1)
                tt(e2[0:nt, :, 0:nt], e1[0:nt, :, 0:nt],
                   pools[1][0:nt, 0:2 * P].rearrange("p (a t) -> p a t", a=2)[:, :, 0:nt], ALU.add).then_inc(S["e8_out"], 1)
                dve.wait_ge(S["fix_ps"], n_u + 1)
                dve.wait_ge(S["y_out"], n_u + 1)
                step(tt(xk[0:nt], yk[0:nt], pools[4][0:nt, 0:2 * P].rearrange("p (a t) -> p a t", a=2), ALU.subtract))
                chunked(nx_bd, xk[:, :, N:P], 1)
                ts(zk[0:nt, :, 0:N], xk[0:nt, :, N:P], -1.0, None, ALU.mult).then_inc(S["x_out"], 1)
                dve.wait_ge(S["gh_ps"], n_u + 1)
                w0 = 4 * m
                for par in range(2):
                    q = slice(64 * par, 64 * par + 64)
                    ins = tt(gpre[q, f, 0:ncn, :], ident[q, q].unsqueeze(1).broadcast_to([64, ncn, N]),
                             wend[q, f, w0:w0 + ncn].unsqueeze(2).broadcast_to([64, ncn, N]), ALU.mult)
                step(ins)
                w = min(8, ncn)
                ins = tt(gpre[:, f, 0:w, :], gpre[:, f, 0:w, :],
                         pools[5][:, 0:w * N].rearrange("p (c v) -> p c v", c=w), ALU.subtract)
                if ncn > 8:
                    ins = tt(gpre[:, f, 8, :], gpre[:, f, 8, :], pools[1][:, 0:N], ALU.subtract)
                ins.then_inc(S["gh_out"], 1)
                dve.wait_ge(S["ro_ps"], n_u + 1)
                tt(rt[:, f, 0:nt], kr[:, f, 1, t0:t0 + nt], pools[3][:, 0:nt], ALU.subtract).then_inc(S["ro_out"], 1)

            def chain(l, m):
                tt = v.tensor_tensor
                t0, nt, chunks = TILES[m]
                dve.wait_ge(S["h_out"], NU * l + CB * (m + 1))
                dve.wait_ge(S["ov_out"], NU * l + CB * (m + 1))
                seq = 4 if m < 2 else 1
                for c in range(seq):
                    n_c = 9 * l + 4 * m + c
                    dve.wait_ge(S["z_ps"], n_c + 1)
                    for par in range(2):
                        q = slice(64 * par, 64 * par + 64)
                        ins = tt(hst[q, :, c, :], hst[q, :, c, :],
                                 pools[par][q, 0:CB * N].rearrange("p (f v) -> p f v", f=CB), ALU.add)
                    ins.then_inc(S["z_out"], 1)
                if m == 2:
                    for n in range(H):
                        f, par = n // 2, n % 2
                        q = slice(64 * par, 64 * par + 64)
                        dve.wait_ge(S["zs_ps"], H * l + n + 1)
                        tt(hst[q, f, 1:9, :], hst[q, f, 1:9, :],
                           pools[2 + par][q, :].rearrange("p (b v) -> p b v", b=NS), ALU.add).then_inc(S["zs_out"], 1)
                for n in range(H):
                    f, par = n // 2, n % 2
                    q = slice(64 * par, 64 * par + 64)
                    k = H * (3 * l + m) + n
                    dve.wait_ge(S["o_ps"], k + 1)
                    tt(o_t[q, f, t0:t0 + nt], ov[q, f, 0:nt], pools[4 + par][q, 0:nt], ALU.add).then_inc(S["o_out"], 1)
                if m < 2:
                    dve.wait_ge(S["z_out"], 9 * l + 4 * (m + 1) + l + 1)
                    v.tensor_copy(zcar, hst[:, :, 3, :]).then_inc(S["zcar_out"], 1)

            def ffn():
                dve.wait_ge(S["rw_out"], 16)
                norm(1, pv[:, 0, PV["norm_ffn"][0]:PV["norm_ffn"][0] + DC], h)
                for n in range(CF):
                    dve.wait_ge(S["up_silu"], n + 1)
                    v.tensor_tensor(act[:, n, :], silu_s[:, n % 2, :], pools[2 * (n % 2) + 1][:, 0:T], ALU.mult)\
                        .then_inc(S["up_out"], 1)
                for n in range(DC):
                    dve.wait_ge(S["down_ps"], n + 1)
                    v.tensor_tensor(x[:, n, :], x[:, n, :], pools[4 + n % 4][:, 0:T], ALU.add).then_inc(S["down_out"], 1)
                dve.wait_ge(S["down_out"], DC)
                v.nop().then_inc(S["x_ready"], 1)

            def routing():
                tt, ts, stt = v.tensor_tensor, v.tensor_scalar, v.scalar_tensor_tensor
                step(v.memset(route, 0.0))
                dve.wait_ge(S["rw_out"], 32)
                norm(3, pv[:, 1, PV["norm_ffn"][0]:PV["norm_ffn"][0] + DC], h)
                dve.wait_ge(S["logit_ps"], 1)
                for m, (t0, nt, _) in enumerate(TILES):
                    step(v.tensor_copy(route[0:nt, 2, m, :], pools[1][0:nt, m * E:(m + 1) * E]))
                for m in range(3):
                    step(v.max(route[:, 3, m, :], route[:, 2, m, :]))
                    step(v.max_index(top_i[:, m, :], route[:, 3, m, :], route[:, 2, m, :]))
                step(v.tensor_copy(route[:, 4], top_i[:]))
                step(tt(route[:, 5, :, 0:1], route[:, 3, :, 0:1], route[:, 3, :, 1:2], ALU.subtract))
                tt(route[:, 5, :, 1:2], route[:, 3, :, 1:2], route[:, 3, :, 0:1], ALU.subtract).then_inc(S["gates_in"], 1)
                for m in range(3):
                    for i in range(2):
                        step(ts(route[:, 7 + i, m, :], iota[:, 0:E], route[:, 4, m, i:i + 1], None, ALU.is_equal))
                dve.wait_ge(S["gates_out"], 1)
                for m, (t0, nt, _) in enumerate(TILES):
                    step(tt(route[0:nt, 0, m, :], route[0:nt, 7, m, :], route[0:nt, 8, m, :], ALU.add))
                    for i in range(2):
                        step(ts(route[:, 7 + i, m, :], route[:, 7 + i, m, :], route[:, 6, m, i:i + 1], None, ALU.mult))
                    step(tt(route[0:nt, 1, m, :], route[0:nt, 7, m, :], route[0:nt, 8, m, :], ALU.add))
                v.nop().then_inc(S["count_in"], 1)
                dve.wait_ge(S["count_ps"], 1)
                for m, (t0, nt, _) in enumerate(TILES):
                    step(v.tensor_copy(route[0:nt, 10, m, :], pools[2][0:nt, m * E:(m + 1) * E]))
                step(v.tensor_reduce(route[:, 11, 0, 0:1], pools[2][:, 3 * E:4 * E], AX.X, ALU.max))
                step(ts(route[:, 11, 0, 1:2], route[:, 11, 0, 0:1], CAP + 0.5, 1.0, ALU.is_gt, ALU.add))
                step(ts(route[:, 11, 0, 2:3], route[:, 11, 0, 0:1], 2 * CAP + 0.5, None, ALU.is_gt))
                step(tt(route[:, 11, 0, 1:2], route[:, 11, 0, 1:2], route[:, 11, 0, 2:3], ALU.add))
                v.tensor_copy(n_int[:], route[:, 11, 0, 1:2]).then_inc(S["n_ready"], 1)
                v.nop().then_inc(S["count_out"], 1)

            def expert(e, i, moved=None):
                ts = v.tensor_scalar
                if moved is not None:
                    dve.wait_ge(S["place_moved"], moved)
                dve.wait_ge(S["sel_used"], i + 1)
                for m, (t0, nt, _) in enumerate(TILES):
                    def rc(k):
                        return route[0:nt, k, m, bass.ds(e, 1)]
                    ts(sel_p[0:nt, m, :], iota[0:nt], rc(10), rc(0), ALU.is_equal, ALU.mult)
                    ins = ts(sel_w[0:nt, m, :], iota[0:nt], rc(10), rc(1), ALU.is_equal, ALU.mult)
                ins.then_inc(S["sel_ready"], 1)
                for g in range(NG):
                    dve.wait_ge(S["eup_silu"], i * NG + (g + 1))
                    if g >= 2:
                        dve.wait_ge(S["et_ps"], i * NG + (g - 1))
                    v.tensor_tensor(act_e[:, g % 2, :], sil_e[:, g % 2, :], pools[g % 2][:, FW:2 * FW], ALU.mult)\
                        .then_inc(S["eup_act"], 1)
                for c in range(DC):
                    dve.wait_ge(S["em_ps"], i * DC + (c + 1))
                    v.tensor_tensor(x[:, c, :], x[:, c, :], pools[6 + c % 2][:, 0:T], ALU.add).then_inc(S["em_out"], 1)

            def experts():
                v.nop().then_inc(S["sel_used"], 1)
                for _ in range(2):
                    v.nop().then_inc(S["eup_act"], 1)
                    v.nop().then_inc(S["em_out"], 1)
                with dve.Fori(0, E) as e:
                    expert(e, e)
                npass = dve.value_load(n_int[0:1, 0:1], min_val=1, max_val=3)
                with dve.If(npass > 1):
                    with dve.Fori(1, npass) as p:
                        v.tensor_scalar(route[:, 10], route[:, 10], float(CAP), None, ALU.subtract)\
                            .then_inc(S["place_moved"], 1)
                        with dve.Fori(0, E) as e:
                            expert(e, p * E + e, moved=p)
                dve.wait_ge(S["em_out"], npass * (E * DC) + 2)
                v.nop().then_inc(S["x_ready"], 1)

            dve.wait_ge(S["consts"], N_CONST)
            discretise()
            mix(0)
            ffn()
            mix(1)
            routing()
            experts()
            norm(4, nfin[:], h)
            dve.wait_ge(S["h_ready"], 5)
            v.nop().then_inc(S["final_out"], 1)


def _constants():
    c = {"ones": np.ones((P, P)), "ident": np.eye(P), "iota": np.tile(np.arange(P), (P, 1)),
         "before": np.triu(np.ones((P, P)), 1)}
    i = np.arange(P)
    c["blk"] = (i[:, None] // N == i[None, :] // N) * 1.0

    def masks(chunk, half, r):
        same = chunk[:, None] == chunk[None, :]
        low, up = r[:, None] > r[None, :], r[:, None] < r[None, :]
        half_same = half[:, None] == half[None, :]
        return np.stack([same & half_same & low, same & half_same & up, same & ~half_same & up,
                         same & up, same & (r[:, None] <= r[None, :])], 1) * 1.0

    c["masks"] = masks(i // CH, i // 16, i)
    r = np.arange(TILES[2][1])
    chunk = np.where(r < 16, 0, r - 15)
    c["masks_s"] = masks(chunk, chunk, r)
    s = (i[:, None] // CH == np.arange(4)[None, :]) * 1.0
    c["sel_c"] = np.stack([s, -s], 1)
    s = (chunk[:, None] == np.arange(MAXC)[None, :]) * 1.0
    c["sel_s"] = np.stack([s, -s], 1)
    t = np.arange(T)
    c["keep"] = np.tile(((t % CH != 0) & (t < TP)) * 1.0, (P, 1))
    c["eps"] = np.tile(np.array([EPS_RMS, EPS_GN]), (P, 1))
    return {k: np.ascontiguousarray(v, dtype=np.float32) for k, v in c.items()}


def _cols(v):
    v = v.reshape(v.shape[:-1] + (-1, P))
    return np.moveaxis(v, -1, 0)


def _slot(parts):
    out = np.zeros((P, SLOT), np.float32)
    at = 0
    for w in parts:
        w = w.reshape(P, -1)
        out[:, at:at + w.shape[1]] = w
        at += w.shape[1]
    return out


def _tile(w, n):
    return w[:, n * P:(n + 1) * P].reshape(-1, P, P).transpose(1, 0, 2)


def _stream(i):
    slots = []
    for l in range(DEPTH):
        n = 0
        for k in WIN_TILES:
            slots.append(_slot([_tile(i["w_in"][l], n + j) for j in range(k)]))
            n += k
        for n in range(0, DC, 2):
            slots.append(_slot([_tile(i[w][l], n + j) for j in range(2) for w in ("s5_glu1", "s5_glu2")]))
        for n in range(0, DC, 4):
            slots.append(_slot([_tile(i["rw_w_bo"][l], n + j) for j in range(4)]))
        for n in range(0, DC, 2):
            slots.append(_slot([_tile(i["w_out"][l], n + j) for j in range(2)]))
        if l == 0:
            for n in range(CF):
                slots.append(_slot([_tile(i[w][0], n) for w in ("ffn_w1", "ffn_w3")]))
            blocks = [_tile(i["ffn_w2"][0], n)[:, k] for n in range(DC) for k in range(CF)]
            for b in range(0, len(blocks), 16):
                slots.append(_slot(blocks[b:b + 16]))
    slots = np.stack(slots)
    assert slots.shape[0] == S_DENSE
    up = [i[w][0].reshape(E, DC, P, NG, FW).transpose(0, 3, 2, 1, 4).reshape(E, NG, P, SLOT) for w in ("moe_w1", "moe_w3")]
    down = i["moe_w2"][0].reshape(E, NG, 2, P, D).transpose(0, 1, 3, 2, 4).reshape(E, NG, P, SLOT)
    experts = np.empty((E, S_EXPERT, P, SLOT), np.float32)
    n = 0
    for kind, g in expert_order():
        if kind == "up":
            experts[:, n], experts[:, n + 1] = up[0][:, g], up[1][:, g]
            n += 2
        else:
            experts[:, n] = down[:, g]
            n += 1
    return np.concatenate([slots, experts.reshape(E * S_EXPERT, P, SLOT)])


def layout(inputs):
    i = {k: np.asarray(v) for k, v in inputs.items()}
    a = _constants()
    a["wstream"] = _stream(i)
    a["x"] = _cols(np.concatenate([i["meta_tokens"], i["x_prompt"][0], i["x_sample"][:, 0]])).transpose(0, 2, 1)
    names = {"norm_mix": "norm_mix", "norm_ffn": "norm_ffn", "d": "s5_d", "mu": "rw_mu", "w0": "rw_w0", "a0": "rw_a0",
             "k_k": "rw_k_k", "k_a": "rw_k_a", "r_k": "rw_r_k", "gn_g": "rw_gn_g", "gn_b": "rw_gn_b"}
    a["pv"] = np.concatenate([_cols(i[names[k]].reshape(DEPTH, -1)) for k in PV], 2)
    a["nfin"] = _cols(i["norm_final"])

    def states(v):
        return _cols(v.reshape(DEPTH, G5 * S5P)).reshape(P, DEPTH * JT)

    a["lam"] = np.stack([states(i["s5_lam_re"]), states(i["s5_lam_im"]),
                         states(np.repeat(i["s5_log_dt"][:, :, None], S5P, 2))], 1)
    a["x0"] = np.stack([_cols(i[k].reshape(DEPTH, NS, -1)).transpose(0, 1, 3, 2) for k in ("state_s5_re", "state_s5_im")], 2)
    a["s0"] = i["state_rwkv"].reshape(DEPTH, NS, CB, 2, N, N).transpose(0, 3, 5, 2, 1, 4).reshape(DEPTH, P, CB, NS, N)
    a["shift0"] = _cols(i["state_shift"]).transpose(0, 1, 3, 2)
    a["router"] = i["moe_router"][0].reshape(DC, P, E).transpose(1, 0, 2)
    sb_, sc_ = np.zeros((DEPTH, P, CA, 2, P), np.float32), np.zeros((DEPTH, P, JT, 2, 32), np.float32)
    for c, (nb, ncc) in enumerate((("s5_b_re", "s5_c_re"), ("s5_b_im", "s5_c_im"))):
        for g in range(G5):
            j, half = g // 2, g % 2
            q = 32 * (j % 4) + S5C * half
            sb_[:, q:q + S5C, j // 4, c, S5P * half:S5P * (half + 1)] = i[nb][:, g].transpose(0, 2, 1)
            sc_[:, S5P * half:S5P * (half + 1), j, c, S5C * half:S5C * (half + 1)] = i[ncc][:, g].transpose(0, 2, 1)
    a["s5_b"], a["s5_c"] = sb_, sc_
    lo = np.empty((DEPTH, P, 2, DB), np.float32)
    lo[:, 0:64, 0], lo[:, 64:, 0], lo[:, :, 1] = i["rw_w_up"], i["rw_a_up"], i["rw_g_up"]
    a["lora_up"] = lo
    return {k: np.ascontiguousarray(v) for k, v in a.items()}


OUTS = {"y": (P, DC, T), "o_shift": (DEPTH, P, CR, 1 + NS), "o_s5": (DEPTH, P, JT, 2, 1 + NS),
        "o_rw": (DEPTH, P, CB, MAXC, N)}


def results(r):
    y = r["y"].transpose(2, 1, 0).reshape(T, D)
    sh = r["o_shift"].transpose(0, 3, 2, 1).reshape(DEPTH, 1 + NS, PRW)
    s5 = r["o_s5"].transpose(3, 0, 4, 2, 1).reshape(2, DEPTH, 1 + NS, G5, S5P)
    rw = r["o_rw"].reshape(DEPTH, 2, N, CB, MAXC, N).transpose(0, 4, 3, 1, 5, 2).reshape(DEPTH, MAXC, H, N, N)
    c = np.ascontiguousarray
    return (c(y[None, N_META:TP]), c(y[TP:, None]), c(s5[0, :, :1]), c(s5[1, :, :1]), c(rw[:, :1]), c(sh[:, :1]),
            c(s5[0, :, 1:]), c(s5[1, :, 1:]), c(rw[:, 1:]), c(sh[:, 1:]))


def kernel(**inputs):
    import concourse.bacc as bacc
    from concourse.bass_utils import run_bass_kernel_spmd

    nc = bacc.Bacc("TRN2", target_bir_lowering=False, num_devices=1)
    arrays = {f"{k}_dram": v for k, v in layout(inputs).items()}
    a = {k[:-5]: nc.dram_tensor(k, v.shape, F32, kind="ExternalInput").ap() for k, v in arrays.items()}
    for k, shape in OUTS.items():
        a[k] = nc.dram_tensor(f"{k}_dram", shape, F32, kind="ExternalOutput").ap()
    build(nc, a)
    r = run_bass_kernel_spmd(nc, [arrays], core_ids=[0]).results[0]
    return results({k: np.asarray(r[f"{k}_dram"]) for k in OUTS})
```

```python
import math
from contextlib import ExitStack

import numpy as np

import concourse.bass as bass
from concourse import mybir

ALU = mybir.AluOpType
ACT = mybir.ActivationFunctionType
AX = mybir.AxisListType
F32 = mybir.dt.float32
I32 = mybir.dt.int32
U32 = mybir.dt.uint32
F32R = mybir.dt.float32r

P = 128
DEPTH = 2
D = 1024
DC = D // P
N_META = 16
TP = 272
NS = 8
T = TP + NS
G5, S5P, S5C = 32, 64, 16
DA = G5 * S5C
CA = DA // P
JT = G5 * S5P // P
LEVELS = 9
H, N = 8, 64
DB = H * N
CB = DB // P
PRW = 3 * DB + 64 + 64 + 128
CR = PRW // P
PIN = DA + PRW + 2 * D
CIN = PIN // P
DFF = 2816
CF = DFF // P
E = 8
DE = 3584
FW = 256
NG = DE // FW
CAP = 128

CH = 32
TILES = [(0, 128, [(32 * c, 32) for c in range(4)]),
         (128, 128, [(32 * c, 32) for c in range(4)]),
         (256, 24, [(0, 16)] + [(16 + b, 1) for b in range(NS)])]
MAXC = 9

SLOT = 2048
RING = 7
WIN_TILES = [2] * 15 + [1] * 4
S_WIN, S_GLU, S_WBO, S_WOUT = len(WIN_TILES), 4, 2, 4
S_MIX = S_WIN + S_GLU + S_WBO + S_WOUT
S_FUP, S_FDOWN = CF, DC * CF // 16
S_DENSE = 2 * S_MIX + S_FUP + S_FDOWN
S_EXPERT = 3 * NG
assert S_DENSE % RING == 0 and S_EXPERT % RING == 0
MIX_AT = [0, S_MIX + S_FUP + S_FDOWN]
FFN_AT = S_MIX

PV = {}
_at = 0
for _n, _w in (("norm_mix", DC), ("norm_ffn", DC), ("d", CA), ("mu", CR), ("w0", CB), ("a0", CB),
               ("k_k", CB), ("k_a", CB), ("r_k", CB), ("gn_g", CB), ("gn_b", CB)):
    PV[_n] = (_at, _w)
    _at += _w
PVW = _at

EPS_RMS, EPS_GN = 1e-6, 64e-5
TWO_PI = 2 * math.pi
C1 = 6.28125
C2 = float(np.float32(TWO_PI - C1))
C3 = TWO_PI - C1 - C2
ROUND = 12582912.0
PI_IN = 3.1415925


SPLIT = 3


def expert_slots():
    order = []
    for g in range(NG + 2):
        if g < NG:
            order += [("w1", g), ("w3", g)]
        if g >= 2:
            order.append(("w2", g - 2))
    return order


ORDER = expert_slots()
SLOT_OF = {k: n for n, k in enumerate(ORDER)}
UP_DONE_BY = {min(SLOT_OF["w3", g] + SPLIT, S_EXPERT - 1): g for g in range(NG)}
TURNED_BY = {SLOT_OF["w1", g + 1] + SPLIT: g for g in range(NG - 1)}


def build(nc, a, debug=None):
    with ExitStack() as ctx:
        def sb(name, shape, dt=F32):
            return ctx.enter_context(nc.sbuf_tensor(name, shape, dt))

        def sem(name):
            return ctx.enter_context(nc.semaphore(name))

        arena = sb("arena", [P, 29472])
        arena_at = nc.sbuf_base - 4 * 29472

        def half(name, at, *shape):
            return nc.alloc_sbuf_tensor_at(name, [P, *shape], F32R, offset=arena_at + 4 * at).ap()

        ring = sb("ring", [P, RING, SLOT])
        x = sb("x", [P, DC, T])
        ones = sb("ones", [P, P])
        blk = sb("blk", [P, P])
        ident = sb("ident", [P, P])
        before = sb("before", [P, P])
        iota = sb("iota", [P, P])
        masks = sb("masks", [P, 5, P])
        masks_s = sb("masks_s", [24, 5, 24])
        sel_c = sb("sel_c", [P, 2, 4])
        sel_s = sb("sel_s", [24, 2, MAXC])
        keep = sb("keep", [P, T])
        eps = sb("eps", [P, 2])
        pv = sb("pv", [P, DEPTH, PVW])
        nfin = sb("nfin", [P, DC])
        lam = sb("lam", [P, 3, DEPTH * JT])
        x0 = sb("x0", [P, DEPTH, 2, JT, NS])
        s0 = sb("s0", [P, CB, NS, N])
        shift0 = sb("shift0", [P, DEPTH, CR, NS])
        router = sb("router", [P, DC, E])
        qq = sb("qq", [P, 3, DEPTH * JT])
        apow = sb("apow", [P, LEVELS, 3, DEPTH * JT])
        axt = sb("axt", [P, 2, JT, NS])
        rstd = sb("rstd", [P, 2, T])
        wend = sb("wend", [P, CB, MAXC + 8])
        s5out = sb("s5out", [P, JT, 2, 1 + NS])
        top_i = sb("top_i", [P, 3, E], U32)
        n_int = sb("n_int", [P, 1], I32)

        pools = [ctx.enter_context(nc.psum_tensor(f"bank{i}", [P, 512], F32)) for i in range(8)]

        def ar(at, *shape):
            n = 1
            for s in shape:
                n *= s
            v = arena[:, at:at + n]
            if len(shape) == 1:
                return v
            names = "abcd"[:len(shape)]
            return v.rearrange(f"p ({' '.join(names)}) -> p {' '.join(names)}",
                               **{k: s for k, s in zip(names[1:], shape[1:])})

        gate = ar(0, 2 * DC, T)
        h = ar(4480, DC, T)
        u = ar(6720, CA, T)
        s5_b = ar(7840, CA, 2, P)
        s5_c = ar(8864, JT, 2, 32)
        lora_up = ar(9888, 2, DB)
        prow = ar(10912, CR, T + 1)
        z = ar(14848, CR, T)
        sq = ar(14848, DC, T)
        s5x = ar(18768, 4, 2, T)
        y5 = ar(21008, CA, T)
        glu_s = ar(18768, 2, T)
        F0 = 20512
        small = ar(22128, 18, DEPTH * JT)
        kr = ar(F0, CB, 2, T)
        beta, chi, beta_e, chi_e, gg, bonus = (ar(F0 + CB * T * (2 + i), CB, T) for i in range(6))
        tmp = [ar(10912 + 1120 * i, CB, T) for i in range(3)] + [ar(4480 + 1120 * i, CB, T) for i in range(2)]
        o_t = z[:, 4:8, :]
        gpre, hst = ar(18208, CB, MAXC, N), ar(4480, CB, MAXC, N)
        rt, ov = ar(14848, CB, P), ar(15360, CB, P)
        U0 = 4480 + CB * MAXC * N
        un = [ar(U0 + 256 * i, 2, P) for i in range(13)]
        am, pm, a2, p2, e1, e2, xk, yk, zk, poff, akt, mbt, mkt = un
        U1 = U0 + 256 * 13
        v_tok, be_tok, ch_tok = (ar(U1 + P * i, 2, N) for i in range(3))
        v_bd, be_bd, nx_bd = (ar(U1 + 3 * P + 1152 * i, 2, MAXC, N) for i in range(3))
        act = ar(10912, CF, T)
        silu_s = ar(17072, 2, T)
        zcar = ar(14300, CB, N)
        route = ar(14560, 12, 3, E)
        chosen, weight, place = (ar(18124 + 30 * i, 3, E + 2) for i in range(3))
        w_hi = [half(f"w_hi{i}", at, SLOT) for i, at in enumerate((0, 18240, 22336))]
        w_lo = [half(f"w_lo{i}", at, SLOT) for i, at in enumerate((2048, 20288, 24384))]
        he_hi, he_lo = half("he_hi", 26432, DC, CAP), half("he_lo", 27456, DC, CAP)
        at_hi, at_lo = half("at_hi", 28480, 2, 2 * CAP), half("at_lo", 6720, 2, 2 * CAP)
        h_tok = ar(7840, 3, D)
        sel_p, sel_w = ar(11936, 3, CAP), ar(12320, 3, CAP)
        mix_w = ar(12704, T)
        sil_e, act_e = ar(13000, 2, FW), ar(13512, 2, FW)
        y_e = ar(17100, D)

        names = ["first_in", "consts", "small_w", "s0_in", "shift_out", "s5_out", "rw_out", "y_stored", "final_out",
                 "norm_sq", "norm_ps", "norm_rt", "h_ready", "x_ready",
                 "disc_exp1", "disc_ang", "disc_exp2", "disc_done",
                 "proj_ps", "proj_out", "pad_zero",
                 "act_quad", "act_oct", "e1_out", "zcar_out", "place_moved", "bu_ps", "bu_q", "bu_used", "scan_done", "y5_ps", "y5_mix", "y5_done",
                 "lora_ps", "lora_in", "lora_out", "z_ready", "kk_sq", "kk_ps", "kk_norm", "cum_ready",
                 "exps_ready", "bonus_in", "bonus_ps", "fm_ready",
                 "glu_ps", "glu_sig", "glu_out",
                 "tr_ps", "tr_out", "gram_ps", "gram_out", "sq_ps", "sq_out", "quad_ps", "quad_out",
                 "oct_ps", "oct_out", "e8_ps", "e8_out", "y_ps", "y_out", "off_ps", "off_out",
                 "fix_ps", "x_out", "gh_ps", "h_out", "gh_out", "ro_ps", "ro_out", "ov_out",
                 "z_ps", "z_out", "zs_ps", "zs_out", "o_ps", "o_out", "o_mean_ps", "o_cent", "o_sq",
                 "o_var_ps", "o_std", "o_ready", "bo_ps", "bo_out", "wo_ps", "wo_out",
                 "up_ps", "up_silu", "up_out", "down_ps", "down_out",
                 "logit_ps", "logit_out", "gates_in", "gates_out", "ht_ps", "ht_out", "count_in",
                 "count_ps", "count_out", "hi_ready", "slot_done", "selp_ready", "selw_ready", "ga_ps", "ga_hi", "ga_lo",
                 "mw_ps", "mw_out", "eup_silu", "eup_act", "et_ps", "et_hi", "et_lo", "ey_out", "em_ps", "em_out",
                 "weights_used", "dve_step", "n_ready"]
        S = {n: sem(n) for n in names}
        slot_in = [sem(f"slot_in{i}") for i in range(RING)]
        nconsts = [0]
        block = ctx.enter_context(nc.Block())

        def slot(n):
            return ring[:, n % RING, :]

        FIRST = [(x, "x"), (lam, "lam"), (ones, "ones"), (eps, "eps"), (pv, "pv")]
        CONSTS = [(blk, "blk"), (ident, "ident"), (before, "before"), (iota, "iota"),
                  (masks, "masks"), (masks_s, "masks_s"), (sel_c, "sel_c"), (sel_s, "sel_s"),
                  (keep, "keep"), (nfin, "nfin"), (x0, "x0"), (shift0, "shift0"), (router, "router")]
        N_FIRST, N_CONST = 16 * len(FIRST), 16 * len(CONSTS)

        @block.sync
        def _(sp):
            for t, n in FIRST:
                sp.dma_start(t[:], a[n]).then_inc(S["first_in"], 16)
            for s in range(RING):
                sp.dma_start(ring[:, s, :], a["wstream"][s]).then_inc(slot_in[s], 16)
            with sp.Fori(1, (S_DENSE + E * S_EXPERT) // RING) as r:
                for s in range(RING):
                    sp.wait_ge(S["weights_used"], r * RING + (s - RING + 1))
                    sp.dma_start(ring[:, s, :], a["wstream"][bass.ds(r * RING + s, 1)].rearrange("o p n -> (o p) n"))\
                        .then_inc(slot_in[s], 16)
            sp.wait_ge(S["n_ready"], 1)
            npass = sp.value_load(n_int[0:1, 0:1], min_val=1, max_val=3)
            with sp.If(npass > 1):
                with sp.Fori(1, npass) as p:
                    with sp.Fori(0, E * S_EXPERT // RING) as r:
                        for s in range(RING):
                            sp.wait_ge(S["weights_used"], p * (E * S_EXPERT) + r * RING + (S_DENSE + s - RING + 1))
                            sp.dma_start(ring[:, s, :], a["wstream"][bass.ds(r * RING + (S_DENSE + s), 1)]
                                         .rearrange("o p n -> (o p) n")).then_inc(slot_in[s], 16)

        @block.gpsimd
        def _(pool):
            for l in range(DEPTH):
                if l:
                    pool.wait_ge(S["x_ready"], 2 * l - 1)
                pool.dma_start(s5_b, a["s5_b"][l]).then_inc(S["small_w"], 16)
                pool.dma_start(s5_c, a["s5_c"][l]).then_inc(S["small_w"], 16)
                pool.dma_start(lora_up, a["lora_up"][l]).then_inc(S["small_w"], 16)
                pool.dma_start(s0[:], a["s0"][l]).then_inc(S["s0_in"], 16)
                pool.wait_ge(S["proj_out"], CIN * l + CA + CR)
                pool.dma_start(a["o_shift"][l], prow[:, :, TP:T + 1]).then_inc(S["shift_out"], 16)
                pool.wait_ge(S["scan_done"], JT * (l + 1))
                pool.dma_start(a["o_s5"][l], s5out[:]).then_inc(S["s5_out"], 16)
                pool.wait_ge(S["zs_out"], H * (l + 1))
                pool.dma_start(a["o_rw"][l], hst).then_inc(S["rw_out"], 16)
            for n in ("shift_out", "s5_out", "rw_out"):
                pool.wait_ge(S[n], 16 * DEPTH)
            pool.wait_ge(S["final_out"], 1)
            pool.dma_start(a["y"], h).then_inc(S["y_stored"], 16)
            pool.wait_ge(S["y_stored"], 16)

        units = [(m, f) for m in range(3) for f in range(CB)]
        NU = len(units)

        @block.tensor
        def _(pe):
            def mm(out, lhsT, rhs, start=True, stop=True, **k):
                return nc.tensor.matmul(out, lhsT, rhs, start=start, stop=stop, **k)

            def products(out, pairs, done, release=False):
                for i, (w, r) in enumerate(pairs):
                    ins = mm(out, w, r, i == 0, i == len(pairs) - 1)
                    if i == 0 and release:
                        ins.then_inc(S["weights_used"], 1)
                if done is not None:
                    ins.then_inc(S[done], 1)

            def give_back():
                pe.nop().then_inc(S["weights_used"], 1)

            def arrived(n):
                pe.wait_ge(slot_in[n % RING], 16 * (n // RING + 1))

            def norm(i):
                pe.wait_ge(S["norm_sq"], i + 1)
                for c in range(DC):
                    last = mm(pools[0][:, 0:T], ones[:], sq[:, c, :], c == 0, c == DC - 1)
                last.then_inc(S["norm_ps"], 1)

            def proj_tile(l, n, at):
                s, j = at
                if j == 0:
                    arrived(s)
                if n >= 3:
                    pe.wait_ge(S["proj_out"], CIN * l + n - 2)
                w = slot(s).rearrange("p (j k m) -> p j k m", j=2, k=DC)
                products(pools[n % 3][:, 0:T], [(w[:, j, k, :], h[:, k, :]) for k in range(DC)], "proj_ps",
                         release=j == 0 and n > 0)

            def bu_tile(l, j):
                aa, b = j // 4, j % 4
                if j == 0:
                    pe.wait_ge(S["small_w"], 48 * (l + 1))
                    pe.wait_ge(S["proj_out"], CIN * l + CA)
                if j >= 2:
                    pe.wait_ge(S["bu_used"], JT * l + j - 1)
                for c in range(2):
                    last = mm(pools[4 + 2 * (j % 2) + c][:, 0:T], s5_b[32 * b:32 * b + 32, aa, c, :],
                              u[32 * b:32 * b + 32, aa, :])
                last.then_inc(S["bu_ps"], 1)

            def y5_tile(l, j):
                aa, b = j // 4, j % 4
                pe.wait_ge(S["scan_done"], JT * l + j + 1)
                if b == 0 and j:
                    pe.wait_ge(S["y5_mix"], CA * l + aa)
                for c in range(2):
                    last = mm(pools[3][32 * b:32 * b + 32, 0:T], s5_c[:, j, c, :], s5x[:, j % 4, c, :],
                              c == 0, c == 1)
                last.then_inc(S["y5_ps"], 1)

            def glu(l):
                base = MIX_AT[l] + S_WIN
                pe.wait_ge(S["y5_done"], CA * (l + 1))
                for n in range(DC):
                    s = base + n // 2
                    if n % 2 == 0:
                        arrived(s)
                    if n >= 2:
                        pe.wait_ge(S["glu_out"], DC * l + n - 1)
                    w = slot(s).rearrange("p (j c k m) -> p j c k m", j=2, c=2, k=CA)
                    for c in range(2):
                        products(pools[2 * (n % 2) + c][:, 0:T], [(w[:, n % 2, c, k, :], y5[:, k, :]) for k in range(CA)],
                                 "glu_ps" if c else None, release=c == 0 and n % 2 == 0 and n > 0)
                pe.wait_ge(S["glu_out"], DC * (l + 1))
                give_back()

            def rwkv_features(l):
                pe.wait_ge(S["lora_in"], l + 1)
                pe.wait_ge(S["bu_used"], JT * (l + 1))
                for i in range(3):
                    for f in range(CB):
                        n = 4 * i + f
                        if n >= 4:
                            pe.wait_ge(S["lora_out"], 3 * CB * l + n - 3)
                        o = pools[4 + n % 4][:, 0:T]
                        if i < 2:
                            last = mm(o, lora_up[64 * i:64 * i + 64, 0, f * P:(f + 1) * P],
                                      z[64 * i:64 * i + 64, 12, :])
                        else:
                            last = mm(o, lora_up[:, 1, f * P:(f + 1) * P], z[:, 13, :])
                        last.then_inc(S["lora_ps"], 1)
                pe.wait_ge(S["kk_sq"], l + 1)
                pe.wait_ge(S["lora_out"], 3 * CB * (l + 1))
                for f in range(CB):
                    last = mm(pools[4 + f][:, 0:T], blk[:], tmp[0][:, f, :])
                last.then_inc(S["kk_ps"], 1)
                pe.wait_ge(S["bonus_in"], l + 1)
                for f in range(CB):
                    last = mm(pools[4 + f][:, 0:T], blk[:], bonus[:, f, :])
                last.then_inc(S["bonus_ps"], 1)

            def unit(l, m, f):
                t0, nt, chunks = TILES[m]
                n_u = NU * l + CB * m + f
                tok = slice(t0, t0 + nt)
                if m == 0 and f == 0:
                    pe.wait_ge(S["fm_ready"], l + 1)
                if n_u:
                    pe.wait_ge(S["gh_out"], n_u)
                    pe.wait_ge(S["ro_out"], n_u)
                    pe.wait_ge(S["ov_out"], n_u)
                    pe.wait_ge(S["h_out"], n_u)
                    if f == 0:
                        pe.wait_ge(S["o_out"], H * (3 * l + m))
                for i, src in enumerate((kr[:, f, 0, tok], z[:, 8 + f, tok], beta_e[:, f, tok], chi_e[:, f, tok])):
                    last = nc.tensor.transpose(pools[0][0:nt, i * P:(i + 1) * P], src, ident[:])
                last.then_inc(S["tr_ps"], 1)
                for par in range(2):
                    q = slice(64 * par, 64 * par + 64)
                    mm(pools[1 + par][0:nt, 0:nt], kr[q, f, 0, tok], beta[q, f, tok])
                    mm(pools[3 + par][0:nt, 0:2 * nt].rearrange("p (c t) -> p c t", c=2), beta[q, f, tok], kr[q, f, :, tok])
                    last = mm(pools[5 + par][0:nt, 0:2 * nt].rearrange("p (c t) -> p c t", c=2), chi[q, f, tok], kr[q, f, :, tok])
                last.then_inc(S["gram_ps"], 1)
                pe.wait_ge(S["tr_out"], n_u + 1)
                pe.wait_ge(S["gram_out"], n_u + 1)
                for par in range(2):
                    mm(pools[1][0:nt, par * P:par * P + nt], pm[0:nt, par, 0:nt], am[0:nt, par, 0:nt])
                    mm(pools[1][0:nt, (2 + par) * P:(2 + par) * P + nt], am[0:nt, par, 0:nt], pm[0:nt, par, 0:nt])
                    last = mm(pools[2][0:nt, par * N:(par + 1) * N], akt[0:nt, par, 0:nt], v_tok[0:nt, par, :])
                last.then_inc(S["sq_ps"], 1)
                pe.wait_ge(S["sq_out"], n_u + 1)
                pe.wait_ge(S["e1_out"], n_u + 1)
                for par in range(2):
                    mm(pools[3][0:nt, par * P:par * P + nt], p2[0:nt, par, 0:nt], a2[0:nt, par, 0:nt])
                    mm(pools[3][0:nt, (2 + par) * P:(2 + par) * P + nt], a2[0:nt, par, 0:nt], p2[0:nt, par, 0:nt])
                    last = mm(pools[4][0:nt, par * P:par * P + nt], a2[0:nt, par, 0:nt], e1[0:nt, par, 0:nt])
                last.then_inc(S["quad_ps"], 1)
                pe.wait_ge(S["quad_out"], n_u + 1)
                for par in range(2):
                    mm(pools[5][0:nt, par * P:par * P + nt], pm[0:nt, par, 0:nt], am[0:nt, par, 0:nt])
                    last = mm(pools[6][0:nt, par * P:par * P + nt], am[0:nt, par, 0:nt], e2[0:nt, par, 0:nt])
                last.then_inc(S["oct_ps"], 1)
                pe.wait_ge(S["oct_out"], n_u + 1)
                for par in range(2):
                    last = mm(pools[1][0:nt, par * P:par * P + nt], a2[0:nt, par, 0:nt], e1[0:nt, par, 0:nt])
                last.then_inc(S["e8_ps"], 1)
                pe.wait_ge(S["e8_out"], n_u + 1)
                for par in range(2):
                    last = mm(pools[2][0:nt, par * P:(par + 1) * P], e2[0:nt, par, 0:nt], xk[0:nt, par, :])
                last.then_inc(S["y_ps"], 1)
                pe.wait_ge(S["y_out"], n_u + 1)
                for par in range(2):
                    last = mm(pools[3][0:nt, par * P:(par + 1) * P], poff[0:nt, par, 0:nt], yk[0:nt, par, :])
                last.then_inc(S["off_ps"], 1)
                pe.wait_ge(S["off_out"], n_u + 1)
                for par in range(2):
                    last = mm(pools[4][0:nt, par * P:(par + 1) * P], e2[0:nt, par, 0:nt], zk[0:nt, par, :])
                last.then_inc(S["fix_ps"], 1)
                pe.wait_ge(S["x_out"], n_u + 1)
                ncn = len(chunks)
                for par in range(2):
                    q = slice(64 * par, 64 * par + 64)
                    c0 = 0
                    for bank_g, bank_h, w in ((5, 6, min(8, ncn)), (1, 2, ncn - 8)):
                        if w <= 0:
                            continue
                        bd = slice(c0, c0 + w)
                        def cv(t, w=w):
                            return t[q, 0:w * N].rearrange("p (c v) -> p c v", c=w)
                        mm(cv(pools[bank_g]), xk[0:nt, par, 0:N], be_bd[0:nt, par, bd, :])
                        mm(cv(pools[bank_h]), ch_tok[0:nt, par, :], v_bd[0:nt, par, bd, :], True, False)
                        last = mm(cv(pools[bank_h]), be_tok[0:nt, par, :], nx_bd[0:nt, par, bd, :], False, True)
                        c0 += w
                last.then_inc(S["gh_ps"], 1)
                for par in range(2):
                    q = slice(64 * par, 64 * par + 64)
                    mm(pools[3][q, 0:nt], xk[0:nt, par, 0:N], mbt[0:nt, par, 0:nt])
                    mm(pools[7][q, 0:nt], zk[0:nt, par, 0:N], mbt[0:nt, par, 0:nt], True, False)
                    last = mm(pools[7][q, 0:nt], v_tok[0:nt, par, :], mkt[0:nt, par, 0:nt], False, True)
                last.then_inc(S["ro_ps"], 1)

            def chain(l, m):
                t0, nt, chunks = TILES[m]
                k = NU * l + CB * (m + 1)
                pe.wait_ge(S["gh_out"], k)
                pe.wait_ge(S["h_out"], k)
                pe.wait_ge(S["ro_out"], k)
                pe.wait_ge(S["ov_out"], k)
                seq = 4 if m < 2 else 1
                if m:
                    pe.wait_ge(S["zcar_out"], 2 * l + m)
                for c in range(seq):
                    n_c = 9 * l + 4 * m + c
                    pe.wait_ge(S["z_out"], n_c + l + 1)
                    for f in range(CB):
                        for par in range(2):
                            q = slice(64 * par, 64 * par + 64)
                            src = zcar[q, f, :] if c == 0 else hst[q, f, c - 1, :]
                            last = mm(pools[par][q, f * N:(f + 1) * N], gpre[q, f, c, :], src)
                    last.then_inc(S["z_ps"], 1)
                if m == 2:
                    pe.wait_ge(S["s0_in"], 16 * (l + 1))
                    for f in range(CB):
                        for par in range(2):
                            n = 2 * f + par
                            q = slice(64 * par, 64 * par + 64)
                            if n >= 2:
                                pe.wait_ge(S["zs_out"], H * l + n - 1)
                            for b in range(NS):
                                last = mm(pools[2 + par][q, b * N:(b + 1) * N], gpre[q, f, 1 + b, :], s0[q, f, b, :])
                            last.then_inc(S["zs_ps"], 1)
                for f in range(CB):
                    for par in range(2):
                        n = 2 * f + par
                        q = slice(64 * par, 64 * par + 64)
                        k = H * (3 * l + m) + n
                        if k >= 2:
                            pe.wait_ge(S["o_out"], k - 1)
                        for c, (r0, w) in enumerate(chunks):
                            if m == 2 and c:
                                src = s0[q, f, c - 1, :]
                            else:
                                src = zcar[q, f, :] if c == 0 else hst[q, f, c - 1, :]
                            last = mm(pools[4 + par][q, r0:r0 + w], src, rt[q, f, r0:r0 + w])
                        last.then_inc(S["o_ps"], 1)

            def finish_rwkv(l):
                pe.wait_ge(S["o_out"], 3 * H * (l + 1))
                for f in range(CB):
                    last = mm(pools[f][:, 0:T], blk[:], o_t[:, f, :])
                last.then_inc(S["o_mean_ps"], 1)
                pe.wait_ge(S["o_sq"], l + 1)
                for f in range(CB):
                    last = mm(pools[4 + f][:, 0:T], blk[:], tmp[1][:, f, :])
                last.then_inc(S["o_var_ps"], 1)
                pe.wait_ge(S["o_ready"], l + 1)
                base = MIX_AT[l] + S_WIN + S_GLU
                for n in range(DC):
                    s = base + n // 4
                    if n % 4 == 0:
                        arrived(s)
                    if n >= 4:
                        pe.wait_ge(S["bo_out"], DC * l + n - 3)
                    w = slot(s).rearrange("p (j k m) -> p j k m", j=4, k=CB)
                    products(pools[n % 4][:, 0:T], [(w[:, n % 4, k, :], o_t[:, k, :]) for k in range(CB)], "bo_ps",
                             release=n == 4)
                base += S_WBO
                pe.wait_ge(S["bo_out"], DC * (l + 1))
                give_back()
                for n in range(DC):
                    s = base + n // 2
                    if n % 2 == 0:
                        arrived(s)
                    if n >= 4:
                        pe.wait_ge(S["wo_out"], DC * l + n - 3)
                    w = slot(s).rearrange("p (j k m) -> p j k m", j=2, k=DC)
                    products(pools[4 + n % 4][:, 0:T], [(w[:, n % 2, k, :], gate[:, k, :]) for k in range(DC)], "wo_ps",
                             release=n % 2 == 0 and n > 0)
                pe.wait_ge(S["wo_out"], DC * (l + 1))
                give_back()

            def mix(l):
                norm(2 * l)
                pe.wait_ge(S["h_ready"], 2 * l + 1)
                pe.wait_ge(S["consts"], N_CONST)
                at, n = [], 0
                for s, k in enumerate(WIN_TILES):
                    at += [(MIX_AT[l] + s, j) for j in range(k)]
                for n in range(CA):
                    proj_tile(l, n, at[n])
                n = CA
                for j in range(JT):
                    bu_tile(l, j)
                    for _ in range(2):
                        if n < CIN:
                            proj_tile(l, n, at[n])
                            n += 1
                    if j >= 4:
                        y5_tile(l, j - 4)
                pe.wait_ge(S["proj_out"], CIN * (l + 1))
                give_back()
                for j in range(JT - 4, JT):
                    y5_tile(l, j)
                glu(l)
                rwkv_features(l)
                for m in range(3):
                    for f in range(CB):
                        unit(l, m, f)
                    chain(l, m)
                finish_rwkv(l)

            def ffn():
                norm(1)
                pe.wait_ge(S["h_ready"], 2)
                for n in range(CF):
                    s = FFN_AT + n
                    arrived(s)
                    if n >= 2:
                        pe.wait_ge(S["up_out"], n - 1)
                    w = slot(s).rearrange("p (c k m) -> p c k m", c=2, k=DC)
                    for c in range(2):
                        products(pools[2 * (n % 2) + c][:, 0:T], [(w[:, c, k, :], h[:, k, :]) for k in range(DC)],
                                 "up_ps" if c else None, release=c == 0 and n > 0)
                pe.wait_ge(S["up_out"], CF)
                give_back()
                for n in range(DC):
                    if n >= 4:
                        pe.wait_ge(S["down_out"], n - 3)
                    for k in range(CF):
                        b = n * CF + k
                        s = FFN_AT + S_FUP + b // 16
                        if b % 16 == 0:
                            arrived(s)
                        last = mm(pools[4 + n % 4][:, 0:T], slot(s)[:, (b % 16) * P:(b % 16 + 1) * P], act[:, k, :],
                                  k == 0, k == CF - 1)
                        if k == CF - 1:
                            last.then_inc(S["down_ps"], 1)
                        elif b % 16 == 15:
                            last.then_inc(S["weights_used"], 1)
                assert (DC * CF) % 16 == 0
                pe.wait_ge(S["down_out"], DC)
                give_back()

            def routing():
                norm(3)
                pe.wait_ge(S["h_ready"], 4)
                for m, (t0, nt, _) in enumerate(TILES):
                    for k in range(DC):
                        last = mm(pools[1][0:nt, m * E:(m + 1) * E], h[:, k, t0:t0 + nt], router[:, k, :], k == 0, k == DC - 1)
                last.then_inc(S["logit_ps"], 1)
                for m, (t0, nt, _) in enumerate(TILES):
                    for half in range(2):
                        n = 2 * m + half
                        if n >= 4:
                            pe.wait_ge(S["ht_out"], n - 3)
                        for j in range(4):
                            last = nc.tensor.transpose(pools[4 + n % 4][0:nt, j * P:(j + 1) * P],
                                                       h[:, 4 * half + j, t0:t0 + nt], ident[:])
                        last.then_inc(S["ht_ps"], 1)
                pe.wait_ge(S["count_in"], 1)
                for m, (t0, nt, _) in enumerate(TILES):
                    o = pools[2][0:nt, m * E:(m + 1) * E]
                    for mp in range(m):
                        mm(o, ones[:, 0:nt], chosen[:, mp, 1:E + 1], mp == 0, False)
                    mm(o, before[0:nt, 0:nt], chosen[0:nt, m, 1:E + 1], m == 0, True)
                for m, (t0, nt, _) in enumerate(TILES):
                    last = mm(pools[2][:, 3 * E:4 * E], ones[0:nt, :], chosen[0:nt, m, 1:E + 1], m == 0, m == 2)
                last.then_inc(S["count_ps"], 1)

            def split_products(out, w, r, start, stop, done=None):
                (wh, wl), (rh, rl) = w, r
                first = mm(out, wh, rh, start, False)
                mm(out, wh, rl, False, False)
                last = mm(out, wl, rh, False, stop)
                return first, last

            def gather(k, half_):
                for j in range(4):
                    for m, (t0, nt, _) in enumerate(TILES):
                        last = mm(pools[7 - half_][:, j * P:(j + 1) * P],
                                  h_tok[0:nt, m, (4 * half_ + j) * P:(4 * half_ + j + 1) * P],
                                  sel_p[0:nt, m, :], m == 0, m == 2)
                last.then_inc(S["ga_ps"], 1)

            def weights_to_rows(k):
                pe.wait_ge(S["selw_ready"], k + 1)
                for m, (t0, nt, _) in enumerate(TILES):
                    last = nc.tensor.transpose(pools[6][:, t0:t0 + nt], sel_w[0:nt, m, :], ident[0:nt, 0:nt])
                last.then_inc(S["mw_ps"], 1)

            def combine(k):
                pe.wait_ge(S["mw_out"], k + 1)
                pe.wait_ge(S["ey_out"], k + 1)
                for c in range(DC):
                    if c >= 2:
                        pe.wait_ge(S["em_out"], k * DC + (c - 1))
                    mm(pools[6 + c % 2][:, 0:T], y_e[:, c * P:(c + 1) * P], mix_w).then_inc(S["em_ps"], 1)

            def expert(i, k):
                pe.wait_ge(S["ga_lo"], k * 2 + 2)
                n = 0
                for g in range(NG + 2):
                    for part in range(2):
                        if g < NG:
                            pe.wait_ge(S["weights_used"], i * S_EXPERT + (S_DENSE + n + 1))
                            w_h, w_l = (t[n % SPLIT].rearrange("p (k m) -> p k m", k=DC) for t in (w_hi, w_lo))
                            for c in range(DC):
                                _, last = split_products(pools[g % 2][:, part * FW:(part + 1) * FW],
                                                         (he_hi[:, c, :], he_lo[:, c, :]), (w_h[:, c, :], w_l[:, c, :]),
                                                         c == 0, c == DC - 1)
                            last.then_inc(S["slot_done"], 1)
                            n += 1
                        if part == 0 and g == 0:
                            weights_to_rows(k)
                        if part == 0 and 1 <= g <= NG:
                            pe.wait_ge(S["eup_act"], i * NG + g)
                            for j in range(2):
                                last = nc.tensor.transpose(pools[2 + (g - 1) % 2][:, j * P:(j + 1) * P],
                                                           act_e[:, (g - 1) % 2, j * P:(j + 1) * P], ident[:])
                            last.then_inc(S["et_ps"], 1)
                        if g == NG and part == 0:
                            pe.wait_ge(S["em_out"], k * DC + DC)
                            pe.wait_ge(S["selp_ready"], k + 2)
                            gather(k, 0)
                    if g == 0:
                        combine(k)
                    if g >= 2:
                        pe.wait_ge(S["weights_used"], i * S_EXPERT + (S_DENSE + n + 1))
                        pe.wait_ge(S["et_lo"], i * NG + (g - 1))
                        if g == 2:
                            pe.wait_ge(S["ey_out"], k + 1)
                        w_h, w_l = (t[n % SPLIT].rearrange("p (k m) -> p k m", k=2) for t in (w_hi, w_lo))
                        for j in range(2):
                            q = slice(j * CAP, (j + 1) * CAP)
                            for hf in range(2):
                                _, last = split_products(pools[4 + hf][:], (at_hi[:, g % 2, q], at_lo[:, g % 2, q]),
                                                         (w_h[:, j, hf * 512:(hf + 1) * 512], w_l[:, j, hf * 512:(hf + 1) * 512]),
                                                         g == 2 and j == 0, g == NG + 1 and j == 1)
                        last.then_inc(S["slot_done"], 1)
                        n += 1
                        if g == NG:
                            gather(k, 1)

            def one_pass(p, i0, k0):
                pe.wait_ge(S["selp_ready"], k0 + 1)
                gather(k0, 0)
                gather(k0, 1)
                with pe.Fori(0, E) as e:
                    expert(e + i0, e + k0)
                weights_to_rows(k0 + E)
                combine(k0 + E)

            def experts():
                pe.wait_ge(S["count_out"], 1)
                pe.wait_ge(S["ht_out"], 6)
                one_pass(0, 0, 0)
                pe.wait_ge(S["n_ready"], 1)
                npass = pe.value_load(n_int[0:1, 0:1], min_val=1, max_val=3)
                with pe.If(npass > 1):
                    with pe.Fori(1, npass) as p:
                        pe.wait_ge(S["em_out"], p * (DC * (E + 1)))
                        one_pass(p, p * E, p * (E + 1))

            pe.wait_ge(S["first_in"], N_FIRST)
            mix(0)
            ffn()
            mix(1)
            routing()
            experts()
            norm(4)

        @block.scalar
        def _(ac):
            for t, n in CONSTS:
                ac.dma_start(t[:], a[n]).then_inc(S["consts"], 16)

            def fn(out, in_, func, **k):
                return nc.scalar.activation(out, in_, func, **k)

            def norm(i):
                if i:
                    ac.wait_ge(S["x_ready"], i)
                fn(sq, x[:], ACT.Square).then_inc(S["norm_sq"], 1)
                ac.wait_ge(S["norm_ps"], i + 1)
                fn(rstd[:, 0, :], pools[0][:, 0:T], ACT.Sqrt, scale=1.0 / D, bias=eps[:, 0:1]).then_inc(S["norm_rt"], 1)

            def proj_out(l, n):
                ac.wait_ge(S["proj_ps"], CIN * l + n + 1)
                src = pools[n % 3][:, 0:T]
                if n < CA:
                    ins = fn(u[:, n, :], src, ACT.Identity)
                elif n < CA + CR:
                    ins = fn(prow[:, n - CA, 1:T + 1], src, ACT.Identity)
                else:
                    ins = fn(gate[:, n - CA - CR, :], src, ACT.Sigmoid)
                ins.then_inc(S["proj_out"], 1)

            def bu_out(l, j):
                ac.wait_ge(S["bu_ps"], JT * l + j + 1)
                if j >= 4:
                    ac.wait_ge(S["y5_ps"], JT * l + j - 3)
                q = qq[:, 0, JT * l + j:JT * l + j + 1]
                for c in range(2):
                    ins = fn(s5x[:, j % 4, c, :], pools[4 + 2 * (j % 2) + c][:, 0:T], ACT.Identity, scale=q)
                ins.then_inc(S["bu_q"], 1)

            def mix(l):
                if l:
                    norm(2 * l)
                for n in range(CA):
                    proj_out(l, n)
                n = CA
                ac.wait_ge(S["disc_done"], 1)
                for j in range(2):
                    bu_out(l, j)
                    for _ in range(2):
                        proj_out(l, n)
                        n += 1
                for j in range(2, JT):
                    bu_out(l, j)
                    for _ in range(2):
                        if n < CIN:
                            proj_out(l, n)
                            n += 1
                for aa in range(CA):
                    ac.wait_ge(S["y5_mix"], CA * l + aa + 1)
                    fn(y5[:, aa, :], y5[:, aa, :], ACT.Gelu_apprx_tanh).then_inc(S["y5_done"], 1)
                for n in range(DC):
                    ac.wait_ge(S["glu_ps"], DC * l + n + 1)
                    if n >= 2:
                        ac.wait_ge(S["glu_out"], DC * l + n - 1)
                    fn(glu_s[:, n % 2, :], pools[2 * (n % 2) + 1][:, 0:T], ACT.Sigmoid).then_inc(S["glu_sig"], 1)
                ac.wait_ge(S["z_ready"], l + 1)
                ac.wait_ge(S["shift_out"], 16 * (l + 1))
                fn(z[0:64, 12, :], z[0:64, 12, :], ACT.Tanh)
                fn(z[:, 13, :], z[:, 13, :], ACT.Sigmoid).then_inc(S["lora_in"], 1)
                for i in range(3):
                    for f in range(CB):
                        k = 4 * i + f
                        ac.wait_ge(S["lora_ps"], 3 * CB * l + k + 1)
                        src = pools[4 + k % 4][:, 0:T]
                        if i < 2:
                            c0 = PV["w0" if i == 0 else "a0"][0]
                            ins = fn(tmp[1 + i][:, f, :], src, ACT.Sigmoid, bias=pv[:, l, c0 + f:c0 + f + 1])
                        else:
                            ins = fn(gg[:, f, :], src, ACT.Identity)
                        ins.then_inc(S["lora_out"], 1)
                ac.wait_ge(S["kk_ps"], l + 1)
                for f in range(CB):
                    ins = fn(tmp[0][:, f, :], pools[4 + f][:, 0:T], ACT.Sqrt)
                ins.then_inc(S["kk_norm"], 1)
                ac.wait_ge(S["cum_ready"], l + 1)
                fn(kr[:, :, 1, :], tmp[3], ACT.Exp)
                fn(kr[:, :, 0, :], tmp[4], ACT.Exp)
                fn(beta, tmp[3], ACT.Exp, scale=-1.0)
                fn(beta_e, chi_e, ACT.Exp).then_inc(S["exps_ready"], 1)
                for m in range(3):
                    t0, nt, chunks = TILES[m]
                    for f in range(CB):
                        n_u = NU * l + CB * m + f
                        ac.wait_ge(S["tr_ps"], n_u + 1)
                        ps = pools[0][0:nt, :].rearrange("p (i a k) -> p i a k", i=4, a=2)
                        fn(xk[0:nt, :, 0:N], ps[:, 0], ACT.Identity)
                        fn(v_tok[0:nt], ps[:, 1], ACT.Identity)
                        fn(be_tok[0:nt], ps[:, 2], ACT.Identity)
                        fn(ch_tok[0:nt], ps[:, 3], ACT.Identity).then_inc(S["tr_out"], 1)
                        ac.wait_ge(S["sq_ps"], n_u + 1)
                        sqv = pools[1][0:nt, :].rearrange("p (i t) -> p i t", i=4)
                        fn(a2[0:nt, :, 0:nt], sqv[:, 0:2, 0:nt], ACT.Identity)
                        fn(p2[0:nt, :, 0:nt], sqv[:, 2:4, 0:nt], ACT.Identity)
                        fn(xk[0:nt, :, N:P], pools[2][0:nt, 0:P].rearrange("p (a k) -> p a k", a=2), ACT.Identity)\
                            .then_inc(S["sq_out"], 1)
                        ac.wait_ge(S["quad_ps"], n_u + 1)
                        qv = pools[3][0:nt, :].rearrange("p (i t) -> p i t", i=4)
                        fn(am[0:nt, :, 0:nt], qv[:, 0:2, 0:nt], ACT.Identity)
                        fn(pm[0:nt, :, 0:nt], qv[:, 2:4, 0:nt], ACT.Identity).then_inc(S["act_quad"], 1)
                        ac.wait_ge(S["oct_ps"], n_u + 1)
                        fn(a2[0:nt, :, 0:nt], pools[5][0:nt, 0:2 * P].rearrange("p (a t) -> p a t", a=2)[:, :, 0:nt],
                           ACT.Identity).then_inc(S["act_oct"], 1)
                        ac.wait_ge(S["y_ps"], n_u + 1)
                        fn(yk[0:nt], pools[2][0:nt, 0:2 * P].rearrange("p (a t) -> p a t", a=2), ACT.Identity)\
                            .then_inc(S["y_out"], 1)
                        ac.wait_ge(S["off_ps"], n_u + 1)
                        fn(zk[0:nt], pools[3][0:nt, 0:2 * P].rearrange("p (a t) -> p a t", a=2), ACT.Identity)\
                            .then_inc(S["off_out"], 1)
                        ac.wait_ge(S["gh_ps"], n_u + 1)
                        w = min(8, len(chunks))
                        ins = fn(hst[:, f, 0:w, :], pools[6][:, 0:w * N].rearrange("p (c v) -> p c v", c=w), ACT.Identity)
                        if len(chunks) > 8:
                            ins = fn(hst[:, f, 8, :], pools[2][:, 0:N], ACT.Identity)
                        ins.then_inc(S["h_out"], 1)
                        ac.wait_ge(S["ro_ps"], n_u + 1)
                        fn(ov[:, f, 0:nt], pools[7][:, 0:nt], ACT.Identity).then_inc(S["ov_out"], 1)
                ac.wait_ge(S["o_cent"], l + 1)
                fn(tmp[1], o_t, ACT.Square).then_inc(S["o_sq"], 1)
                ac.wait_ge(S["o_var_ps"], l + 1)
                for f in range(CB):
                    ins = fn(tmp[0][:, f, :], pools[4 + f][:, 0:T], ACT.Sqrt, scale=1.0 / N, bias=eps[:, 1:2])
                ins.then_inc(S["o_std"], 1)

            def ffn():
                norm(1)
                for n in range(CF):
                    ac.wait_ge(S["up_ps"], n + 1)
                    if n >= 2:
                        ac.wait_ge(S["up_out"], n - 1)
                    fn(silu_s[:, n % 2, :], pools[2 * (n % 2)][:, 0:T], ACT.Silu).then_inc(S["up_silu"], 1)

            def routing():
                norm(3)
                for m, (t0, nt, _) in enumerate(TILES):
                    for half in range(2):
                        n = 2 * m + half
                        ac.wait_ge(S["ht_ps"], n + 1)
                        fn(h_tok[0:nt, m, 512 * half:512 * half + 512], pools[4 + n % 4][0:nt, :], ACT.Identity)\
                            .then_inc(S["ht_out"], 1)
                ac.wait_ge(S["gates_in"], 1)
                fn(route[:, 6, :, 0:2], route[:, 5, :, 0:2], ACT.Sigmoid).then_inc(S["gates_out"], 1)

            def gather_out(k, half_):
                ac.wait_ge(S["ga_ps"], k * 2 + (half_ + 1))
                fn(he_hi[:, 4 * half_:4 * half_ + 4, :], pools[7 - half_][:].rearrange("p (c s) -> p c s", c=4),
                   ACT.Identity).then_inc(S["ga_hi"], 1)

            def weights_to_rows(k):
                ac.wait_ge(S["mw_ps"], k + 1)
                fn(mix_w, pools[6][:, 0:T], ACT.Identity).then_inc(S["mw_out"], 1)

            def y_out():
                fn(y_e[:, 0:512], pools[4][:], ACT.Identity)
                fn(y_e[:, 512:1024], pools[5][:], ACT.Identity).then_inc(S["ey_out"], 1)

            def expert(i, k):
                def high(n):
                    ac.wait_ge(slot_in[n % RING], (i * (S_EXPERT // RING) + (S_DENSE // RING + n // RING + 1)) * 16)
                    ac.wait_ge(S["slot_done"], i * S_EXPERT + (n + 1))
                    fn(w_hi[n % SPLIT], slot(n), ACT.Identity).then_inc(S["hi_ready"], 1)

                for n in range(S_EXPERT):
                    if n == 2:
                        y_out()
                        weights_to_rows(k)
                    g = UP_DONE_BY.get(n)
                    if g is not None:
                        silu_out(i, g)
                    high(n)
                    g = TURNED_BY.get(n)
                    if g is not None:
                        turned_out(i, g)
                turned_out(i, NG - 1)
                gather_out(k + 1, 0)
                gather_out(k + 1, 1)
                ac.wait_ge(S["slot_done"], i * S_EXPERT + (SPLIT + S_EXPERT))

            def silu_out(i, g):
                ac.wait_ge(S["slot_done"], i * S_EXPERT + (SPLIT + SLOT_OF["w3", g] + 1))
                fn(sil_e[:, g % 2, :], pools[g % 2][:, 0:FW], ACT.Silu).then_inc(S["eup_silu"], 1)

            def turned_out(i, g):
                ac.wait_ge(S["et_ps"], i * NG + (g + 1))
                fn(at_hi[:, g % 2, :], pools[2 + g % 2][:, 0:2 * P], ACT.Identity).then_inc(S["et_hi"], 1)

            def one_pass(i0, k0):
                gather_out(k0, 0)
                gather_out(k0, 1)
                with ac.Fori(0, E) as e:
                    expert(e + i0, e + k0)
                y_out()
                weights_to_rows(k0 + E)

            def experts():
                for _ in range(SPLIT):
                    nc.scalar.nop().then_inc(S["slot_done"], 1)
                ac.wait_ge(S["count_out"], 1)
                one_pass(0, 0)
                ac.wait_ge(S["n_ready"], 1)
                npass = ac.value_load(n_int[0:1, 0:1], min_val=1, max_val=3)
                with ac.If(npass > 1):
                    with ac.Fori(1, npass) as p:
                        one_pass(p * E, p * (E + 1))

            ac.wait_ge(S["first_in"], N_FIRST)
            norm(0)
            fn(small[:, 2, :], lam[:, 2, :], ACT.Exp).then_inc(S["disc_exp1"], 1)
            ac.wait_ge(S["disc_ang"], 1)
            fn(small[:, 3, :], small[:, 4, :], ACT.Exp)
            fn(small[:, 5:7, :], small[:, 7:9, :], ACT.Sin).then_inc(S["disc_exp2"], 1)
            mix(0)
            ffn()
            mix(1)
            routing()
            experts()
            norm(4)

        @block.vector
        def _(dve):
            steps = [0]
            v = nc.vector

            def step(ins):
                steps[0] += 1
                ins.then_inc(S["dve_step"], 1)
                dve.wait_ge(S["dve_step"], steps[0])

            def col(l, name, i):
                c0 = PV[name][0]
                return pv[:, l, c0 + i:c0 + i + 1]

            def norm(i, gains, out):
                dve.wait_ge(S["norm_rt"], i + 1)
                step(v.reciprocal(rstd[:, 1, :], rstd[:, 0, :]))
                for c in range(DC):
                    ins = v.scalar_tensor_tensor(out=out[:, c, :], in0=x[:, c, :], scalar=gains[:, c:c + 1],
                                                 in1=rstd[:, 1, :], op0=ALU.mult, op1=ALU.mult)
                ins.then_inc(S["h_ready"], 1)

            def discretise():
                s = lambda i: small[:, i, :]
                lr, li = lam[:, 0, :], lam[:, 1, :]
                tt, ts = v.tensor_tensor, v.tensor_scalar
                dve.wait_ge(S["disc_exp1"], 1)
                step(tt(s(4), lr, s(2), ALU.mult))
                step(tt(s(9), li, s(2), ALU.mult))
                step(ts(s(10), s(9), 1 / TWO_PI, ROUND, ALU.mult, ALU.add))
                step(ts(s(10), s(10), ROUND, None, ALU.subtract))
                for c in (C1, C2, C3):
                    step(v.scalar_tensor_tensor(out=s(9), in0=s(10), scalar=-c, in1=s(9), op0=ALU.mult, op1=ALU.add))
                step(ts(s(7), s(9), -PI_IN, PI_IN, ALU.max, ALU.min))
                step(ts(s(10), s(9), math.pi / 2, None, ALU.add))
                step(ts(s(11), s(10), math.pi, -TWO_PI, ALU.is_gt, ALU.mult))
                step(tt(s(10), s(10), s(11), ALU.add))
                ts(s(8), s(10), -PI_IN, PI_IN, ALU.max, ALU.min).then_inc(S["disc_ang"], 1)
                dve.wait_ge(S["disc_exp2"], 1)
                ar_, ai_, na = apow[:, 0, 0, :], apow[:, 0, 1, :], apow[:, 0, 2, :]
                step(tt(ar_, s(3), s(6), ALU.mult))
                step(tt(ai_, s(3), s(5), ALU.mult))
                step(tt(s(12), lr, lr, ALU.mult))
                step(tt(s(13), li, li, ALU.mult))
                step(tt(s(12), s(12), s(13), ALU.add))
                step(v.reciprocal(s(12), s(12)))
                step(ts(s(13), ar_, 1.0, None, ALU.subtract))
                step(tt(s(14), s(13), lr, ALU.mult))
                step(tt(s(15), ai_, li, ALU.mult))
                step(tt(s(14), s(14), s(15), ALU.add))
                step(tt(qq[:, 0, :], s(14), s(12), ALU.mult))
                step(tt(s(14), ai_, lr, ALU.mult))
                step(tt(s(15), s(13), li, ALU.mult))
                step(tt(s(14), s(14), s(15), ALU.subtract))
                step(tt(qq[:, 1, :], s(14), s(12), ALU.mult))
                step(ts(qq[:, 2, :], qq[:, 1, :], -1.0, None, ALU.mult))
                step(ts(na, ai_, -1.0, None, ALU.mult))
                for k in range(1, LEVELS):
                    br, bi, bn = (apow[:, k - 1, i, :] for i in range(3))
                    step(tt(s(14), br, br, ALU.mult))
                    step(tt(s(15), bi, bi, ALU.mult))
                    step(tt(apow[:, k, 0, :], s(14), s(15), ALU.subtract))
                    step(tt(s(14), br, bi, ALU.mult))
                    step(ts(apow[:, k, 1, :], s(14), 2.0, None, ALU.mult))
                    step(ts(apow[:, k, 2, :], s(14), -2.0, None, ALU.mult))
                dve.wait_ge(S["consts"], N_CONST)
                for l in range(DEPTH):
                    def ab(i):
                        return apow[:, 0, i, JT * l:JT * (l + 1)].unsqueeze(2).broadcast_to([P, JT, NS])
                    tt(axt[:, 0], x0[:, l, 1], ab(2), ALU.mult)
                    step(tt(axt[:, 1], x0[:, l, 0], ab(1), ALU.mult))
                    for c in range(2):
                        step(tt(x0[:, l, c], x0[:, l, c], ab(0), ALU.mult))
                    step(tt(x0[:, l], x0[:, l], axt[:], ALU.add))
                v.nop().then_inc(S["disc_done"], 1)

            def scan_pair(l, j0):
                stt = v.scalar_tensor_tensor
                X = [s5x[:, (j0 + i) % 4] for i in range(2)]
                for i in range(2):
                    k_ = JT * l + j0 + i
                    dve.wait_ge(S["bu_q"], k_ + 1)
                    stt(out=X[i][:, 0, :], in0=pools[4 + 2 * i + 1][:, 0:T], scalar=qq[:, 2, k_:k_ + 1],
                        in1=X[i][:, 0, :], op0=ALU.mult, op1=ALU.add)
                    stt(out=X[i][:, 1, :], in0=pools[4 + 2 * i][:, 0:T], scalar=qq[:, 1, k_:k_ + 1],
                        in1=X[i][:, 1, :], op0=ALU.mult, op1=ALU.add).then_inc(S["bu_used"], 1)
                dve.wait_ge(S["bu_used"], JT * l + j0 + 2)
                for i in range(2):
                    v.tensor_tensor(X[i][:, :, TP:T], X[i][:, :, TP:T], x0[:, l, :, j0 + i, :], ALU.add)
                levels = []
                for k in range(LEVELS):
                    d = 1 << k
                    if 2 * d <= TP:
                        levels.append((k, d - 1, 2 * d - 1, TP // (2 * d)))
                for k in reversed(range(LEVELS)):
                    d = 1 << k
                    n = (TP - 3 * d) // (2 * d) + 1 if TP >= 3 * d else 0
                    if n:
                        levels.append((k, 2 * d - 1, 3 * d - 1, n))
                done = [0, 0]
                for k, src, dst, n in levels:
                    w = 2 << k
                    end = lambda at: at + w * (n - 1) + 1
                    for i in range(2):
                        if done[i]:
                            dve.wait_ge(S["dve_step"], done[i])
                        k_ = JT * l + j0 + i
                        stt(out=X[i][:, :, dst:end(dst):w], in0=X[i][:, :, src:end(src):w], scalar=apow[:, k, 0, k_:k_ + 1],
                            in1=X[i][:, :, dst:end(dst):w], op0=ALU.mult, op1=ALU.add).then_inc(S["dve_step"], 1)
                        steps[0] += 1
                        done[i] = steps[0]
                    for i in range(2):
                        k_ = JT * l + j0 + i
                        dve.wait_ge(S["dve_step"], done[i])
                        for c in range(2):
                            ins = stt(out=X[i][:, c, dst:end(dst):w], in0=X[i][:, 1 - c, src:end(src):w],
                                      scalar=apow[:, k, 2 - c, k_:k_ + 1], in1=X[i][:, c, dst:end(dst):w],
                                      op0=ALU.mult, op1=ALU.add)
                        ins.then_inc(S["dve_step"], 1)
                        steps[0] += 1
                        done[i] = steps[0]
                dve.wait_ge(S["dve_step"], steps[0])
                if l and j0 == 0:
                    dve.wait_ge(S["s5_out"], 16 * l)
                for i in range(2):
                    v.tensor_copy(s5out[:, j0 + i], X[i][:, :, TP - 1:T]).then_inc(S["scan_done"], 1)

            def y5_add(l, aa):
                dve.wait_ge(S["y5_ps"], JT * l + 4 * aa + 4)
                v.scalar_tensor_tensor(out=y5[:, aa, :], in0=u[:, aa, :], scalar=col(l, "d", aa),
                                       in1=pools[3][:, 0:T], op0=ALU.mult, op1=ALU.add).then_inc(S["y5_mix"], 1)

            def mix(l):
                tt, ts, stt = v.tensor_tensor, v.tensor_scalar, v.scalar_tensor_tensor
                if l:
                    norm(2 * l, pv[:, l, PV["norm_mix"][0]:PV["norm_mix"][0] + DC], h)
                v.memset(prow[:, :, 0:1], 0.0).then_inc(S["pad_zero"], 1)
                dve.wait_ge(S["small_w"], 48 * (l + 1))
                step(ts(s5_c[:, :, 1, :], s5_c[:, :, 1, :], -1.0, None, ALU.mult))
                for j in range(0, JT, 2):
                    scan_pair(l, j)
                    if j >= 6 and j % 4 == 2:
                        y5_add(l, j // 4 - 1)
                y5_add(l, CA - 1)
                dve.wait_ge(S["proj_out"], CIN * l + CA + CR)
                dve.wait_ge(S["pad_zero"], l + 1)
                tt(z[:, :, 0:TP], prow[:, :, 0:TP], prow[:, :, 1:TP + 1], ALU.subtract)
                step(tt(z[:, :, TP:T], shift0[:, l], prow[:, :, TP + 1:T + 1], ALU.subtract))
                for c in range(CR):
                    ins = stt(out=z[:, c, :], in0=z[:, c, :], scalar=col(l, "mu", c), in1=prow[:, c, 1:T + 1],
                              op0=ALU.mult, op1=ALU.add)
                ins.then_inc(S["z_ready"], 1)
                for n in range(DC):
                    dve.wait_ge(S["glu_sig"], DC * l + n + 1)
                    step(tt(gate[:, n, :], gate[:, n, :], glu_s[:, n % 2, :], ALU.mult))
                    tt(gate[:, n, :], gate[:, n, :], pools[2 * (n % 2)][:, 0:T], ALU.mult).then_inc(S["glu_out"], 1)
                dve.wait_ge(S["z_ready"], l + 1)
                dve.wait_ge(S["shift_out"], 16 * (l + 1))
                kk = chi
                for f in range(CB):
                    ins = ts(kk[:, f, :], z[:, 4 + f, :], col(l, "k_k", f), None, ALU.mult)
                step(ins)
                tt(tmp[0], kk, kk, ALU.mult).then_inc(S["kk_sq"], 1)
                dve.wait_ge(S["lora_out"], 3 * CB * (l + 1))
                step(ts(tmp[1], tmp[1], -math.exp(-0.5), None, ALU.mult))
                flat = "p a t -> p (a t)"
                for f in range(CB):
                    ins = v.tensor_tensor_scan(tmp[3][:, f, :], keep[:], tmp[1][:, f, :], 0.0, ALU.mult, ALU.add)
                step(ins)
                tt(tmp[4], tmp[3], tmp[1], ALU.subtract)
                full = TP // CH
                cv = tmp[3][:, :, 0:full * CH].rearrange("p a (c t) -> p a c t", t=CH)
                for f in range(CB):
                    tt(chi_e[:, f, 0:full * CH].rearrange("p (c t) -> p c t", t=CH),
                       cv[:, f, :, CH - 1:CH].broadcast_to([P, full, CH]), cv[:, f], ALU.subtract)
                tt(chi_e[:, :, full * CH:TP], tmp[3][:, :, TP - 1:TP].broadcast_to([P, CB, TP - full * CH]),
                   tmp[3][:, :, full * CH:TP], ALU.subtract)
                v.memset(chi_e[:, :, TP:T], 0.0).then_inc(S["cum_ready"], 1)
                dve.wait_ge(S["kk_norm"], l + 1)
                step(ts(tmp[0], tmp[0], 1e-12, None, ALU.max))
                step(v.reciprocal(tmp[0], tmp[0]))
                step(tt(kk, kk, tmp[0], ALU.mult))
                kp = z[:, 4:8, :]
                for f in range(CB):
                    ins = ts(tmp[0][:, f, :], tmp[2][:, f, :], 1.0, col(l, "k_a", f), ALU.subtract, ALU.mult)
                step(ins)
                step(stt(out=kp.rearrange(flat), in0=tmp[0].rearrange(flat), scalar=1.0, in1=kp.rearrange(flat),
                         op0=ALU.add, op1=ALU.mult))
                for f in range(CB):
                    ins = stt(out=bonus[:, f, :], in0=z[:, f, :], scalar=col(l, "r_k", f), in1=kp[:, f, :],
                              op0=ALU.mult, op1=ALU.mult)
                ins.then_inc(S["bonus_in"], 1)
                step(tt(tmp[2], tmp[2], kk, ALU.mult))
                dve.wait_ge(S["exps_ready"], l + 1)
                for f in range(CB):
                    v.tensor_copy(wend[:, f, 0:full], kr[:, f, 1, CH - 1:full * CH:CH])
                v.tensor_copy(wend[:, :, full:full + 1 + NS], kr[:, :, 1, TP - 1:T])
                step(tt(kr[:, :, 0, :], kr[:, :, 0, :], kk, ALU.mult))
                step(tt(kr[:, :, 1, :], kr[:, :, 1, :], z[:, 0:4, :], ALU.mult))
                tt(chi, beta, kp, ALU.mult)
                step(tt(chi_e, beta_e, kp, ALU.mult))
                tt(beta, beta, tmp[2], ALU.mult)
                tt(beta_e, beta_e, tmp[2], ALU.mult)
                v.memset(zcar, 0.0).then_inc(S["z_out"], 1)
                dve.wait_ge(S["bonus_ps"], l + 1)
                for f in range(CB):
                    ins = tt(bonus[:, f, :], z[:, 8 + f, :], pools[4 + f][:, 0:T], ALU.mult)
                ins.then_inc(S["fm_ready"], 1)
                dve.wait_ge(S["fm_ready"], l + 1)
                for m in range(3):
                    for f in range(CB):
                        unit(l, m, f)
                    chain(l, m)
                dve.wait_ge(S["o_mean_ps"], l + 1)
                for f in range(CB):
                    ins = stt(out=o_t[:, f, :], in0=pools[f][:, 0:T], scalar=-1.0 / N, in1=o_t[:, f, :],
                              op0=ALU.mult, op1=ALU.add)
                ins.then_inc(S["o_cent"], 1)
                dve.wait_ge(S["o_std"], l + 1)
                dve.wait_ge(S["o_cent"], l + 1)
                step(v.reciprocal(tmp[0], tmp[0]))
                step(tt(o_t, o_t, tmp[0], ALU.mult))
                for f in range(CB):
                    ins = ts(o_t[:, f, :], o_t[:, f, :], col(l, "gn_g", f), col(l, "gn_b", f), ALU.mult, ALU.add)
                step(ins)
                step(tt(o_t, o_t, bonus, ALU.add))
                tt(o_t, o_t, gg, ALU.mult).then_inc(S["o_ready"], 1)
                for n in range(DC):
                    dve.wait_ge(S["bo_ps"], DC * l + n + 1)
                    step(tt(gate[:, DC + n, :], gate[:, DC + n, :], pools[n % 4][:, 0:T], ALU.mult))
                    tt(gate[:, n, :], gate[:, n, :], gate[:, DC + n, :], ALU.add).then_inc(S["bo_out"], 1)
                for n in range(DC):
                    dve.wait_ge(S["wo_ps"], DC * l + n + 1)
                    tt(x[:, n, :], x[:, n, :], pools[4 + n % 4][:, 0:T], ALU.add).then_inc(S["wo_out"], 1)
                dve.wait_ge(S["wo_out"], DC * (l + 1))
                v.nop().then_inc(S["x_ready"], 1)

            def unit(l, m, f):
                tt, ts, stt = v.tensor_tensor, v.tensor_scalar, v.scalar_tensor_tensor
                t0, nt, chunks = TILES[m]
                ncn = len(chunks)
                n_u = NU * l + CB * m + f
                mk = masks[:] if m < 2 else masks_s[:]
                sc = sel_c[:] if m < 2 else sel_s[:]
                dve.wait_ge(S["gram_ps"], n_u + 1)
                for par in range(2):
                    tt(am[0:nt, par, 0:nt], pools[1 + par][0:nt, 0:nt], mk[:, 0], ALU.mult)
                    g3 = pools[3 + par][0:nt, 0:2 * nt].rearrange("p (c t) -> p c t", c=2)
                    g5 = pools[5 + par][0:nt, 0:2 * nt].rearrange("p (c t) -> p c t", c=2)
                    tt(pm[0:nt, par, 0:nt], g3[:, 0], mk[:, 1], ALU.mult)
                    tt(poff[0:nt, par, 0:nt], g3[:, 0], mk[:, 2], ALU.mult)
                    tt(mbt[0:nt, par, 0:nt], g3[:, 1], mk[:, 4], ALU.mult)
                    tt(akt[0:nt, par, 0:nt], g5[:, 0], mk[:, 3], ALU.mult)
                    ins = tt(mkt[0:nt, par, 0:nt], g5[:, 1], mk[:, 4], ALU.mult)
                ins.then_inc(S["gram_out"], 1)
                dve.wait_ge(S["gram_out"], n_u + 1)
                for par in range(2):
                    ins = tt(e1[0:nt, par, 0:nt], ident[0:nt, 0:nt], pm[0:nt, par, 0:nt], ALU.subtract)
                ins.then_inc(S["e1_out"], 1)
                dve.wait_ge(S["tr_out"], n_u + 1)

                def chunked(out, src, sign):
                    for par in range(2):
                        tt(out[0:nt, par, 0:ncn, :], src[0:nt, par, :].unsqueeze(1).broadcast_to([nt, ncn, N]),
                           sc[:, sign].unsqueeze(2).broadcast_to([nt, ncn, N]), ALU.mult)

                chunked(v_bd, v_tok, 0)
                chunked(be_bd, be_tok, 0)
                dve.wait_ge(S["quad_ps"], n_u + 1)
                dve.wait_ge(S["act_quad"], n_u + 1)
                tt(e2[0:nt, :, 0:nt], e1[0:nt, :, 0:nt],
                   pools[4][0:nt, 0:2 * P].rearrange("p (a t) -> p a t", a=2)[:, :, 0:nt], ALU.add).then_inc(S["quad_out"], 1)
                dve.wait_ge(S["quad_out"], n_u + 1)
                dve.wait_ge(S["oct_ps"], n_u + 1)
                dve.wait_ge(S["act_oct"], n_u + 1)
                tt(e1[0:nt, :, 0:nt], e2[0:nt, :, 0:nt],
                   pools[6][0:nt, 0:2 * P].rearrange("p (a t) -> p a t", a=2)[:, :, 0:nt], ALU.add).then_inc(S["oct_out"], 1)
                dve.wait_ge(S["oct_out"], n_u + 1)
                dve.wait_ge(S["e8_ps"], n_u + 1)
                tt(e2[0:nt, :, 0:nt], e1[0:nt, :, 0:nt],
                   pools[1][0:nt, 0:2 * P].rearrange("p (a t) -> p a t", a=2)[:, :, 0:nt], ALU.add).then_inc(S["e8_out"], 1)
                dve.wait_ge(S["fix_ps"], n_u + 1)
                dve.wait_ge(S["y_out"], n_u + 1)
                step(tt(xk[0:nt], yk[0:nt], pools[4][0:nt, 0:2 * P].rearrange("p (a t) -> p a t", a=2), ALU.subtract))
                chunked(nx_bd, xk[:, :, N:P], 1)
                ts(zk[0:nt, :, 0:N], xk[0:nt, :, N:P], -1.0, None, ALU.mult).then_inc(S["x_out"], 1)
                dve.wait_ge(S["gh_ps"], n_u + 1)
                w0 = 4 * m
                for par in range(2):
                    q = slice(64 * par, 64 * par + 64)
                    ins = tt(gpre[q, f, 0:ncn, :], ident[q, q].unsqueeze(1).broadcast_to([64, ncn, N]),
                             wend[q, f, w0:w0 + ncn].unsqueeze(2).broadcast_to([64, ncn, N]), ALU.mult)
                step(ins)
                w = min(8, ncn)
                ins = tt(gpre[:, f, 0:w, :], gpre[:, f, 0:w, :],
                         pools[5][:, 0:w * N].rearrange("p (c v) -> p c v", c=w), ALU.subtract)
                if ncn > 8:
                    ins = tt(gpre[:, f, 8, :], gpre[:, f, 8, :], pools[1][:, 0:N], ALU.subtract)
                ins.then_inc(S["gh_out"], 1)
                dve.wait_ge(S["ro_ps"], n_u + 1)
                tt(rt[:, f, 0:nt], kr[:, f, 1, t0:t0 + nt], pools[3][:, 0:nt], ALU.subtract).then_inc(S["ro_out"], 1)

            def chain(l, m):
                tt = v.tensor_tensor
                t0, nt, chunks = TILES[m]
                dve.wait_ge(S["h_out"], NU * l + CB * (m + 1))
                dve.wait_ge(S["ov_out"], NU * l + CB * (m + 1))
                seq = 4 if m < 2 else 1
                for c in range(seq):
                    n_c = 9 * l + 4 * m + c
                    dve.wait_ge(S["z_ps"], n_c + 1)
                    for par in range(2):
                        q = slice(64 * par, 64 * par + 64)
                        ins = tt(hst[q, :, c, :], hst[q, :, c, :],
                                 pools[par][q, 0:CB * N].rearrange("p (f v) -> p f v", f=CB), ALU.add)
                    ins.then_inc(S["z_out"], 1)
                if m == 2:
                    for n in range(H):
                        f, par = n // 2, n % 2
                        q = slice(64 * par, 64 * par + 64)
                        dve.wait_ge(S["zs_ps"], H * l + n + 1)
                        tt(hst[q, f, 1:9, :], hst[q, f, 1:9, :],
                           pools[2 + par][q, :].rearrange("p (b v) -> p b v", b=NS), ALU.add).then_inc(S["zs_out"], 1)
                for n in range(H):
                    f, par = n // 2, n % 2
                    q = slice(64 * par, 64 * par + 64)
                    k = H * (3 * l + m) + n
                    dve.wait_ge(S["o_ps"], k + 1)
                    tt(o_t[q, f, t0:t0 + nt], ov[q, f, 0:nt], pools[4 + par][q, 0:nt], ALU.add).then_inc(S["o_out"], 1)
                if m < 2:
                    dve.wait_ge(S["z_out"], 9 * l + 4 * (m + 1) + l + 1)
                    v.tensor_copy(zcar, hst[:, :, 3, :]).then_inc(S["zcar_out"], 1)

            def ffn():
                dve.wait_ge(S["rw_out"], 16)
                norm(1, pv[:, 0, PV["norm_ffn"][0]:PV["norm_ffn"][0] + DC], h)
                for n in range(CF):
                    dve.wait_ge(S["up_silu"], n + 1)
                    v.tensor_tensor(act[:, n, :], silu_s[:, n % 2, :], pools[2 * (n % 2) + 1][:, 0:T], ALU.mult)\
                        .then_inc(S["up_out"], 1)
                for n in range(DC):
                    dve.wait_ge(S["down_ps"], n + 1)
                    v.tensor_tensor(x[:, n, :], x[:, n, :], pools[4 + n % 4][:, 0:T], ALU.add).then_inc(S["down_out"], 1)
                dve.wait_ge(S["down_out"], DC)
                v.nop().then_inc(S["x_ready"], 1)

            def routing():
                tt, ts, stt = v.tensor_tensor, v.tensor_scalar, v.scalar_tensor_tensor
                step(v.memset(route, 0.0))
                dve.wait_ge(S["rw_out"], 32)
                norm(3, pv[:, 1, PV["norm_ffn"][0]:PV["norm_ffn"][0] + DC], h)
                dve.wait_ge(S["logit_ps"], 1)
                for m, (t0, nt, _) in enumerate(TILES):
                    step(v.tensor_copy(route[0:nt, 2, m, :], pools[1][0:nt, m * E:(m + 1) * E]))
                for m in range(3):
                    step(v.max(route[:, 3, m, :], route[:, 2, m, :]))
                    step(v.max_index(top_i[:, m, :], route[:, 3, m, :], route[:, 2, m, :]))
                step(v.tensor_copy(route[:, 4], top_i[:]))
                step(tt(route[:, 5, :, 0:1], route[:, 3, :, 0:1], route[:, 3, :, 1:2], ALU.subtract))
                tt(route[:, 5, :, 1:2], route[:, 3, :, 1:2], route[:, 3, :, 0:1], ALU.subtract).then_inc(S["gates_in"], 1)
                for m in range(3):
                    for i in range(2):
                        step(ts(route[:, 7 + i, m, :], iota[:, 0:E], route[:, 4, m, i:i + 1], None, ALU.is_equal))
                dve.wait_ge(S["gates_out"], 1)
                step(v.memset(ar(18124, 90), 0.0))
                for m, (t0, nt, _) in enumerate(TILES):
                    step(tt(chosen[0:nt, m, 1:E + 1], route[0:nt, 7, m, :], route[0:nt, 8, m, :], ALU.add))
                    for i in range(2):
                        step(ts(route[:, 7 + i, m, :], route[:, 7 + i, m, :], route[:, 6, m, i:i + 1], None, ALU.mult))
                    step(tt(weight[0:nt, m, 1:E + 1], route[0:nt, 7, m, :], route[0:nt, 8, m, :], ALU.add))
                v.nop().then_inc(S["count_in"], 1)
                dve.wait_ge(S["count_ps"], 1)
                for m, (t0, nt, _) in enumerate(TILES):
                    step(v.tensor_copy(place[0:nt, m, 1:E + 1], pools[2][0:nt, m * E:(m + 1) * E]))
                step(v.tensor_reduce(route[:, 11, 0, 0:1], pools[2][:, 3 * E:4 * E], AX.X, ALU.max))
                step(ts(route[:, 11, 0, 1:2], route[:, 11, 0, 0:1], CAP + 0.5, 1.0, ALU.is_gt, ALU.add))
                step(ts(route[:, 11, 0, 2:3], route[:, 11, 0, 0:1], 2 * CAP + 0.5, None, ALU.is_gt))
                step(tt(route[:, 11, 0, 1:2], route[:, 11, 0, 1:2], route[:, 11, 0, 2:3], ALU.add))
                v.tensor_copy(n_int[:], route[:, 11, 0, 1:2]).then_inc(S["n_ready"], 1)
                step(v.memset(y_e, 0.0))
                v.nop().then_inc(S["count_out"], 1)

            def select(e, table, out):
                for m, (t0, nt, _) in enumerate(TILES):
                    ins = v.tensor_scalar(out[0:nt, m, :], iota[0:nt], place[0:nt, m, bass.ds(e, 1)],
                                          table[0:nt, m, bass.ds(e, 1)], ALU.is_equal, ALU.mult)
                return ins

            def gather_out(k, half_):
                dve.wait_ge(S["ga_hi"], k * 2 + (half_ + 1))
                q = slice(4 * half_, 4 * half_ + 4)
                v.tensor_tensor(he_lo[:, q, :], pools[7 - half_][:].rearrange("p (c s) -> p c s", c=4),
                                he_hi[:, q, :].bitcast(F32), ALU.subtract).then_inc(S["ga_lo"], 1)

            def act_out(i, g):
                dve.wait_ge(S["eup_silu"], i * NG + (g + 1))
                v.tensor_tensor(act_e[:, g % 2, :], sil_e[:, g % 2, :], pools[g % 2][:, FW:2 * FW], ALU.mult)\
                    .then_inc(S["eup_act"], 1)

            def turned_out(i, g):
                dve.wait_ge(S["et_hi"], i * NG + (g + 1))
                v.tensor_tensor(at_lo[:, g % 2, :], pools[2 + g % 2][:, 0:2 * P], at_hi[:, g % 2, :].bitcast(F32),
                                ALU.subtract).then_inc(S["et_lo"], 1)

            def combine_out(k):
                for c in range(DC):
                    dve.wait_ge(S["em_ps"], k * DC + (c + 1))
                    v.tensor_tensor(x[:, c, :], x[:, c, :], pools[6 + c % 2][:, 0:T], ALU.add).then_inc(S["em_out"], 1)

            def expert(e, i, k):
                def low(n):
                    dve.wait_ge(S["hi_ready"], i * S_EXPERT + (n + 1))
                    v.tensor_tensor(w_lo[n % SPLIT], slot(n), w_hi[n % SPLIT].bitcast(F32), ALU.subtract)\
                        .then_inc(S["weights_used"], 1)

                for n in range(S_EXPERT):
                    if n == 1:
                        select(e, weight, sel_w).then_inc(S["selw_ready"], 1)
                    if n == 3:
                        combine_out(k)
                    g = UP_DONE_BY.get(n)
                    if g is not None:
                        act_out(i, g)
                    low(n)
                    g = TURNED_BY.get(n)
                    if g is not None:
                        turned_out(i, g)
                    if n == S_EXPERT - 8:
                        select(e + 2, chosen, sel_p).then_inc(S["selp_ready"], 1)
                turned_out(i, NG - 1)
                gather_out(k + 1, 0)
                gather_out(k + 1, 1)

            def one_pass(p, i0, k0):
                select(1, chosen, sel_p).then_inc(S["selp_ready"], 1)
                gather_out(k0, 0)
                gather_out(k0, 1)
                with dve.Fori(0, E) as e:
                    expert(e, e + i0, e + k0)
                select(E, weight, sel_w).then_inc(S["selw_ready"], 1)
                combine_out(k0 + E)

            def experts():
                one_pass(0, 0, 0)
                npass = dve.value_load(n_int[0:1, 0:1], min_val=1, max_val=3)
                with dve.If(npass > 1):
                    with dve.Fori(1, npass) as p:
                        v.tensor_scalar(place, place, float(CAP), None, ALU.subtract).then_inc(S["place_moved"], 1)
                        dve.wait_ge(S["place_moved"], p)
                        one_pass(p, p * E, p * (E + 1))
                dve.wait_ge(S["em_out"], npass * (DC * (E + 1)))
                v.nop().then_inc(S["x_ready"], 1)

            dve.wait_ge(S["first_in"], N_FIRST)
            norm(0, pv[:, 0, PV["norm_mix"][0]:PV["norm_mix"][0] + DC], h)
            discretise()
            mix(0)
            ffn()
            mix(1)
            routing()
            experts()
            norm(4, nfin[:], h)
            dve.wait_ge(S["h_ready"], 5)
            v.nop().then_inc(S["final_out"], 1)


def _constants():
    c = {"ones": np.ones((P, P)), "ident": np.eye(P), "iota": np.tile(np.arange(P), (P, 1)),
         "before": np.triu(np.ones((P, P)), 1)}
    i = np.arange(P)
    c["blk"] = (i[:, None] // N == i[None, :] // N) * 1.0

    def masks(chunk, half, r):
        same = chunk[:, None] == chunk[None, :]
        low, up = r[:, None] > r[None, :], r[:, None] < r[None, :]
        half_same = half[:, None] == half[None, :]
        return np.stack([same & half_same & low, same & half_same & up, same & ~half_same & up,
                         same & up, same & (r[:, None] <= r[None, :])], 1) * 1.0

    c["masks"] = masks(i // CH, i // 16, i)
    r = np.arange(TILES[2][1])
    chunk = np.where(r < 16, 0, r - 15)
    c["masks_s"] = masks(chunk, chunk, r)
    s = (i[:, None] // CH == np.arange(4)[None, :]) * 1.0
    c["sel_c"] = np.stack([s, -s], 1)
    s = (chunk[:, None] == np.arange(MAXC)[None, :]) * 1.0
    c["sel_s"] = np.stack([s, -s], 1)
    t = np.arange(T)
    c["keep"] = np.tile(((t % CH != 0) & (t < TP)) * 1.0, (P, 1))
    c["eps"] = np.tile(np.array([EPS_RMS, EPS_GN]), (P, 1))
    return {k: np.ascontiguousarray(v, dtype=np.float32) for k, v in c.items()}


def _cols(v):
    v = v.reshape(v.shape[:-1] + (-1, P))
    return np.moveaxis(v, -1, 0)


def _slot(parts):
    out = np.zeros((P, SLOT), np.float32)
    at = 0
    for w in parts:
        w = w.reshape(P, -1)
        out[:, at:at + w.shape[1]] = w
        at += w.shape[1]
    return out


def _tile(w, n):
    return w[:, n * P:(n + 1) * P].reshape(-1, P, P).transpose(1, 0, 2)


def _stream(i):
    slots = []
    for l in range(DEPTH):
        n = 0
        for k in WIN_TILES:
            slots.append(_slot([_tile(i["w_in"][l], n + j) for j in range(k)]))
            n += k
        for n in range(0, DC, 2):
            slots.append(_slot([_tile(i[w][l], n + j) for j in range(2) for w in ("s5_glu1", "s5_glu2")]))
        for n in range(0, DC, 4):
            slots.append(_slot([_tile(i["rw_w_bo"][l], n + j) for j in range(4)]))
        for n in range(0, DC, 2):
            slots.append(_slot([_tile(i["w_out"][l], n + j) for j in range(2)]))
        if l == 0:
            for n in range(CF):
                slots.append(_slot([_tile(i[w][0], n) for w in ("ffn_w1", "ffn_w3")]))
            blocks = [_tile(i["ffn_w2"][0], n)[:, k] for n in range(DC) for k in range(CF)]
            for b in range(0, len(blocks), 16):
                slots.append(_slot(blocks[b:b + 16]))
    slots = np.stack(slots)
    assert slots.shape[0] == S_DENSE
    up = [i[w][0].reshape(E, DC, P, NG, FW).transpose(0, 3, 2, 1, 4).reshape(E, NG, P, SLOT) for w in ("moe_w1", "moe_w3")]
    down = i["moe_w2"][0].reshape(E, NG, 2, P, D).transpose(0, 1, 3, 2, 4).reshape(E, NG, P, SLOT)
    experts = np.empty((E, S_EXPERT, P, SLOT), np.float32)
    parts = {"w1": up[0], "w3": up[1], "w2": down}
    for n, (kind, g) in enumerate(ORDER):
        experts[:, n] = parts[kind][:, g]
    return np.concatenate([slots, experts.reshape(E * S_EXPERT, P, SLOT)])


def layout(inputs):
    i = {k: np.asarray(v) for k, v in inputs.items()}
    a = _constants()
    a["wstream"] = _stream(i)
    a["x"] = _cols(np.concatenate([i["meta_tokens"], i["x_prompt"][0], i["x_sample"][:, 0]])).transpose(0, 2, 1)
    names = {"norm_mix": "norm_mix", "norm_ffn": "norm_ffn", "d": "s5_d", "mu": "rw_mu", "w0": "rw_w0", "a0": "rw_a0",
             "k_k": "rw_k_k", "k_a": "rw_k_a", "r_k": "rw_r_k", "gn_g": "rw_gn_g", "gn_b": "rw_gn_b"}
    a["pv"] = np.concatenate([_cols(i[names[k]].reshape(DEPTH, -1)) for k in PV], 2)
    a["nfin"] = _cols(i["norm_final"])

    def states(v):
        return _cols(v.reshape(DEPTH, G5 * S5P)).reshape(P, DEPTH * JT)

    a["lam"] = np.stack([states(i["s5_lam_re"]), states(i["s5_lam_im"]),
                         states(np.repeat(i["s5_log_dt"][:, :, None], S5P, 2))], 1)
    a["x0"] = np.stack([_cols(i[k].reshape(DEPTH, NS, -1)).transpose(0, 1, 3, 2) for k in ("state_s5_re", "state_s5_im")], 2)
    a["s0"] = i["state_rwkv"].reshape(DEPTH, NS, CB, 2, N, N).transpose(0, 3, 5, 2, 1, 4).reshape(DEPTH, P, CB, NS, N)
    a["shift0"] = _cols(i["state_shift"]).transpose(0, 1, 3, 2)
    a["router"] = i["moe_router"][0].reshape(DC, P, E).transpose(1, 0, 2)
    sb_, sc_ = np.zeros((DEPTH, P, CA, 2, P), np.float32), np.zeros((DEPTH, P, JT, 2, 32), np.float32)
    for c, (nb, ncc) in enumerate((("s5_b_re", "s5_c_re"), ("s5_b_im", "s5_c_im"))):
        for g in range(G5):
            j, half = g // 2, g % 2
            q = 32 * (j % 4) + S5C * half
            sb_[:, q:q + S5C, j // 4, c, S5P * half:S5P * (half + 1)] = i[nb][:, g].transpose(0, 2, 1)
            sc_[:, S5P * half:S5P * (half + 1), j, c, S5C * half:S5C * (half + 1)] = i[ncc][:, g].transpose(0, 2, 1)
    a["s5_b"], a["s5_c"] = sb_, sc_
    lo = np.empty((DEPTH, P, 2, DB), np.float32)
    lo[:, 0:64, 0], lo[:, 64:, 0], lo[:, :, 1] = i["rw_w_up"], i["rw_a_up"], i["rw_g_up"]
    a["lora_up"] = lo
    return {k: np.ascontiguousarray(v) for k, v in a.items()}


OUTS = {"y": (P, DC, T), "o_shift": (DEPTH, P, CR, 1 + NS), "o_s5": (DEPTH, P, JT, 2, 1 + NS),
        "o_rw": (DEPTH, P, CB, MAXC, N)}


def results(r):
    y = r["y"].transpose(2, 1, 0).reshape(T, D)
    sh = r["o_shift"].transpose(0, 3, 2, 1).reshape(DEPTH, 1 + NS, PRW)
    s5 = r["o_s5"].transpose(3, 0, 4, 2, 1).reshape(2, DEPTH, 1 + NS, G5, S5P)
    rw = r["o_rw"].reshape(DEPTH, 2, N, CB, MAXC, N).transpose(0, 4, 3, 1, 5, 2).reshape(DEPTH, MAXC, H, N, N)
    c = np.ascontiguousarray
    return (c(y[None, N_META:TP]), c(y[TP:, None]), c(s5[0, :, :1]), c(s5[1, :, :1]), c(rw[:, :1]), c(sh[:, :1]),
            c(s5[0, :, 1:]), c(s5[1, :, 1:]), c(rw[:, 1:]), c(sh[:, 1:]))


def kernel(**inputs):
    import concourse.bacc as bacc
    from concourse.bass_utils import run_bass_kernel_spmd

    nc = bacc.Bacc("TRN2", target_bir_lowering=False, num_devices=1)
    arrays = {f"{k}_dram": v for k, v in layout(inputs).items()}
    a = {k[:-5]: nc.dram_tensor(k, v.shape, F32, kind="ExternalInput").ap() for k, v in arrays.items()}
    for k, shape in OUTS.items():
        a[k] = nc.dram_tensor(f"{k}_dram", shape, F32, kind="ExternalOutput").ap()
    build(nc, a)
    r = run_bass_kernel_spmd(nc, [arrays], core_ids=[0]).results[0]
    return results({k: np.asarray(r[f"{k}_dram"]) for k in OUTS})
```

```python
import math
from contextlib import ExitStack

import numpy as np

import concourse.bass as bass
from concourse import mybir

ALU = mybir.AluOpType
ACT = mybir.ActivationFunctionType
AX = mybir.AxisListType
F32 = mybir.dt.float32
I32 = mybir.dt.int32
U32 = mybir.dt.uint32
F32R = mybir.dt.float32r

P = 128
DEPTH = 2
D = 1024
DC = D // P
N_META = 16
TP = 272
NS = 8
T = TP + NS
G5, S5P, S5C = 32, 64, 16
DA = G5 * S5C
CA = DA // P
JT = G5 * S5P // P
LEVELS = 9
H, N = 8, 64
DB = H * N
CB = DB // P
PRW = 3 * DB + 64 + 64 + 128
CR = PRW // P
PIN = DA + PRW + 2 * D
CIN = PIN // P
DFF = 2816
CF = DFF // P
E = 8
DE = 3584
FW = 256
NG = DE // FW
CAP = 128

CH = 32
TILES = [(0, 128, [(32 * c, 32) for c in range(4)]),
         (128, 128, [(32 * c, 32) for c in range(4)]),
         (256, 24, [(0, 16)] + [(16 + b, 1) for b in range(NS)])]
MAXC = 9

SLOT = 2048
RING = 7
WIN_TILES = [2] * 15 + [1] * 4
S_WIN, S_GLU, S_WBO, S_WOUT = len(WIN_TILES), 4, 2, 4
S_MIX = S_WIN + S_GLU + S_WBO + S_WOUT
S_FUP, S_FDOWN = CF, DC * CF // 16
S_DENSE = 2 * S_MIX + S_FUP + S_FDOWN
S_EXPERT = 3 * NG
assert S_DENSE % RING == 0 and S_EXPERT % RING == 0
MIX_AT = [0, S_MIX + S_FUP + S_FDOWN]
FFN_AT = S_MIX

PV = {}
_at = 0
for _n, _w in (("norm_mix", DC), ("norm_ffn", DC), ("d", CA), ("mu", CR), ("w0", CB), ("a0", CB),
               ("k_k", CB), ("k_a", CB), ("r_k", CB), ("gn_g", CB), ("gn_b", CB)):
    PV[_n] = (_at, _w)
    _at += _w
PVW = _at

EPS_RMS, EPS_GN = 1e-6, 64e-5
TWO_PI = 2 * math.pi
C1 = 6.28125
C2 = float(np.float32(TWO_PI - C1))
C3 = TWO_PI - C1 - C2
ROUND = 12582912.0
PI_IN = 3.1415925


SPLIT = 3


def expert_slots():
    order = []
    for g in range(NG + 2):
        if g < NG:
            order += [("w1", g), ("w3", g)]
        if g >= 2:
            order.append(("w2", g - 2))
    return order


ORDER = expert_slots()
SLOT_OF = {k: n for n, k in enumerate(ORDER)}
UP_DONE_BY = {min(SLOT_OF["w3", g] + SPLIT, S_EXPERT - 1): g for g in range(NG)}
TURNED_BY = {SLOT_OF["w1", g + 1] + SPLIT: g for g in range(NG - 1)}


def build(nc, a, debug=None):
    with ExitStack() as ctx:
        def sb(name, shape, dt=F32):
            return ctx.enter_context(nc.sbuf_tensor(name, shape, dt))

        def sem(name):
            return ctx.enter_context(nc.semaphore(name))

        arena = sb("arena", [P, 29472])
        arena_at = nc.sbuf_base - 4 * 29472

        def half(name, at, *shape):
            return nc.alloc_sbuf_tensor_at(name, [P, *shape], F32R, offset=arena_at + 4 * at).ap()

        ring = sb("ring", [P, RING, SLOT])
        x = sb("x", [P, DC, T])
        ones = sb("ones", [P, P])
        blk = sb("blk", [P, P])
        ident = sb("ident", [P, P])
        before = sb("before", [P, P])
        iota = sb("iota", [P, P])
        masks = sb("masks", [P, 5, P])
        masks_s = sb("masks_s", [24, 5, 24])
        sel_c = sb("sel_c", [P, 2, 4])
        sel_s = sb("sel_s", [24, 2, MAXC])
        keep = sb("keep", [P, T])
        eps = sb("eps", [P, 2])
        pv = sb("pv", [P, DEPTH, PVW])
        nfin = sb("nfin", [P, DC])
        lam = sb("lam", [P, 3, DEPTH * JT])
        x0 = sb("x0", [P, DEPTH, 2, JT, NS])
        s0 = sb("s0", [P, CB, NS, N])
        shift0 = sb("shift0", [P, DEPTH, CR, NS])
        router = sb("router", [P, DC, E])
        qq = sb("qq", [P, 3, DEPTH * JT])
        apow = sb("apow", [P, LEVELS, 3, DEPTH * JT])
        axt = sb("axt", [P, 2, JT, NS])
        rstd = sb("rstd", [P, 2, T])
        wend = sb("wend", [P, CB, MAXC + 8])
        s5out = sb("s5out", [P, JT, 2, 1 + NS])
        top_i = sb("top_i", [P, 3, E], U32)
        n_int = sb("n_int", [P, 1], I32)

        pools = [ctx.enter_context(nc.psum_tensor(f"bank{i}", [P, 512], F32)) for i in range(8)]

        def ar(at, *shape):
            n = 1
            for s in shape:
                n *= s
            v = arena[:, at:at + n]
            if len(shape) == 1:
                return v
            names = "abcd"[:len(shape)]
            return v.rearrange(f"p ({' '.join(names)}) -> p {' '.join(names)}",
                               **{k: s for k, s in zip(names[1:], shape[1:])})

        gate = ar(0, 2 * DC, T)
        h = ar(4480, DC, T)
        u = ar(6720, CA, T)
        s5_b = ar(7840, CA, 2, P)
        s5_c = ar(8864, JT, 2, 32)
        lora_up = ar(9888, 2, DB)
        prow = ar(10912, CR, T + 1)
        z = ar(14848, CR, T)
        sq = ar(14848, DC, T)
        sq_2 = ar(4480, DC, T)
        s5x = ar(18768, 4, 2, T)
        y5 = ar(21008, CA, T)
        glu_s = ar(18768, 2, T)
        F0 = 20512
        small = ar(22128, 18, DEPTH * JT)
        kr = ar(F0, CB, 2, T)
        beta, chi, beta_e, chi_e, gg, bonus = (ar(F0 + CB * T * (2 + i), CB, T) for i in range(6))
        tmp = [ar(10912 + 1120 * i, CB, T) for i in range(3)] + [ar(4480 + 1120 * i, CB, T) for i in range(2)]
        o_t = z[:, 4:8, :]
        gpre, hst = ar(18208, CB, MAXC, N), ar(4480, CB, MAXC, N)
        rt, ov = ar(14848, CB, P), ar(15360, CB, P)
        v_bd, be_bd, nx_bd = (ar(4480 + CB * MAXC * N + 2304 * i, 2, 2, MAXC, N) for i in range(3))
        PAIR_BUFFERS = ("am", "pm", "a2", "p2", "e1", "e2", "xk", "yk", "zk", "poff", "akt", "mbt", "mkt")
        PAIR_TOKENS = ("v_tok", "be_tok", "ch_tok")
        h_f = ar(10912, DC, T)
        silu_s, act_f = ar(6720, 2, T), ar(7280, 2, T)
        h_hi, h_lo = half("h_hi", 4480, DC, T), half("h_lo", 2048, DC, T)
        act_hi, act_lo = half("act_hi", 10912, CF, T), half("act_lo", 17072, CF, T)
        fw_hi = [half(f"fw_hi{i}", at, SLOT) for i, at in enumerate((0, 25280))]
        fw_lo = [half(f"fw_lo{i}", at, SLOT) for i, at in enumerate((23232, 27328))]
        zcar = ar(14300, CB, N)
        route = ar(14560, 12, 3, E)
        chosen, weight, place = (ar(18124 + 30 * i, 3, E + 2) for i in range(3))
        w_hi = [half(f"w_hi{i}", at, SLOT) for i, at in enumerate((0, 18240, 22336))]
        w_lo = [half(f"w_lo{i}", at, SLOT) for i, at in enumerate((2048, 20288, 24384))]
        he_hi, he_lo = half("he_hi", 26432, DC, CAP), half("he_lo", 27456, DC, CAP)
        at_hi, at_lo = half("at_hi", 28480, 2, 2 * CAP), half("at_lo", 6720, 2, 2 * CAP)
        h_tok = ar(7840, 3, D)
        sel_p, sel_w = ar(11936, 3, CAP), ar(12320, 3, CAP)
        mix_w = ar(12704, T)
        sil_e, act_e = ar(13000, 2, FW), ar(13512, 2, FW)
        y_e = ar(17100, D)

        names = ["first_in", "consts", "small_w", "s0_in", "shift_out", "s5_out", "rw_out", "y_stored",
                 "final_out", "norm_sq", "norm_ps", "norm_rt", "h_ready", "x_ready", "disc_exp1", "disc_ang",
                 "disc_exp2", "disc_done", "proj_ps", "proj_out", "pad_zero", "act_quad", "act_oct",
                 "zcar_out", "place_moved", "bu_ps", "bu_q", "bu_used", "scan_done", "y5_ps", "y5_mix",
                 "y5_done", "lora_ps", "lora_in", "lora_out", "z_diff", "z_mu", "ka_one", "bonus_rk", "kk_out",
                 "ka_out", "kp_out", "exps_inverse", "z_ready", "kk_sq", "kk_ps", "kk_norm", "cum_ready",
                 "exps_ready", "bonus_in", "bonus_ps", "fm_ready", "glu_ps", "glu_sig", "glu_out", "tr_ps",
                 "tr_out", "gram_a_ps", "gram_b_ps", "gram_c_ps", "gram_out", "gram_rest_out", "sq_ps",
                 "sq_out", "quad_ps", "quad_out", "oct_ps", "oct_out", "e8_ps", "e8_out", "y_ps", "y_out",
                 "off_ps", "off_out", "fix_ps", "x_out", "gh_ps", "h_out", "gh_out", "ro_ps", "ro_out",
                 "ov_out", "z_ps", "z_out", "zs_ps", "zs_out", "o_ps", "o_out", "o_mean_ps", "o_cent", "o_sq",
                 "o_var_ps", "o_std", "o_ready", "bo_ps", "bo_out", "wo_ps", "wo_out", "h_hi_out", "h_split",
                 "up_ps", "up_silu", "act_ready", "act_hi_out", "act_split", "ffn_hi", "down_slot", "down_ps",
                 "down_out", "logit_ps", "gates_in", "gates_out", "ht_ps", "ht_out", "count_in", "count_ps",
                 "count_out", "hi_ready", "slot_done", "selp_ready", "selw_ready", "ga_ps", "ga_hi", "ga_lo",
                 "mw_ps", "mw_out", "eup_silu", "eup_act", "et_ps", "et_hi", "et_lo", "ey_out", "em_ps",
                 "em_out", "weights_used", "dve_step", "n_ready"]
        S = {n: sem(n) for n in names}
        slot_in = [sem(f"slot_in{i}") for i in range(RING)]
        block = ctx.enter_context(nc.Block())

        def slot(n):
            return ring[:, n % RING, :]

        def squares(i):
            return sq_2 if i == 2 else sq

        def pair_buffers(l):
            base = MIX_AT[l] + S_WIN
            views = {}
            for i, name in enumerate(PAIR_BUFFERS):
                at = slot(base + i // 4)[:, i % 4 * 512:(i % 4 + 1) * 512]
                views[name] = at.rearrange("p (i a t) -> p i a t", i=2, a=2)
            for i, name in enumerate(PAIR_TOKENS):
                at = slot(base + 3)[:, 512 + i * 256:512 + (i + 1) * 256]
                views[name] = at.rearrange("p (i a k) -> p i a k", i=2, a=2)
            return views

        FIRST = [(x, "x"), (lam, "lam"), (ones, "ones"), (eps, "eps"), (pv, "pv")]
        CONSTS = [(blk, "blk"), (ident, "ident"), (before, "before"), (iota, "iota"),
                  (masks, "masks"), (masks_s, "masks_s"), (sel_c, "sel_c"), (sel_s, "sel_s"),
                  (keep, "keep"), (nfin, "nfin"), (x0, "x0"), (shift0, "shift0"), (router, "router")]
        N_FIRST, N_CONST = 16 * len(FIRST), 16 * len(CONSTS)

        @block.sync
        def _(sp):
            for t, n in FIRST:
                sp.dma_start(t[:], a[n]).then_inc(S["first_in"], 16)
            for s in range(RING):
                sp.dma_start(ring[:, s, :], a["wstream"][s]).then_inc(slot_in[s], 16)
            with sp.Fori(1, (S_DENSE + E * S_EXPERT) // RING) as r:
                for s in range(RING):
                    sp.wait_ge(S["weights_used"], r * RING + (s - RING + 1))
                    sp.dma_start(ring[:, s, :], a["wstream"][bass.ds(r * RING + s, 1)].rearrange("o p n -> (o p) n"))\
                        .then_inc(slot_in[s], 16)
            sp.wait_ge(S["n_ready"], 1)
            npass = sp.value_load(n_int[0:1, 0:1], min_val=1, max_val=3)
            with sp.If(npass > 1):
                with sp.Fori(1, npass) as p:
                    with sp.Fori(0, E * S_EXPERT // RING) as r:
                        for s in range(RING):
                            sp.wait_ge(S["weights_used"], p * (E * S_EXPERT) + r * RING + (S_DENSE + s - RING + 1))
                            sp.dma_start(ring[:, s, :], a["wstream"][bass.ds(r * RING + (S_DENSE + s), 1)]
                                         .rearrange("o p n -> (o p) n")).then_inc(slot_in[s], 16)

        @block.gpsimd
        def _(pool):
            def col(l, name, i):
                c0 = PV[name][0]
                return pv[:, l, c0 + i:c0 + i + 1]

            def mixer_features(l):
                g = nc.gpsimd
                pool.wait_ge(S["first_in"], N_FIRST)
                pool.wait_ge(S["consts"], N_CONST)
                pool.wait_ge(S["pad_zero"], l + 1)
                g.tensor_tensor(z[:, :, 0:TP], prow[:, :, 0:TP], prow[:, :, 1:TP + 1], ALU.subtract)
                g.tensor_tensor(z[:, :, TP:T], shift0[:, l], prow[:, :, TP + 1:T + 1], ALU.subtract)\
                    .then_inc(S["z_diff"], 1)
                pool.wait_ge(S["z_diff"], l + 1)
                for c in range(CR):
                    ins = g.tensor_scalar(z[:, c, :], z[:, c, :], col(l, "mu", c), None, ALU.mult)
                ins.then_inc(S["z_mu"], 1)
                pool.wait_ge(S["z_mu"], l + 1)
                g.tensor_tensor(z, z, prow[:, :, 1:T + 1], ALU.add).then_inc(S["z_ready"], 1)
                pool.wait_ge(S["z_ready"], l + 1)
                for f in range(CB):
                    ins = g.tensor_scalar(chi[:, f, :], z[:, 4 + f, :], col(l, "k_k", f), None, ALU.mult)
                ins.then_inc(S["kk_out"], 1)
                pool.wait_ge(S["lora_out"], 3 * CB * l + 2 * CB)
                pool.wait_ge(S["kk_sq"], l + 1)
                pool.wait_ge(S["kk_out"], l + 1)
                for f in range(CB):
                    ins = g.tensor_scalar(bonus[:, f, :], tmp[2][:, f, :], 1.0, col(l, "k_a", f), ALU.subtract, ALU.mult)
                ins.then_inc(S["ka_out"], 1)
                pool.wait_ge(S["ka_out"], l + 1)
                kp = z[:, 4:8, :]
                g.tensor_scalar(bonus, bonus, 1.0, None, ALU.add).then_inc(S["ka_one"], 1)
                pool.wait_ge(S["ka_one"], l + 1)
                g.tensor_tensor(kp, bonus, kp, ALU.mult).then_inc(S["kp_out"], 1)
                pool.wait_ge(S["kp_out"], l + 1)
                g.tensor_tensor(bonus, z[:, 0:4, :], kp, ALU.mult).then_inc(S["bonus_rk"], 1)
                pool.wait_ge(S["bonus_rk"], l + 1)
                for f in range(CB):
                    ins = g.tensor_scalar(bonus[:, f, :], bonus[:, f, :], col(l, "r_k", f), None, ALU.mult)
                ins.then_inc(S["bonus_in"], 1)

            for l in range(DEPTH):
                if l:
                    pool.wait_ge(S["x_ready"], 2 * l - 1)
                pool.dma_start(s5_b, a["s5_b"][l]).then_inc(S["small_w"], 16)
                pool.dma_start(s5_c, a["s5_c"][l]).then_inc(S["small_w"], 16)
                pool.dma_start(lora_up, a["lora_up"][l]).then_inc(S["small_w"], 16)
                pool.dma_start(s0[:], a["s0"][l]).then_inc(S["s0_in"], 16)
                pool.wait_ge(S["proj_out"], CIN * l + CA + CR)
                pool.dma_start(a["o_shift"][l], prow[:, :, TP:T + 1]).then_inc(S["shift_out"], 16)
                mixer_features(l)
                pool.wait_ge(S["scan_done"], JT * (l + 1))
                pool.dma_start(a["o_s5"][l], s5out[:]).then_inc(S["s5_out"], 16)
                pool.wait_ge(S["zs_out"], H * (l + 1))
                pool.dma_start(a["o_rw"][l], hst).then_inc(S["rw_out"], 16)
            for n in ("shift_out", "s5_out", "rw_out"):
                pool.wait_ge(S[n], 16 * DEPTH)
            pool.wait_ge(S["final_out"], 1)
            pool.dma_start(a["y"], h).then_inc(S["y_stored"], 16)
            pool.wait_ge(S["y_stored"], 16)

        PAIRS = 3 * CB // 2
        NU = 2 * PAIRS

        @block.tensor
        def _(pe):
            def mm(out, lhsT, rhs, start=True, stop=True, **k):
                return nc.tensor.matmul(out, lhsT, rhs, start=start, stop=stop, **k)

            def products(out, pairs, done, release=False):
                for i, (w, r) in enumerate(pairs):
                    ins = mm(out, w, r, i == 0, i == len(pairs) - 1)
                    if i == 0 and release:
                        ins.then_inc(S["weights_used"], 1)
                if done is not None:
                    ins.then_inc(S[done], 1)

            def give_back():
                pe.nop().then_inc(S["weights_used"], 1)

            def arrived(n):
                pe.wait_ge(slot_in[n % RING], 16 * (n // RING + 1))

            def norm(i):
                for c in range(DC):
                    pe.wait_ge(S["norm_sq"], DC * i + c + 1)
                    last = mm(pools[0][:, 0:T], ones[:], squares(i)[:, c, :], c == 0, c == DC - 1)
                    if c == 0 and i in (1, 3):
                        last.then_inc(S["weights_used"], 1)
                last.then_inc(S["norm_ps"], 1)

            def proj_tile(l, n, at):
                s, j = at
                if j == 0:
                    arrived(s)
                if n >= 3:
                    pe.wait_ge(S["proj_out"], CIN * l + n - 2)
                w = slot(s).rearrange("p (j k m) -> p j k m", j=2, k=DC)
                if n == 0:
                    for k in range(DC):
                        pe.wait_ge(S["h_ready"], 2 * l * DC + k + 1)
                        last = mm(pools[0][:, 0:T], w[:, j, k, :], h[:, k, :], k == 0, k == DC - 1)
                    last.then_inc(S["proj_ps"], 1)
                    return
                products(pools[n % 3][:, 0:T], [(w[:, j, k, :], h[:, k, :]) for k in range(DC)], "proj_ps",
                         release=j == 0)

            def bu_tile(l, j):
                aa, b = j // 4, j % 4
                if j == 0:
                    pe.wait_ge(S["small_w"], 48 * (l + 1))
                    pe.wait_ge(S["proj_out"], CIN * l + CA)
                if j >= 2:
                    pe.wait_ge(S["bu_used"], JT * l + j - 1)
                for c in range(2):
                    last = mm(pools[4 + 2 * (j % 2) + c][:, 0:T], s5_b[32 * b:32 * b + 32, aa, c, :],
                              u[32 * b:32 * b + 32, aa, :])
                last.then_inc(S["bu_ps"], 1)

            def y5_tile(l, j):
                aa, b = j // 4, j % 4
                pe.wait_ge(S["scan_done"], JT * l + j + 1)
                if b == 0 and j:
                    pe.wait_ge(S["y5_mix"], CA * l + aa)
                for c in range(2):
                    last = mm(pools[3][32 * b:32 * b + 32, 0:T], s5_c[:, j, c, :], s5x[:, j % 4, c, :],
                              c == 0, c == 1)
                last.then_inc(S["y5_ps"], 1)

            def glu(l):
                base = MIX_AT[l] + S_WIN
                pe.wait_ge(S["y5_done"], CA * (l + 1))
                for n in range(DC):
                    s = base + n // 2
                    if n % 2 == 0:
                        arrived(s)
                    if n >= 2:
                        pe.wait_ge(S["glu_out"], DC * l + n - 1)
                    w = slot(s).rearrange("p (j c k m) -> p j c k m", j=2, c=2, k=CA)
                    for c in range(2):
                        products(pools[2 * (n % 2) + c][:, 0:T], [(w[:, n % 2, c, k, :], y5[:, k, :]) for k in range(CA)],
                                 "glu_ps" if c else None)

            def lora(l):
                pe.wait_ge(S["lora_in"], l + 1)
                pe.wait_ge(S["bu_used"], JT * (l + 1))
                for i in range(3):
                    for f in range(CB):
                        n = 4 * i + f
                        if n >= 4:
                            pe.wait_ge(S["lora_out"], 3 * CB * l + n - 3)
                        o = pools[4 + n % 4][:, 0:T]
                        if i < 2:
                            last = mm(o, lora_up[64 * i:64 * i + 64, 0, f * P:(f + 1) * P],
                                      z[64 * i:64 * i + 64, 12, :])
                        else:
                            last = mm(o, lora_up[:, 1, f * P:(f + 1) * P], z[:, 13, :])
                        last.then_inc(S["lora_ps"], 1)
                pe.wait_ge(S["kk_sq"], l + 1)
                pe.wait_ge(S["lora_out"], 3 * CB * (l + 1))
                for f in range(CB):
                    last = mm(pools[4 + f][:, 0:T], blk[:], tmp[0][:, f, :])
                last.then_inc(S["kk_ps"], 1)

            def bonus_sums(l):
                pe.wait_ge(S["bonus_in"], l + 1)
                pe.wait_ge(S["kk_norm"], l + 1)
                for f in range(CB):
                    last = mm(pools[4 + f][:, 0:T], blk[:], bonus[:, f, :])
                last.then_inc(S["bonus_ps"], 1)

            def pair(l, m, f0):
                t0, nt, chunks = TILES[m]
                ncn = len(chunks)
                n_p = PAIRS * l + 2 * m + f0 // 2
                n_u = 2 * n_p
                tok = slice(t0, t0 + nt)
                w = pair_buffers(l)
                if m == 0 and f0 == 0:
                    pe.wait_ge(S["fm_ready"], l + 1)
                if n_p:
                    pe.wait_ge(S["ov_out"], n_u)
                    if f0 == 0:
                        pe.wait_ge(S["o_out"], H * (3 * l + m))
                for i in range(2):
                    f = f0 + i
                    for j, src in enumerate((kr[:, f, 0, tok], z[:, 8 + f, tok], beta_e[:, f, tok], chi_e[:, f, tok])):
                        last = nc.tensor.transpose(pools[4 * i][0:nt, j * P:(j + 1) * P], src, ident[:])
                    last.then_inc(S["tr_ps"], 1)
                if n_p:
                    pe.wait_ge(S["ro_out"], n_u)
                for i in range(2):
                    for par in range(2):
                        q = slice(64 * par, 64 * par + 64)
                        last = mm(pools[1 + 4 * par][0:nt, i * P:i * P + nt], kr[q, f0 + i, 0, tok], beta[q, f0 + i, tok])
                last.then_inc(S["gram_a_ps"], 1)
                if n_p:
                    pe.wait_ge(S["gh_out"], n_u)
                    pe.wait_ge(S["h_out"], n_u)
                for bank, left, signal in ((2, beta, "gram_b_ps"), (3, chi, "gram_c_ps")):
                    for i in range(2):
                        for par in range(2):
                            q = slice(64 * par, 64 * par + 64)
                            out = pools[bank + 4 * par][0:nt, i * 256:(i + 1) * 256].rearrange("p (c t) -> p c t", c=2)
                            last = mm(out[:, :, 0:nt], left[q, f0 + i, tok], kr[q, f0 + i, :, tok])
                    last.then_inc(S[signal], 1)

                def at(bank, i, n=nt):
                    return [pools[bank + 4 * i][0:nt, par * P:par * P + n] for par in range(2)]

                def low(m_, i, par):
                    return m_[0:nt, i, par, 0:nt]

                pe.wait_ge(S["gram_out"], n_p + 1)
                for i in range(2):
                    pe.wait_ge(S["tr_out"], n_u + i + 1)
                    for par in range(2):
                        mm(at(0, i)[par], low(w["pm"], i, par), low(w["am"], i, par))
                        mm(pools[4 * i][0:nt, (2 + par) * P:(2 + par) * P + nt], low(w["am"], i, par), low(w["pm"], i, par))
                        last = mm(pools[1 + 4 * i][0:nt, par * N:(par + 1) * N], low(w["akt"], i, par), w["v_tok"][0:nt, i, par, :])
                    last.then_inc(S["sq_ps"], 1)
                pe.wait_ge(S["gram_rest_out"], n_p + 1)
                for i in range(2):
                    pe.wait_ge(S["sq_out"], n_u + i + 1)
                    for par in range(2):
                        mm(at(2, i)[par], low(w["p2"], i, par), low(w["a2"], i, par))
                        mm(pools[2 + 4 * i][0:nt, (2 + par) * P:(2 + par) * P + nt], low(w["a2"], i, par), low(w["p2"], i, par))
                        last = mm(at(3, i)[par], low(w["a2"], i, par), low(w["e1"], i, par))
                    last.then_inc(S["quad_ps"], 1)
                for i in range(2):
                    pe.wait_ge(S["quad_out"], n_u + i + 1)
                    for par in range(2):
                        mm(at(1, i)[par], low(w["pm"], i, par), low(w["am"], i, par))
                        last = mm(at(0, i)[par], low(w["am"], i, par), low(w["e2"], i, par))
                    last.then_inc(S["oct_ps"], 1)
                for i in range(2):
                    pe.wait_ge(S["oct_out"], n_u + i + 1)
                    for par in range(2):
                        last = mm(at(2, i)[par], low(w["a2"], i, par), low(w["e1"], i, par))
                    last.then_inc(S["e8_ps"], 1)
                for i in range(2):
                    pe.wait_ge(S["e8_out"], n_u + i + 1)
                    for par in range(2):
                        last = mm(at(0, i, P)[par], low(w["e2"], i, par), w["xk"][0:nt, i, par, :])
                    last.then_inc(S["y_ps"], 1)
                for i in range(2):
                    pe.wait_ge(S["y_out"], n_u + i + 1)
                    for par in range(2):
                        last = mm(at(3, i, P)[par], low(w["poff"], i, par), w["yk"][0:nt, i, par, :])
                    last.then_inc(S["off_ps"], 1)
                for i in range(2):
                    pe.wait_ge(S["off_out"], n_u + i + 1)
                    for par in range(2):
                        last = mm(at(1, i, P)[par], low(w["e2"], i, par), w["zk"][0:nt, i, par, :])
                    last.then_inc(S["fix_ps"], 1)
                for i in range(2):
                    pe.wait_ge(S["x_out"], n_u + i + 1)

                    def transition(bank_g, bank_h, c0, n_c, col_):
                        for par in range(2):
                            q = slice(64 * par, 64 * par + 64)
                            g_, h_ = (pools[b + 4 * i][q, col_:col_ + n_c * N].rearrange("p (c v) -> p c v", c=n_c)
                                      for b in (bank_g, bank_h))
                            bd = slice(c0, c0 + n_c)
                            mm(g_, w["xk"][0:nt, i, par, 0:N], be_bd[0:nt, i, par, bd, :])
                            mm(h_, w["ch_tok"][0:nt, i, par, :], v_bd[0:nt, i, par, bd, :], True, False)
                            last_ = mm(h_, w["be_tok"][0:nt, i, par, :], nx_bd[0:nt, i, par, bd, :], False, True)
                        return last_
                    if ncn > 8:
                        transition(1, 0, 8, 1, P)
                    for par in range(2):
                        q = slice(64 * par, 64 * par + 64)
                        mm(pools[1 + 4 * i][q, 0:nt], w["xk"][0:nt, i, par, 0:N], low(w["mbt"], i, par))
                        mm(pools[4 * i][q, 0:nt], w["zk"][0:nt, i, par, 0:N], low(w["mbt"], i, par), True, False)
                        last = mm(pools[4 * i][q, 0:nt], w["v_tok"][0:nt, i, par, :], low(w["mkt"], i, par), False, True)
                    last.then_inc(S["ro_ps"], 1)
                    transition(2, 3, 0, min(8, ncn), 0).then_inc(S["gh_ps"], 1)

            def chain(l, m):
                t0, nt, chunks = TILES[m]
                k = NU * l + CB * (m + 1)
                pe.wait_ge(S["gh_out"], k)
                pe.wait_ge(S["h_out"], k)
                pe.wait_ge(S["ro_out"], k)
                pe.wait_ge(S["ov_out"], k)
                seq = 4 if m < 2 else 1
                if m:
                    pe.wait_ge(S["zcar_out"], 2 * l + m)
                for c in range(seq):
                    n_c = 9 * l + 4 * m + c
                    pe.wait_ge(S["z_out"], n_c + l + 1)
                    for f in range(CB):
                        for par in range(2):
                            q = slice(64 * par, 64 * par + 64)
                            src = zcar[q, f, :] if c == 0 else hst[q, f, c - 1, :]
                            last = mm(pools[par][q, f * N:(f + 1) * N], gpre[q, f, c, :], src)
                    last.then_inc(S["z_ps"], 1)
                if m == 2:
                    pe.wait_ge(S["s0_in"], 16 * (l + 1))
                    for f in range(CB):
                        for par in range(2):
                            n = 2 * f + par
                            q = slice(64 * par, 64 * par + 64)
                            if n >= 2:
                                pe.wait_ge(S["zs_out"], H * l + n - 1)
                            for b in range(NS):
                                last = mm(pools[2 + par][q, b * N:(b + 1) * N], gpre[q, f, 1 + b, :], s0[q, f, b, :])
                            last.then_inc(S["zs_ps"], 1)
                for f in range(CB):
                    for par in range(2):
                        n = 2 * f + par
                        q = slice(64 * par, 64 * par + 64)
                        k = H * (3 * l + m) + n
                        if k >= 2:
                            pe.wait_ge(S["o_out"], k - 1)
                        for c, (r0, w) in enumerate(chunks):
                            if m == 2 and c:
                                src = s0[q, f, c - 1, :]
                            else:
                                src = zcar[q, f, :] if c == 0 else hst[q, f, c - 1, :]
                            last = mm(pools[4 + par][q, r0:r0 + w], src, rt[q, f, r0:r0 + w])
                        last.then_inc(S["o_ps"], 1)

            def finish_rwkv(l):
                pe.wait_ge(S["o_out"], 3 * H * (l + 1))
                pe.nop().then_inc(S["weights_used"], S_GLU)
                for f in range(CB):
                    last = mm(pools[f][:, 0:T], blk[:], o_t[:, f, :])
                last.then_inc(S["o_mean_ps"], 1)
                pe.wait_ge(S["o_sq"], l + 1)
                for f in range(CB):
                    last = mm(pools[4 + f][:, 0:T], blk[:], tmp[1][:, f, :])
                last.then_inc(S["o_var_ps"], 1)
                pe.wait_ge(S["o_ready"], l + 1)
                base = MIX_AT[l] + S_WIN + S_GLU
                for n in range(DC):
                    s = base + n // 4
                    if n % 4 == 0:
                        arrived(s)
                    if n >= 4:
                        pe.wait_ge(S["bo_out"], DC * l + n - 3)
                    w = slot(s).rearrange("p (j k m) -> p j k m", j=4, k=CB)
                    products(pools[n % 4][:, 0:T], [(w[:, n % 4, k, :], o_t[:, k, :]) for k in range(CB)], "bo_ps",
                             release=n == 4)
                base += S_WBO
                pe.wait_ge(S["bo_out"], DC * (l + 1))
                give_back()
                for n in range(DC):
                    s = base + n // 2
                    if n % 2 == 0:
                        arrived(s)
                    if n >= 4:
                        pe.wait_ge(S["wo_out"], DC * l + n - 3)
                    w = slot(s).rearrange("p (j k m) -> p j k m", j=2, k=DC)
                    products(pools[4 + n % 4][:, 0:T], [(w[:, n % 2, k, :], gate[:, k, :]) for k in range(DC)], "wo_ps",
                             release=n % 2 == 0 and n > 0)
                norm(1 + 2 * l)

            def mix(l):
                norm(2 * l)
                pe.wait_ge(S["consts"], N_CONST)
                at, n = [], 0
                for s, k in enumerate(WIN_TILES):
                    at += [(MIX_AT[l] + s, j) for j in range(k)]
                for n in range(CA):
                    proj_tile(l, n, at[n])
                n = CA
                for j in range(JT):
                    bu_tile(l, j)
                    for _ in range(2):
                        if n < CIN:
                            proj_tile(l, n, at[n])
                            n += 1
                    if j >= 4:
                        y5_tile(l, j - 4)
                pe.wait_ge(S["proj_out"], CIN * (l + 1))
                give_back()
                lora(l)
                for j in range(JT - 4, JT):
                    y5_tile(l, j)
                glu(l)
                bonus_sums(l)
                for m in range(3):
                    for f0 in range(0, CB, 2):
                        pair(l, m, f0)
                    chain(l, m)
                finish_rwkv(l)

            def split_products(out, w, r, start, stop):
                (wh, wl), (rh, rl) = w, r
                mm(out, wh, rh, start, False)
                mm(out, wh, rl, False, False)
                return mm(out, wl, rh, False, stop)

            def ffn():
                for n in range(CF):
                    pe.wait_ge(S["weights_used"], FFN_AT + n + 1)
                    if n >= 2:
                        pe.wait_ge(S["act_ready"], n - 1)
                    w_h, w_l = (t[n % 2].rearrange("p (c k m) -> p c k m", c=2, k=DC) for t in (fw_hi, fw_lo))
                    for c in range(2):
                        for k in range(DC):
                            if n == 0 and c == 0 and k % 4 == 0:
                                pe.wait_ge(S["h_split"], k // 4 + 1)
                            last = split_products(pools[2 * (n % 2) + c][:, 0:T], (w_h[:, c, k, :], w_l[:, c, k, :]),
                                                  (h_hi[:, k, :], h_lo[:, k, :]), k == 0, k == DC - 1)
                    last.then_inc(S["up_ps"], 1)
                for n in range(DC):
                    if n >= 4:
                        pe.wait_ge(S["down_out"], n - 3)
                    for k in range(CF):
                        b = n * CF + k
                        s = CF + b // 16
                        if b % 16 == 0:
                            pe.wait_ge(S["weights_used"], FFN_AT + s + 1)
                        if n == 0:
                            pe.wait_ge(S["act_split"], k + 1)
                        q = slice((b % 16) * P, (b % 16 + 1) * P)
                        last = split_products(pools[4 + n % 4][:, 0:T], (fw_hi[s % 2][:, q], fw_lo[s % 2][:, q]),
                                              (act_hi[:, k, :], act_lo[:, k, :]), k == 0, k == CF - 1)
                        if k == CF - 1:
                            last.then_inc(S["down_ps"], 1)
                        elif b % 16 == 15:
                            last.then_inc(S["down_slot"], 1)

            def routing():
                pe.wait_ge(S["h_ready"], 4 * DC)
                for m, (t0, nt, _) in enumerate(TILES):
                    for k in range(DC):
                        last = mm(pools[1][0:nt, m * E:(m + 1) * E], h[:, k, t0:t0 + nt], router[:, k, :], k == 0, k == DC - 1)
                last.then_inc(S["logit_ps"], 1)
                for m, (t0, nt, _) in enumerate(TILES):
                    for half in range(2):
                        n = 2 * m + half
                        if n >= 4:
                            pe.wait_ge(S["ht_out"], n - 3)
                        for j in range(4):
                            last = nc.tensor.transpose(pools[4 + n % 4][0:nt, j * P:(j + 1) * P],
                                                       h[:, 4 * half + j, t0:t0 + nt], ident[:])
                        last.then_inc(S["ht_ps"], 1)
                pe.wait_ge(S["count_in"], 1)
                for m, (t0, nt, _) in enumerate(TILES):
                    o = pools[2][0:nt, m * E:(m + 1) * E]
                    for mp in range(m):
                        mm(o, ones[:, 0:nt], chosen[:, mp, 1:E + 1], mp == 0, False)
                    mm(o, before[0:nt, 0:nt], chosen[0:nt, m, 1:E + 1], m == 0, True)
                for m, (t0, nt, _) in enumerate(TILES):
                    last = mm(pools[2][:, 3 * E:4 * E], ones[0:nt, :], chosen[0:nt, m, 1:E + 1], m == 0, m == 2)
                last.then_inc(S["count_ps"], 1)

            def gather(k, half_):
                for j in range(4):
                    for m, (t0, nt, _) in enumerate(TILES):
                        last = mm(pools[7 - half_][:, j * P:(j + 1) * P],
                                  h_tok[0:nt, m, (4 * half_ + j) * P:(4 * half_ + j + 1) * P],
                                  sel_p[0:nt, m, :], m == 0, m == 2)
                last.then_inc(S["ga_ps"], 1)

            def weights_to_rows(k):
                pe.wait_ge(S["selw_ready"], k + 1)
                for m, (t0, nt, _) in enumerate(TILES):
                    last = nc.tensor.transpose(pools[6][:, t0:t0 + nt], sel_w[0:nt, m, :], ident[0:nt, 0:nt])
                last.then_inc(S["mw_ps"], 1)

            def combine(k):
                pe.wait_ge(S["mw_out"], k + 1)
                pe.wait_ge(S["ey_out"], k + 1)
                for c in range(DC):
                    if c >= 2:
                        pe.wait_ge(S["em_out"], k * DC + (c - 1))
                    mm(pools[6 + c % 2][:, 0:T], y_e[:, c * P:(c + 1) * P], mix_w).then_inc(S["em_ps"], 1)

            def expert(i, k):
                pe.wait_ge(S["ga_lo"], k * 2 + 2)
                n = 0
                for g in range(NG + 2):
                    for part in range(2):
                        if g < NG:
                            pe.wait_ge(S["weights_used"], i * S_EXPERT + (S_DENSE + n + 1))
                            w_h, w_l = (t[n % SPLIT].rearrange("p (k m) -> p k m", k=DC) for t in (w_hi, w_lo))
                            for c in range(DC):
                                last = split_products(pools[g % 2][:, part * FW:(part + 1) * FW],
                                                         (he_hi[:, c, :], he_lo[:, c, :]), (w_h[:, c, :], w_l[:, c, :]),
                                                         c == 0, c == DC - 1)
                            last.then_inc(S["slot_done"], 1)
                            n += 1
                        if part == 0 and g == 0:
                            weights_to_rows(k)
                        if part == 0 and 1 <= g <= NG:
                            pe.wait_ge(S["eup_act"], i * NG + g)
                            for j in range(2):
                                last = nc.tensor.transpose(pools[2 + (g - 1) % 2][:, j * P:(j + 1) * P],
                                                           act_e[:, (g - 1) % 2, j * P:(j + 1) * P], ident[:])
                            last.then_inc(S["et_ps"], 1)
                        if g == NG and part == 0:
                            pe.wait_ge(S["em_out"], k * DC + DC)
                            pe.wait_ge(S["selp_ready"], k + 2)
                            gather(k, 0)
                    if g == 0:
                        combine(k)
                    if g >= 2:
                        pe.wait_ge(S["weights_used"], i * S_EXPERT + (S_DENSE + n + 1))
                        pe.wait_ge(S["et_lo"], i * NG + (g - 1))
                        if g == 2:
                            pe.wait_ge(S["ey_out"], k + 1)
                        w_h, w_l = (t[n % SPLIT].rearrange("p (k m) -> p k m", k=2) for t in (w_hi, w_lo))
                        for j in range(2):
                            q = slice(j * CAP, (j + 1) * CAP)
                            for hf in range(2):
                                last = split_products(pools[4 + hf][:], (at_hi[:, g % 2, q], at_lo[:, g % 2, q]),
                                                         (w_h[:, j, hf * 512:(hf + 1) * 512], w_l[:, j, hf * 512:(hf + 1) * 512]),
                                                         g == 2 and j == 0, g == NG + 1 and j == 1)
                        last.then_inc(S["slot_done"], 1)
                        n += 1
                        if g == NG:
                            gather(k, 1)

            def one_pass(p, i0, k0):
                pe.wait_ge(S["selp_ready"], k0 + 1)
                gather(k0, 0)
                gather(k0, 1)
                with pe.Fori(0, E) as e:
                    expert(e + i0, e + k0)
                weights_to_rows(k0 + E)
                combine(k0 + E)

            def experts():
                pe.wait_ge(S["count_out"], 1)
                pe.wait_ge(S["ht_out"], 6)
                one_pass(0, 0, 0)
                pe.wait_ge(S["n_ready"], 1)
                npass = pe.value_load(n_int[0:1, 0:1], min_val=1, max_val=3)
                with pe.If(npass > 1):
                    with pe.Fori(1, npass) as p:
                        pe.wait_ge(S["em_out"], p * (DC * (E + 1)))
                        one_pass(p, p * E, p * (E + 1))

            pe.wait_ge(S["first_in"], N_FIRST)
            mix(0)
            ffn()
            mix(1)
            routing()
            experts()
            norm(4)

        @block.scalar
        def _(ac):
            for t, n in CONSTS:
                ac.dma_start(t[:], a[n]).then_inc(S["consts"], 16)

            def fn(out, in_, func, **k):
                return nc.scalar.activation(out, in_, func, **k)

            def norm(i):
                if i == 4:
                    ac.wait_ge(S["x_ready"], i)
                for c in range(DC):
                    if i in (1, 3):
                        ac.wait_ge(S["wo_out"], DC * (i // 2) + c + 1)
                    if i == 2:
                        ac.wait_ge(S["down_out"], c + 1)
                    fn(squares(i)[:, c, :], x[:, c, :], ACT.Square).then_inc(S["norm_sq"], 1)
                ac.wait_ge(S["norm_ps"], i + 1)
                fn(rstd[:, 0, :], pools[0][:, 0:T], ACT.Sqrt, scale=1.0 / D, bias=eps[:, 0:1]).then_inc(S["norm_rt"], 1)

            def proj_out(l, n):
                ac.wait_ge(S["proj_ps"], CIN * l + n + 1)
                src = pools[n % 3][:, 0:T]
                if n < CA:
                    ins = fn(u[:, n, :], src, ACT.Identity)
                elif n < CA + CR:
                    ins = fn(prow[:, n - CA, 1:T + 1], src, ACT.Identity)
                else:
                    ins = fn(gate[:, n - CA - CR, :], src, ACT.Sigmoid)
                ins.then_inc(S["proj_out"], 1)

            def bu_out(l, j):
                ac.wait_ge(S["bu_ps"], JT * l + j + 1)
                if j >= 4:
                    ac.wait_ge(S["y5_ps"], JT * l + j - 3)
                q = qq[:, 0, JT * l + j:JT * l + j + 1]
                for c in range(2):
                    ins = fn(s5x[:, j % 4, c, :], pools[4 + 2 * (j % 2) + c][:, 0:T], ACT.Identity, scale=q)
                ins.then_inc(S["bu_q"], 1)

            def mix(l):
                if l:
                    norm(2 * l)
                for n in range(CA):
                    proj_out(l, n)
                n = CA
                ac.wait_ge(S["disc_done"], 1)
                for j in range(2):
                    bu_out(l, j)
                    for _ in range(2):
                        proj_out(l, n)
                        n += 1
                for j in range(2, JT):
                    bu_out(l, j)
                    for _ in range(2):
                        if n < CIN:
                            proj_out(l, n)
                            n += 1
                ac.wait_ge(S["z_ready"], l + 1)
                ac.wait_ge(S["shift_out"], 16 * (l + 1))
                fn(z[0:64, 12, :], z[0:64, 12, :], ACT.Tanh)
                fn(z[:, 13, :], z[:, 13, :], ACT.Sigmoid).then_inc(S["lora_in"], 1)
                c0 = PV["k_k"][0]
                for f in range(CB):
                    ins = fn(tmp[0][:, f, :], z[:, 4 + f, :], ACT.Square, scale=pv[:, l, c0 + f:c0 + f + 1])
                ins.then_inc(S["kk_sq"], 1)
                for i in range(3):
                    for f in range(CB):
                        k = 4 * i + f
                        ac.wait_ge(S["lora_ps"], 3 * CB * l + k + 1)
                        src = pools[4 + k % 4][:, 0:T]
                        if i < 2:
                            c0 = PV["w0" if i == 0 else "a0"][0]
                            ins = fn(tmp[1 + i][:, f, :], src, ACT.Sigmoid, bias=pv[:, l, c0 + f:c0 + f + 1])
                        else:
                            ins = fn(gg[:, f, :], src, ACT.Identity)
                        ins.then_inc(S["lora_out"], 1)
                ac.wait_ge(S["kk_ps"], l + 1)
                for f in range(CB):
                    ins = fn(tmp[0][:, f, :], pools[4 + f][:, 0:T], ACT.Sqrt)
                ins.then_inc(S["kk_norm"], 1)
                for aa in range(CA):
                    ac.wait_ge(S["y5_mix"], CA * l + aa + 1)
                    fn(y5[:, aa, :], y5[:, aa, :], ACT.Gelu_apprx_tanh).then_inc(S["y5_done"], 1)
                for n in range(DC):
                    ac.wait_ge(S["glu_ps"], DC * l + n + 1)
                    if n >= 2:
                        ac.wait_ge(S["glu_out"], DC * l + n - 1)
                    fn(glu_s[:, n % 2, :], pools[2 * (n % 2) + 1][:, 0:T], ACT.Sigmoid).then_inc(S["glu_sig"], 1)
                    if n == 3:
                        ac.wait_ge(S["cum_ready"], l + 1)
                        fn(beta, tmp[3], ACT.Exp, scale=math.exp(-0.5))
                        fn(beta_e, chi_e, ACT.Exp, scale=-math.exp(-0.5)).then_inc(S["exps_inverse"], 1)
                fn(kr[:, :, 1, :], tmp[3], ACT.Exp, scale=-math.exp(-0.5))
                fn(kr[:, :, 0, :], tmp[4], ACT.Exp, scale=-math.exp(-0.5)).then_inc(S["exps_ready"], 1)
                for m in range(3):
                    for f0 in range(0, CB, 2):
                        pair(l, m, f0)
                ac.wait_ge(S["o_cent"], l + 1)
                fn(tmp[1], o_t, ACT.Square).then_inc(S["o_sq"], 1)
                ac.wait_ge(S["o_var_ps"], l + 1)
                for f in range(CB):
                    ins = fn(tmp[0][:, f, :], pools[4 + f][:, 0:T], ACT.Sqrt, scale=1.0 / N, bias=eps[:, 1:2])
                ins.then_inc(S["o_std"], 1)

            def pair(l, m, f0):
                t0, nt, chunks = TILES[m]
                n_u = NU * l + CB * m + f0
                w = pair_buffers(l)

                def heads(bank, i, n):
                    return pools[bank + 4 * i][0:nt, 0:n * P].rearrange("p (a t) -> p a t", a=n)

                for i in range(2):
                    ac.wait_ge(S["tr_ps"], n_u + i + 1)
                    ps = pools[4 * i][0:nt, :].rearrange("p (j a k) -> p j a k", j=4, a=2)
                    for j, out in enumerate((w["xk"][0:nt, i, :, 0:N], w["v_tok"][0:nt, i], w["be_tok"][0:nt, i], w["ch_tok"][0:nt, i])):
                        ins = fn(out, ps[:, j], ACT.Identity)
                    ins.then_inc(S["tr_out"], 1)
                for i in range(2):
                    ac.wait_ge(S["sq_ps"], n_u + i + 1)
                    fn(w["a2"][0:nt, i, :, 0:nt], heads(0, i, 4)[:, 0:2, 0:nt], ACT.Identity)
                    fn(w["p2"][0:nt, i, :, 0:nt], heads(0, i, 4)[:, 2:4, 0:nt], ACT.Identity)
                    fn(w["xk"][0:nt, i, :, N:P], pools[1 + 4 * i][0:nt, 0:P].rearrange("p (a k) -> p a k", a=2), ACT.Identity)\
                        .then_inc(S["sq_out"], 1)
                for i in range(2):
                    ac.wait_ge(S["quad_ps"], n_u + i + 1)
                    fn(w["am"][0:nt, i, :, 0:nt], heads(2, i, 4)[:, 0:2, 0:nt], ACT.Identity)
                    fn(w["pm"][0:nt, i, :, 0:nt], heads(2, i, 4)[:, 2:4, 0:nt], ACT.Identity).then_inc(S["act_quad"], 1)
                for i in range(2):
                    ac.wait_ge(S["oct_ps"], n_u + i + 1)
                    fn(w["a2"][0:nt, i, :, 0:nt], heads(1, i, 2)[:, :, 0:nt], ACT.Identity).then_inc(S["act_oct"], 1)
                for i in range(2):
                    ac.wait_ge(S["y_ps"], n_u + i + 1)
                    fn(w["yk"][0:nt, i], heads(0, i, 2), ACT.Identity).then_inc(S["y_out"], 1)
                for i in range(2):
                    ac.wait_ge(S["off_ps"], n_u + i + 1)
                    fn(w["zk"][0:nt, i], heads(3, i, 2), ACT.Identity).then_inc(S["off_out"], 1)
                for i in range(2):
                    f = f0 + i
                    ac.wait_ge(S["ro_ps"], n_u + i + 1)
                    if len(chunks) > 8:
                        fn(hst[:, f, 8, :], pools[4 * i][:, P:P + N], ACT.Identity)
                    fn(ov[:, f, 0:nt], pools[4 * i][:, 0:nt], ACT.Identity).then_inc(S["ov_out"], 1)
                    ac.wait_ge(S["gh_ps"], n_u + i + 1)
                    n = min(8, len(chunks))
                    fn(hst[:, f, 0:n, :], pools[3 + 4 * i][:, 0:n * N].rearrange("p (c v) -> p c v", c=n), ACT.Identity)\
                        .then_inc(S["h_out"], 1)

            def ffn():
                norm(1)
                for q in (slice(0, DC // 2), slice(DC // 2, DC)):
                    ac.wait_ge(S["h_ready"], DC + q.stop)
                    fn(h_hi[:, q], h_f[:, q], ACT.Identity).then_inc(S["h_hi_out"], 1)
                for n in range(S_FUP + S_FDOWN + 2):
                    m = n - 2
                    if 0 <= m < CF:
                        ac.wait_ge(S["up_ps"], m + 1)
                        fn(silu_s[:, m % 2, :], pools[2 * (m % 2)][:, 0:T], ACT.Silu).then_inc(S["up_silu"], 1)
                    if n < S_FUP + S_FDOWN:
                        k = FFN_AT + n
                        ac.wait_ge(slot_in[k % RING], 16 * (k // RING + 1))
                        if m >= CF:
                            ac.wait_ge(S["down_slot"], m - CF + 1)
                        fn(fw_hi[n % 2], slot(k), ACT.Identity).then_inc(S["ffn_hi"], 1)
                    if 0 <= m < CF:
                        ac.wait_ge(S["act_ready"], m + 1)
                        fn(act_hi[:, m, :], act_f[:, m % 2, :], ACT.Identity).then_inc(S["act_hi_out"], 1)

            def routing():
                norm(3)
                for m, (t0, nt, _) in enumerate(TILES):
                    for half in range(2):
                        n = 2 * m + half
                        ac.wait_ge(S["ht_ps"], n + 1)
                        fn(h_tok[0:nt, m, 512 * half:512 * half + 512], pools[4 + n % 4][0:nt, :], ACT.Identity)\
                            .then_inc(S["ht_out"], 1)
                ac.wait_ge(S["gates_in"], 1)
                fn(route[:, 6, :, 0:2], route[:, 5, :, 0:2], ACT.Sigmoid).then_inc(S["gates_out"], 1)

            def gather_out(k, half_):
                ac.wait_ge(S["ga_ps"], k * 2 + (half_ + 1))
                fn(he_hi[:, 4 * half_:4 * half_ + 4, :], pools[7 - half_][:].rearrange("p (c s) -> p c s", c=4),
                   ACT.Identity).then_inc(S["ga_hi"], 1)

            def weights_to_rows(k):
                ac.wait_ge(S["mw_ps"], k + 1)
                fn(mix_w, pools[6][:, 0:T], ACT.Identity).then_inc(S["mw_out"], 1)

            def y_out():
                fn(y_e[:, 0:512], pools[4][:], ACT.Identity)
                fn(y_e[:, 512:1024], pools[5][:], ACT.Identity).then_inc(S["ey_out"], 1)

            def expert(i, k):
                def high(n):
                    ac.wait_ge(slot_in[n % RING], (i * (S_EXPERT // RING) + (S_DENSE // RING + n // RING + 1)) * 16)
                    ac.wait_ge(S["slot_done"], i * S_EXPERT + (n + 1))
                    fn(w_hi[n % SPLIT], slot(n), ACT.Identity).then_inc(S["hi_ready"], 1)

                for n in range(S_EXPERT):
                    if n == 2:
                        y_out()
                        weights_to_rows(k)
                    g = UP_DONE_BY.get(n)
                    if g is not None:
                        silu_out(i, g)
                    high(n)
                    g = TURNED_BY.get(n)
                    if g is not None:
                        turned_out(i, g)
                turned_out(i, NG - 1)
                gather_out(k + 1, 0)
                gather_out(k + 1, 1)
                ac.wait_ge(S["slot_done"], i * S_EXPERT + (SPLIT + S_EXPERT))

            def silu_out(i, g):
                ac.wait_ge(S["slot_done"], i * S_EXPERT + (SPLIT + SLOT_OF["w3", g] + 1))
                fn(sil_e[:, g % 2, :], pools[g % 2][:, 0:FW], ACT.Silu).then_inc(S["eup_silu"], 1)

            def turned_out(i, g):
                ac.wait_ge(S["et_ps"], i * NG + (g + 1))
                fn(at_hi[:, g % 2, :], pools[2 + g % 2][:, 0:2 * P], ACT.Identity).then_inc(S["et_hi"], 1)

            def one_pass(i0, k0):
                gather_out(k0, 0)
                gather_out(k0, 1)
                with ac.Fori(0, E) as e:
                    expert(e + i0, e + k0)
                y_out()
                weights_to_rows(k0 + E)

            def experts():
                for _ in range(SPLIT):
                    nc.scalar.nop().then_inc(S["slot_done"], 1)
                ac.wait_ge(S["count_out"], 1)
                one_pass(0, 0)
                ac.wait_ge(S["n_ready"], 1)
                npass = ac.value_load(n_int[0:1, 0:1], min_val=1, max_val=3)
                with ac.If(npass > 1):
                    with ac.Fori(1, npass) as p:
                        one_pass(p * E, p * (E + 1))

            ac.wait_ge(S["first_in"], N_FIRST)
            norm(0)
            fn(small[:, 2, :], lam[:, 2, :], ACT.Exp).then_inc(S["disc_exp1"], 1)
            ac.wait_ge(S["disc_ang"], 1)
            fn(small[:, 3, :], small[:, 4, :], ACT.Exp)
            fn(small[:, 5:7, :], small[:, 7:9, :], ACT.Sin).then_inc(S["disc_exp2"], 1)
            mix(0)
            ffn()
            mix(1)
            routing()
            experts()
            norm(4)

        @block.vector
        def _(dve):
            steps = [0]
            v = nc.vector

            def step(ins):
                steps[0] += 1
                ins.then_inc(S["dve_step"], 1)
                dve.wait_ge(S["dve_step"], steps[0])

            def col(l, name, i):
                c0 = PV[name][0]
                return pv[:, l, c0 + i:c0 + i + 1]

            def norm(i, gains, out):
                dve.wait_ge(S["norm_rt"], i + 1)
                step(v.reciprocal(rstd[:, 1, :], rstd[:, 0, :]))
                for c in range(DC):
                    ins = v.scalar_tensor_tensor(out=out[:, c, :], in0=x[:, c, :], scalar=gains[:, c:c + 1],
                                                 in1=rstd[:, 1, :], op0=ALU.mult, op1=ALU.mult)
                    ins.then_inc(S["h_ready"], 1)

            def discretise():
                s = lambda i: small[:, i, :]
                lr, li = lam[:, 0, :], lam[:, 1, :]
                tt, ts = v.tensor_tensor, v.tensor_scalar
                dve.wait_ge(S["disc_exp1"], 1)
                step(tt(s(4), lr, s(2), ALU.mult))
                step(tt(s(9), li, s(2), ALU.mult))
                step(ts(s(10), s(9), 1 / TWO_PI, ROUND, ALU.mult, ALU.add))
                step(ts(s(10), s(10), ROUND, None, ALU.subtract))
                for c in (C1, C2, C3):
                    step(v.scalar_tensor_tensor(out=s(9), in0=s(10), scalar=-c, in1=s(9), op0=ALU.mult, op1=ALU.add))
                step(ts(s(7), s(9), -PI_IN, PI_IN, ALU.max, ALU.min))
                step(ts(s(10), s(9), math.pi / 2, None, ALU.add))
                step(ts(s(11), s(10), math.pi, -TWO_PI, ALU.is_gt, ALU.mult))
                step(tt(s(10), s(10), s(11), ALU.add))
                ts(s(8), s(10), -PI_IN, PI_IN, ALU.max, ALU.min).then_inc(S["disc_ang"], 1)
                dve.wait_ge(S["disc_exp2"], 1)
                ar_, ai_, na = apow[:, 0, 0, :], apow[:, 0, 1, :], apow[:, 0, 2, :]
                step(tt(ar_, s(3), s(6), ALU.mult))
                step(tt(ai_, s(3), s(5), ALU.mult))
                step(tt(s(12), lr, lr, ALU.mult))
                step(tt(s(13), li, li, ALU.mult))
                step(tt(s(12), s(12), s(13), ALU.add))
                step(v.reciprocal(s(12), s(12)))
                step(ts(s(13), ar_, 1.0, None, ALU.subtract))
                step(tt(s(14), s(13), lr, ALU.mult))
                step(tt(s(15), ai_, li, ALU.mult))
                step(tt(s(14), s(14), s(15), ALU.add))
                step(tt(qq[:, 0, :], s(14), s(12), ALU.mult))
                step(tt(s(14), ai_, lr, ALU.mult))
                step(tt(s(15), s(13), li, ALU.mult))
                step(tt(s(14), s(14), s(15), ALU.subtract))
                step(tt(qq[:, 1, :], s(14), s(12), ALU.mult))
                step(ts(qq[:, 2, :], qq[:, 1, :], -1.0, None, ALU.mult))
                step(ts(na, ai_, -1.0, None, ALU.mult))
                for k in range(1, LEVELS):
                    br, bi, bn = (apow[:, k - 1, i, :] for i in range(3))
                    step(tt(s(14), br, br, ALU.mult))
                    step(tt(s(15), bi, bi, ALU.mult))
                    step(tt(apow[:, k, 0, :], s(14), s(15), ALU.subtract))
                    step(tt(s(14), br, bi, ALU.mult))
                    step(ts(apow[:, k, 1, :], s(14), 2.0, None, ALU.mult))
                    step(ts(apow[:, k, 2, :], s(14), -2.0, None, ALU.mult))
                dve.wait_ge(S["consts"], N_CONST)
                for l in range(DEPTH):
                    def ab(i):
                        return apow[:, 0, i, JT * l:JT * (l + 1)].unsqueeze(2).broadcast_to([P, JT, NS])
                    tt(axt[:, 0], x0[:, l, 1], ab(2), ALU.mult)
                    step(tt(axt[:, 1], x0[:, l, 0], ab(1), ALU.mult))
                    for c in range(2):
                        step(tt(x0[:, l, c], x0[:, l, c], ab(0), ALU.mult))
                    step(tt(x0[:, l], x0[:, l], axt[:], ALU.add))
                v.nop().then_inc(S["disc_done"], 1)

            def scan_pair(l, j0):
                stt = v.scalar_tensor_tensor
                X = [s5x[:, (j0 + i) % 4] for i in range(2)]
                for i in range(2):
                    k_ = JT * l + j0 + i
                    dve.wait_ge(S["bu_q"], k_ + 1)
                    stt(out=X[i][:, 0, :], in0=pools[4 + 2 * i + 1][:, 0:T], scalar=qq[:, 2, k_:k_ + 1],
                        in1=X[i][:, 0, :], op0=ALU.mult, op1=ALU.add)
                    stt(out=X[i][:, 1, :], in0=pools[4 + 2 * i][:, 0:T], scalar=qq[:, 1, k_:k_ + 1],
                        in1=X[i][:, 1, :], op0=ALU.mult, op1=ALU.add).then_inc(S["bu_used"], 1)
                dve.wait_ge(S["bu_used"], JT * l + j0 + 2)
                for i in range(2):
                    v.tensor_tensor(X[i][:, :, TP:T], X[i][:, :, TP:T], x0[:, l, :, j0 + i, :], ALU.add)
                levels = []
                for k in range(LEVELS):
                    d = 1 << k
                    if 2 * d <= TP:
                        levels.append((k, d - 1, 2 * d - 1, TP // (2 * d)))
                for k in reversed(range(LEVELS)):
                    d = 1 << k
                    n = (TP - 3 * d) // (2 * d) + 1 if TP >= 3 * d else 0
                    if n:
                        levels.append((k, 2 * d - 1, 3 * d - 1, n))
                done = [0, 0]
                for k, src, dst, n in levels:
                    w = 2 << k
                    end = lambda at: at + w * (n - 1) + 1
                    for i in range(2):
                        if done[i]:
                            dve.wait_ge(S["dve_step"], done[i])
                        k_ = JT * l + j0 + i
                        stt(out=X[i][:, :, dst:end(dst):w], in0=X[i][:, :, src:end(src):w], scalar=apow[:, k, 0, k_:k_ + 1],
                            in1=X[i][:, :, dst:end(dst):w], op0=ALU.mult, op1=ALU.add).then_inc(S["dve_step"], 1)
                        steps[0] += 1
                        done[i] = steps[0]
                    for i in range(2):
                        k_ = JT * l + j0 + i
                        dve.wait_ge(S["dve_step"], done[i])
                        for c in range(2):
                            ins = stt(out=X[i][:, c, dst:end(dst):w], in0=X[i][:, 1 - c, src:end(src):w],
                                      scalar=apow[:, k, 2 - c, k_:k_ + 1], in1=X[i][:, c, dst:end(dst):w],
                                      op0=ALU.mult, op1=ALU.add)
                        ins.then_inc(S["dve_step"], 1)
                        steps[0] += 1
                        done[i] = steps[0]
                dve.wait_ge(S["dve_step"], steps[0])
                if l and j0 == 0:
                    dve.wait_ge(S["s5_out"], 16 * l)
                for i in range(2):
                    v.tensor_copy(s5out[:, j0 + i], X[i][:, :, TP - 1:T]).then_inc(S["scan_done"], 1)

            def y5_add(l, aa):
                dve.wait_ge(S["y5_ps"], JT * l + 4 * aa + 4)
                v.scalar_tensor_tensor(out=y5[:, aa, :], in0=u[:, aa, :], scalar=col(l, "d", aa),
                                       in1=pools[3][:, 0:T], op0=ALU.mult, op1=ALU.add).then_inc(S["y5_mix"], 1)

            def mix(l):
                tt, ts, stt = v.tensor_tensor, v.tensor_scalar, v.scalar_tensor_tensor
                if l:
                    norm(2 * l, pv[:, l, PV["norm_mix"][0]:PV["norm_mix"][0] + DC], h)
                v.memset(prow[:, :, 0:1], 0.0).then_inc(S["pad_zero"], 1)
                dve.wait_ge(S["small_w"], 48 * (l + 1))
                step(ts(s5_c[:, :, 1, :], s5_c[:, :, 1, :], -1.0, None, ALU.mult))
                for j in range(0, JT, 2):
                    scan_pair(l, j)
                    if j >= 6 and j % 4 == 2:
                        y5_add(l, j // 4 - 1)
                y5_add(l, CA - 1)

                def glu_out(*tiles):
                    for n in tiles:
                        dve.wait_ge(S["glu_sig"], DC * l + n + 1)
                        step(tt(gate[:, n, :], gate[:, n, :], glu_s[:, n % 2, :], ALU.mult))
                        tt(gate[:, n, :], gate[:, n, :], pools[2 * (n % 2)][:, 0:T], ALU.mult).then_inc(S["glu_out"], 1)

                dve.wait_ge(S["lora_out"], 3 * CB * (l + 1))
                for f in range(CB):
                    ins = v.tensor_tensor_scan(tmp[3][:, f, :], keep[:], tmp[1][:, f, :], 0.0, ALU.mult, ALU.add)
                step(ins)
                tt(tmp[4], tmp[3], tmp[1], ALU.subtract)
                full = TP // CH
                cv = tmp[3][:, :, 0:full * CH].rearrange("p a (c t) -> p a c t", t=CH)
                for f in range(CB):
                    tt(chi_e[:, f, 0:full * CH].rearrange("p (c t) -> p c t", t=CH),
                       cv[:, f, :, CH - 1:CH].broadcast_to([P, full, CH]), cv[:, f], ALU.subtract)
                tt(chi_e[:, :, full * CH:TP], tmp[3][:, :, TP - 1:TP].broadcast_to([P, CB, TP - full * CH]),
                   tmp[3][:, :, full * CH:TP], ALU.subtract)
                v.memset(chi_e[:, :, TP:T], 0.0).then_inc(S["cum_ready"], 1)
                dve.wait_ge(S["kk_norm"], l + 1)
                step(ts(tmp[0], tmp[0], 1e-12, None, ALU.max))
                glu_out(0)
                for f in range(CB):
                    ins = v.reciprocal(tmp[0][:, f, :], tmp[0][:, f, :])
                    if f < CB - 1:
                        glu_out(f + 1)
                step(ins)
                dve.wait_ge(S["kk_out"], l + 1)
                kk, kp = tmp[0], z[:, 4:8, :]
                step(tt(kk, chi, tmp[0], ALU.mult))
                dve.wait_ge(S["bonus_in"], l + 1)
                step(tt(tmp[2], tmp[2], kk, ALU.mult))
                glu_out(4)
                dve.wait_ge(S["exps_inverse"], l + 1)
                tt(chi, beta, kp, ALU.mult)
                glu_out(5)
                step(tt(chi_e, beta_e, kp, ALU.mult))
                glu_out(6)
                tt(beta, beta, tmp[2], ALU.mult)
                glu_out(7)
                tt(beta_e, beta_e, tmp[2], ALU.mult)
                dve.wait_ge(S["exps_ready"], l + 1)
                for f in range(CB):
                    v.tensor_copy(wend[:, f, 0:full], kr[:, f, 1, CH - 1:full * CH:CH])
                v.tensor_copy(wend[:, :, full:full + 1 + NS], kr[:, :, 1, TP - 1:T])
                step(tt(kr[:, :, 0, :], kr[:, :, 0, :], kk, ALU.mult))
                tt(kr[:, :, 1, :], kr[:, :, 1, :], z[:, 0:4, :], ALU.mult)
                v.memset(zcar, 0.0).then_inc(S["z_out"], 1)
                dve.wait_ge(S["bonus_ps"], l + 1)
                for f in range(CB):
                    ins = tt(bonus[:, f, :], z[:, 8 + f, :], pools[4 + f][:, 0:T], ALU.mult)
                ins.then_inc(S["fm_ready"], 1)
                dve.wait_ge(S["fm_ready"], l + 1)
                for m in range(3):
                    for f0 in range(0, CB, 2):
                        pair(l, m, f0)
                    chain(l, m)
                dve.wait_ge(S["o_mean_ps"], l + 1)
                for f in range(CB):
                    ins = stt(out=o_t[:, f, :], in0=pools[f][:, 0:T], scalar=-1.0 / N, in1=o_t[:, f, :],
                              op0=ALU.mult, op1=ALU.add)
                ins.then_inc(S["o_cent"], 1)
                dve.wait_ge(S["o_std"], l + 1)
                dve.wait_ge(S["o_cent"], l + 1)
                step(v.reciprocal(tmp[0], tmp[0]))
                step(tt(o_t, o_t, tmp[0], ALU.mult))
                for f in range(CB):
                    ins = ts(o_t[:, f, :], o_t[:, f, :], col(l, "gn_g", f), col(l, "gn_b", f), ALU.mult, ALU.add)
                step(ins)
                step(tt(o_t, o_t, bonus, ALU.add))
                tt(o_t, o_t, gg, ALU.mult).then_inc(S["o_ready"], 1)
                for n in range(DC):
                    dve.wait_ge(S["bo_ps"], DC * l + n + 1)
                    step(tt(gate[:, DC + n, :], gate[:, DC + n, :], pools[n % 4][:, 0:T], ALU.mult))
                    tt(gate[:, n, :], gate[:, n, :], gate[:, DC + n, :], ALU.add).then_inc(S["bo_out"], 1)
                for n in range(DC):
                    dve.wait_ge(S["wo_ps"], DC * l + n + 1)
                    tt(x[:, n, :], x[:, n, :], pools[4 + n % 4][:, 0:T], ALU.add).then_inc(S["wo_out"], 1)
                dve.wait_ge(S["wo_out"], DC * (l + 1))
                v.nop().then_inc(S["x_ready"], 1)

            def pair(l, m, f0):
                tt, ts = v.tensor_tensor, v.tensor_scalar
                t0, nt, chunks = TILES[m]
                ncn = len(chunks)
                n_p = PAIRS * l + 2 * m + f0 // 2
                n_u = 2 * n_p
                mk = masks[:] if m < 2 else masks_s[:]
                sc = sel_c[:] if m < 2 else sel_s[:]
                w = pair_buffers(l)

                def masked(out, bank, c, mask):
                    for par in range(2):
                        if c is None:
                            src = pools[bank + 4 * par][0:nt, 0:2 * P].rearrange("p (i t) -> p i t", i=2)
                        else:
                            src = pools[bank + 4 * par][0:nt, :].rearrange("p (i c t) -> p i c t", i=2, c=2)[:, :, c]
                        ins_ = tt(out[0:nt, :, par, 0:nt], src[:, :, 0:nt],
                                  mk[:, mask].unsqueeze(1).broadcast_to([nt, 2, nt]), ALU.mult)
                    return ins_

                dve.wait_ge(S["gram_a_ps"], n_p + 1)
                masked(w["am"], 1, None, 0)
                dve.wait_ge(S["gram_b_ps"], n_p + 1)
                masked(w["pm"], 2, 0, 1)
                dve.wait_ge(S["gram_c_ps"], n_p + 1)
                masked(w["akt"], 3, 0, 3).then_inc(S["gram_out"], 1)
                dve.wait_ge(S["gram_out"], n_p + 1)
                for i in range(2):
                    tt(w["e1"][0:nt, i, :, 0:nt], ident[0:nt, 0:nt].unsqueeze(1).broadcast_to([nt, 2, nt]),
                       w["pm"][0:nt, i, :, 0:nt], ALU.subtract)
                masked(w["poff"], 2, 0, 2)
                masked(w["mbt"], 2, 1, 4)
                masked(w["mkt"], 3, 1, 4).then_inc(S["gram_rest_out"], 1)

                def chunked(out, src, i, sign):
                    for par in range(2):
                        tt(out[0:nt, i, par, 0:ncn, :], src[0:nt, i, par, :].unsqueeze(1).broadcast_to([nt, ncn, N]),
                           sc[:, sign].unsqueeze(2).broadcast_to([nt, ncn, N]), ALU.mult)

                def inverse(out, in_, bank, i):
                    return tt(out[0:nt, i, :, 0:nt], in_[0:nt, i, :, 0:nt],
                              pools[bank + 4 * i][0:nt, 0:2 * P].rearrange("p (a t) -> p a t", a=2)[:, :, 0:nt], ALU.add)

                for i in range(2):
                    dve.wait_ge(S["tr_out"], n_u + i + 1)
                    chunked(v_bd, w["v_tok"], i, 0)
                dve.wait_ge(S["gram_rest_out"], n_p + 1)
                for i in range(2):
                    dve.wait_ge(S["quad_ps"], n_u + i + 1)
                    dve.wait_ge(S["act_quad"], n_u + i + 1)
                    inverse(w["e2"], w["e1"], 3, i).then_inc(S["quad_out"], 1)
                chunked(be_bd, w["be_tok"], 0, 0)
                for i in range(2):
                    dve.wait_ge(S["quad_out"], n_u + i + 1)
                    dve.wait_ge(S["oct_ps"], n_u + i + 1)
                    dve.wait_ge(S["act_oct"], n_u + i + 1)
                    inverse(w["e1"], w["e2"], 0, i).then_inc(S["oct_out"], 1)
                for i in range(2):
                    dve.wait_ge(S["oct_out"], n_u + i + 1)
                    dve.wait_ge(S["e8_ps"], n_u + i + 1)
                    inverse(w["e2"], w["e1"], 2, i).then_inc(S["e8_out"], 1)
                chunked(be_bd, w["be_tok"], 1, 0)
                w0 = 4 * m
                for i in range(2):
                    for par in range(2):
                        q = slice(64 * par, 64 * par + 64)
                        tt(gpre[q, f0 + i, 0:ncn, :], ident[q, q].unsqueeze(1).broadcast_to([64, ncn, N]),
                           wend[q, f0 + i, w0:w0 + ncn].unsqueeze(2).broadcast_to([64, ncn, N]), ALU.mult)
                for i in range(2):
                    dve.wait_ge(S["fix_ps"], n_u + i + 1)
                    dve.wait_ge(S["y_out"], n_u + i + 1)
                    step(tt(w["xk"][0:nt, i], w["yk"][0:nt, i], pools[1 + 4 * i][0:nt, 0:2 * P].rearrange("p (a t) -> p a t", a=2),
                            ALU.subtract))
                    chunked(nx_bd, w["xk"][:, :, :, N:P], i, 1)
                    ts(w["zk"][0:nt, i, :, 0:N], w["xk"][0:nt, i, :, N:P], -1.0, None, ALU.mult).then_inc(S["x_out"], 1)
                for i in range(2):
                    f = f0 + i
                    dve.wait_ge(S["ro_ps"], n_u + i + 1)
                    if ncn > 8:
                        tt(gpre[:, f, 8, :], gpre[:, f, 8, :], pools[1 + 4 * i][:, P:P + N], ALU.subtract)
                    tt(rt[:, f, 0:nt], kr[:, f, 1, t0:t0 + nt], pools[1 + 4 * i][:, 0:nt], ALU.subtract).then_inc(S["ro_out"], 1)
                    dve.wait_ge(S["gh_ps"], n_u + i + 1)
                    n = min(8, ncn)
                    tt(gpre[:, f, 0:n, :], gpre[:, f, 0:n, :],
                       pools[2 + 4 * i][:, 0:n * N].rearrange("p (c v) -> p c v", c=n), ALU.subtract).then_inc(S["gh_out"], 1)

            def chain(l, m):
                tt = v.tensor_tensor
                t0, nt, chunks = TILES[m]
                dve.wait_ge(S["h_out"], NU * l + CB * (m + 1))
                dve.wait_ge(S["ov_out"], NU * l + CB * (m + 1))
                seq = 4 if m < 2 else 1
                for c in range(seq):
                    n_c = 9 * l + 4 * m + c
                    dve.wait_ge(S["z_ps"], n_c + 1)
                    for par in range(2):
                        q = slice(64 * par, 64 * par + 64)
                        ins = tt(hst[q, :, c, :], hst[q, :, c, :],
                                 pools[par][q, 0:CB * N].rearrange("p (f v) -> p f v", f=CB), ALU.add)
                    ins.then_inc(S["z_out"], 1)
                if m == 2:
                    for n in range(H):
                        f, par = n // 2, n % 2
                        q = slice(64 * par, 64 * par + 64)
                        dve.wait_ge(S["zs_ps"], H * l + n + 1)
                        tt(hst[q, f, 1:9, :], hst[q, f, 1:9, :],
                           pools[2 + par][q, :].rearrange("p (b v) -> p b v", b=NS), ALU.add).then_inc(S["zs_out"], 1)
                for n in range(H):
                    f, par = n // 2, n % 2
                    q = slice(64 * par, 64 * par + 64)
                    k = H * (3 * l + m) + n
                    dve.wait_ge(S["o_ps"], k + 1)
                    tt(o_t[q, f, t0:t0 + nt], ov[q, f, 0:nt], pools[4 + par][q, 0:nt], ALU.add).then_inc(S["o_out"], 1)
                if m < 2:
                    dve.wait_ge(S["z_out"], 9 * l + 4 * (m + 1) + l + 1)
                    v.tensor_copy(zcar, hst[:, :, 3, :]).then_inc(S["zcar_out"], 1)

            def ffn():
                dve.wait_ge(S["rw_out"], 16)
                norm(1, pv[:, 0, PV["norm_ffn"][0]:PV["norm_ffn"][0] + DC], h_f)
                dve.wait_ge(S["h_ready"], 2 * DC)
                for i, q in enumerate((slice(0, DC // 2), slice(DC // 2, DC))):
                    dve.wait_ge(S["h_hi_out"], i + 1)
                    v.tensor_tensor(h_lo[:, q], h_f[:, q], h_hi[:, q].bitcast(F32), ALU.subtract).then_inc(S["h_split"], 1)
                added = 0
                for n in range(S_FUP + S_FDOWN + 2):
                    m = n - 2
                    if 0 <= m < CF:
                        dve.wait_ge(S["up_silu"], m + 1)
                        v.tensor_tensor(act_f[:, m % 2, :], silu_s[:, m % 2, :], pools[2 * (m % 2) + 1][:, 0:T], ALU.mult)\
                            .then_inc(S["act_ready"], 1)
                    while added < DC and (added + 1) * CF <= 16 * (n - 1 - CF):
                        dve.wait_ge(S["down_ps"], added + 1)
                        v.tensor_tensor(x[:, added, :], x[:, added, :], pools[4 + added % 4][:, 0:T], ALU.add)\
                            .then_inc(S["down_out"], 1)
                        added += 1
                    if n < S_FUP + S_FDOWN:
                        dve.wait_ge(S["ffn_hi"], n + 1)
                        v.tensor_tensor(fw_lo[n % 2], slot(FFN_AT + n), fw_hi[n % 2].bitcast(F32), ALU.subtract)\
                            .then_inc(S["weights_used"], 1)
                    if 0 <= m < CF:
                        dve.wait_ge(S["act_hi_out"], m + 1)
                        dve.wait_ge(S["act_ready"], m + 1)
                        v.tensor_tensor(act_lo[:, m, :], act_f[:, m % 2, :], act_hi[:, m, :].bitcast(F32), ALU.subtract)\
                            .then_inc(S["act_split"], 1)
                dve.wait_ge(S["down_out"], DC)
                v.nop().then_inc(S["x_ready"], 1)

            def routing():
                tt, ts, stt = v.tensor_tensor, v.tensor_scalar, v.scalar_tensor_tensor
                step(v.memset(route, 0.0))
                dve.wait_ge(S["rw_out"], 32)
                norm(3, pv[:, 1, PV["norm_ffn"][0]:PV["norm_ffn"][0] + DC], h)
                dve.wait_ge(S["logit_ps"], 1)
                for m, (t0, nt, _) in enumerate(TILES):
                    step(v.tensor_copy(route[0:nt, 2, m, :], pools[1][0:nt, m * E:(m + 1) * E]))
                for m in range(3):
                    step(v.max(route[:, 3, m, :], route[:, 2, m, :]))
                    step(v.max_index(top_i[:, m, :], route[:, 3, m, :], route[:, 2, m, :]))
                step(v.tensor_copy(route[:, 4], top_i[:]))
                step(tt(route[:, 5, :, 0:1], route[:, 3, :, 0:1], route[:, 3, :, 1:2], ALU.subtract))
                tt(route[:, 5, :, 1:2], route[:, 3, :, 1:2], route[:, 3, :, 0:1], ALU.subtract).then_inc(S["gates_in"], 1)
                for m in range(3):
                    for i in range(2):
                        step(ts(route[:, 7 + i, m, :], iota[:, 0:E], route[:, 4, m, i:i + 1], None, ALU.is_equal))
                dve.wait_ge(S["gates_out"], 1)
                step(v.memset(ar(18124, 90), 0.0))
                for m, (t0, nt, _) in enumerate(TILES):
                    step(tt(chosen[0:nt, m, 1:E + 1], route[0:nt, 7, m, :], route[0:nt, 8, m, :], ALU.add))
                    for i in range(2):
                        step(ts(route[:, 7 + i, m, :], route[:, 7 + i, m, :], route[:, 6, m, i:i + 1], None, ALU.mult))
                    step(tt(weight[0:nt, m, 1:E + 1], route[0:nt, 7, m, :], route[0:nt, 8, m, :], ALU.add))
                v.nop().then_inc(S["count_in"], 1)
                dve.wait_ge(S["count_ps"], 1)
                for m, (t0, nt, _) in enumerate(TILES):
                    step(v.tensor_copy(place[0:nt, m, 1:E + 1], pools[2][0:nt, m * E:(m + 1) * E]))
                step(v.tensor_reduce(route[:, 11, 0, 0:1], pools[2][:, 3 * E:4 * E], AX.X, ALU.max))
                step(ts(route[:, 11, 0, 1:2], route[:, 11, 0, 0:1], CAP + 0.5, 1.0, ALU.is_gt, ALU.add))
                step(ts(route[:, 11, 0, 2:3], route[:, 11, 0, 0:1], 2 * CAP + 0.5, None, ALU.is_gt))
                step(tt(route[:, 11, 0, 1:2], route[:, 11, 0, 1:2], route[:, 11, 0, 2:3], ALU.add))
                v.tensor_copy(n_int[:], route[:, 11, 0, 1:2]).then_inc(S["n_ready"], 1)
                step(v.memset(y_e, 0.0))
                v.nop().then_inc(S["count_out"], 1)

            def select(e, table, out):
                for m, (t0, nt, _) in enumerate(TILES):
                    ins = v.tensor_scalar(out[0:nt, m, :], iota[0:nt], place[0:nt, m, bass.ds(e, 1)],
                                          table[0:nt, m, bass.ds(e, 1)], ALU.is_equal, ALU.mult)
                return ins

            def gather_out(k, half_):
                dve.wait_ge(S["ga_hi"], k * 2 + (half_ + 1))
                q = slice(4 * half_, 4 * half_ + 4)
                v.tensor_tensor(he_lo[:, q, :], pools[7 - half_][:].rearrange("p (c s) -> p c s", c=4),
                                he_hi[:, q, :].bitcast(F32), ALU.subtract).then_inc(S["ga_lo"], 1)

            def act_out(i, g):
                dve.wait_ge(S["eup_silu"], i * NG + (g + 1))
                v.tensor_tensor(act_e[:, g % 2, :], sil_e[:, g % 2, :], pools[g % 2][:, FW:2 * FW], ALU.mult)\
                    .then_inc(S["eup_act"], 1)

            def turned_out(i, g):
                dve.wait_ge(S["et_hi"], i * NG + (g + 1))
                v.tensor_tensor(at_lo[:, g % 2, :], pools[2 + g % 2][:, 0:2 * P], at_hi[:, g % 2, :].bitcast(F32),
                                ALU.subtract).then_inc(S["et_lo"], 1)

            def combine_out(k):
                for c in range(DC):
                    dve.wait_ge(S["em_ps"], k * DC + (c + 1))
                    v.tensor_tensor(x[:, c, :], x[:, c, :], pools[6 + c % 2][:, 0:T], ALU.add).then_inc(S["em_out"], 1)

            def expert(e, i, k):
                def low(n):
                    dve.wait_ge(S["hi_ready"], i * S_EXPERT + (n + 1))
                    v.tensor_tensor(w_lo[n % SPLIT], slot(n), w_hi[n % SPLIT].bitcast(F32), ALU.subtract)\
                        .then_inc(S["weights_used"], 1)

                for n in range(S_EXPERT):
                    if n == 1:
                        select(e, weight, sel_w).then_inc(S["selw_ready"], 1)
                    if n == 3:
                        combine_out(k)
                    g = UP_DONE_BY.get(n)
                    if g is not None:
                        act_out(i, g)
                    low(n)
                    g = TURNED_BY.get(n)
                    if g is not None:
                        turned_out(i, g)
                    if n == S_EXPERT - 8:
                        select(e + 2, chosen, sel_p).then_inc(S["selp_ready"], 1)
                turned_out(i, NG - 1)
                gather_out(k + 1, 0)
                gather_out(k + 1, 1)

            def one_pass(p, i0, k0):
                select(1, chosen, sel_p).then_inc(S["selp_ready"], 1)
                gather_out(k0, 0)
                gather_out(k0, 1)
                with dve.Fori(0, E) as e:
                    expert(e, e + i0, e + k0)
                select(E, weight, sel_w).then_inc(S["selw_ready"], 1)
                combine_out(k0 + E)

            def experts():
                one_pass(0, 0, 0)
                npass = dve.value_load(n_int[0:1, 0:1], min_val=1, max_val=3)
                with dve.If(npass > 1):
                    with dve.Fori(1, npass) as p:
                        v.tensor_scalar(place, place, float(CAP), None, ALU.subtract).then_inc(S["place_moved"], 1)
                        dve.wait_ge(S["place_moved"], p)
                        one_pass(p, p * E, p * (E + 1))
                dve.wait_ge(S["em_out"], npass * (DC * (E + 1)))
                v.nop().then_inc(S["x_ready"], 1)

            dve.wait_ge(S["first_in"], N_FIRST)
            norm(0, pv[:, 0, PV["norm_mix"][0]:PV["norm_mix"][0] + DC], h)
            discretise()
            mix(0)
            ffn()
            mix(1)
            routing()
            experts()
            norm(4, nfin[:], h)
            dve.wait_ge(S["h_ready"], 5 * DC)
            v.nop().then_inc(S["final_out"], 1)


def _constants():
    c = {"ones": np.ones((P, P)), "ident": np.eye(P), "iota": np.tile(np.arange(P), (P, 1)),
         "before": np.triu(np.ones((P, P)), 1)}
    i = np.arange(P)
    c["blk"] = (i[:, None] // N == i[None, :] // N) * 1.0

    def masks(chunk, half, r):
        same = chunk[:, None] == chunk[None, :]
        low, up = r[:, None] > r[None, :], r[:, None] < r[None, :]
        half_same = half[:, None] == half[None, :]
        return np.stack([same & half_same & low, same & half_same & up, same & ~half_same & up,
                         same & up, same & (r[:, None] <= r[None, :])], 1) * 1.0

    c["masks"] = masks(i // CH, i // 16, i)
    r = np.arange(TILES[2][1])
    chunk = np.where(r < 16, 0, r - 15)
    c["masks_s"] = masks(chunk, chunk, r)
    s = (i[:, None] // CH == np.arange(4)[None, :]) * 1.0
    c["sel_c"] = np.stack([s, -s], 1)
    s = (chunk[:, None] == np.arange(MAXC)[None, :]) * 1.0
    c["sel_s"] = np.stack([s, -s], 1)
    t = np.arange(T)
    c["keep"] = np.tile(((t % CH != 0) & (t < TP)) * 1.0, (P, 1))
    c["eps"] = np.tile(np.array([EPS_RMS, EPS_GN]), (P, 1))
    return {k: np.ascontiguousarray(v, dtype=np.float32) for k, v in c.items()}


def _cols(v):
    v = v.reshape(v.shape[:-1] + (-1, P))
    return np.moveaxis(v, -1, 0)


def _slot(parts):
    out = np.zeros((P, SLOT), np.float32)
    at = 0
    for w in parts:
        w = w.reshape(P, -1)
        out[:, at:at + w.shape[1]] = w
        at += w.shape[1]
    return out


def _tile(w, n):
    return w[:, n * P:(n + 1) * P].reshape(-1, P, P).transpose(1, 0, 2)


def _stream(i):
    slots = []
    for l in range(DEPTH):
        n = 0
        for k in WIN_TILES:
            slots.append(_slot([_tile(i["w_in"][l], n + j) for j in range(k)]))
            n += k
        for n in range(0, DC, 2):
            slots.append(_slot([_tile(i[w][l], n + j) for j in range(2) for w in ("s5_glu1", "s5_glu2")]))
        for n in range(0, DC, 4):
            slots.append(_slot([_tile(i["rw_w_bo"][l], n + j) for j in range(4)]))
        for n in range(0, DC, 2):
            slots.append(_slot([_tile(i["w_out"][l], n + j) for j in range(2)]))
        if l == 0:
            for n in range(CF):
                slots.append(_slot([_tile(i[w][0], n) for w in ("ffn_w1", "ffn_w3")]))
            blocks = [_tile(i["ffn_w2"][0], n)[:, k] for n in range(DC) for k in range(CF)]
            for b in range(0, len(blocks), 16):
                slots.append(_slot(blocks[b:b + 16]))
    slots = np.stack(slots)
    assert slots.shape[0] == S_DENSE
    up = [i[w][0].reshape(E, DC, P, NG, FW).transpose(0, 3, 2, 1, 4).reshape(E, NG, P, SLOT) for w in ("moe_w1", "moe_w3")]
    down = i["moe_w2"][0].reshape(E, NG, 2, P, D).transpose(0, 1, 3, 2, 4).reshape(E, NG, P, SLOT)
    experts = np.empty((E, S_EXPERT, P, SLOT), np.float32)
    parts = {"w1": up[0], "w3": up[1], "w2": down}
    for n, (kind, g) in enumerate(ORDER):
        experts[:, n] = parts[kind][:, g]
    return np.concatenate([slots, experts.reshape(E * S_EXPERT, P, SLOT)])


def layout(inputs):
    i = {k: np.asarray(v) for k, v in inputs.items()}
    a = _constants()
    a["wstream"] = _stream(i)
    a["x"] = _cols(np.concatenate([i["meta_tokens"], i["x_prompt"][0], i["x_sample"][:, 0]])).transpose(0, 2, 1)
    names = {"norm_mix": "norm_mix", "norm_ffn": "norm_ffn", "d": "s5_d", "mu": "rw_mu", "w0": "rw_w0", "a0": "rw_a0",
             "k_k": "rw_k_k", "k_a": "rw_k_a", "r_k": "rw_r_k", "gn_g": "rw_gn_g", "gn_b": "rw_gn_b"}
    a["pv"] = np.concatenate([_cols(i[names[k]].reshape(DEPTH, -1)) for k in PV], 2)
    a["nfin"] = _cols(i["norm_final"])

    def states(v):
        return _cols(v.reshape(DEPTH, G5 * S5P)).reshape(P, DEPTH * JT)

    a["lam"] = np.stack([states(i["s5_lam_re"]), states(i["s5_lam_im"]),
                         states(np.repeat(i["s5_log_dt"][:, :, None], S5P, 2))], 1)
    a["x0"] = np.stack([_cols(i[k].reshape(DEPTH, NS, -1)).transpose(0, 1, 3, 2) for k in ("state_s5_re", "state_s5_im")], 2)
    a["s0"] = i["state_rwkv"].reshape(DEPTH, NS, CB, 2, N, N).transpose(0, 3, 5, 2, 1, 4).reshape(DEPTH, P, CB, NS, N)
    a["shift0"] = _cols(i["state_shift"]).transpose(0, 1, 3, 2)
    a["router"] = i["moe_router"][0].reshape(DC, P, E).transpose(1, 0, 2)
    sb_, sc_ = np.zeros((DEPTH, P, CA, 2, P), np.float32), np.zeros((DEPTH, P, JT, 2, 32), np.float32)
    for c, (nb, ncc) in enumerate((("s5_b_re", "s5_c_re"), ("s5_b_im", "s5_c_im"))):
        for g in range(G5):
            j, half = g // 2, g % 2
            q = 32 * (j % 4) + S5C * half
            sb_[:, q:q + S5C, j // 4, c, S5P * half:S5P * (half + 1)] = i[nb][:, g].transpose(0, 2, 1)
            sc_[:, S5P * half:S5P * (half + 1), j, c, S5C * half:S5C * (half + 1)] = i[ncc][:, g].transpose(0, 2, 1)
    a["s5_b"], a["s5_c"] = sb_, sc_
    lo = np.empty((DEPTH, P, 2, DB), np.float32)
    lo[:, 0:64, 0], lo[:, 64:, 0], lo[:, :, 1] = i["rw_w_up"], i["rw_a_up"], i["rw_g_up"]
    a["lora_up"] = lo
    return {k: np.ascontiguousarray(v) for k, v in a.items()}


OUTS = {"y": (P, DC, T), "o_shift": (DEPTH, P, CR, 1 + NS), "o_s5": (DEPTH, P, JT, 2, 1 + NS),
        "o_rw": (DEPTH, P, CB, MAXC, N)}


def results(r):
    y = r["y"].transpose(2, 1, 0).reshape(T, D)
    sh = r["o_shift"].transpose(0, 3, 2, 1).reshape(DEPTH, 1 + NS, PRW)
    s5 = r["o_s5"].transpose(3, 0, 4, 2, 1).reshape(2, DEPTH, 1 + NS, G5, S5P)
    rw = r["o_rw"].reshape(DEPTH, 2, N, CB, MAXC, N).transpose(0, 4, 3, 1, 5, 2).reshape(DEPTH, MAXC, H, N, N)
    c = np.ascontiguousarray
    return (c(y[None, N_META:TP]), c(y[TP:, None]), c(s5[0, :, :1]), c(s5[1, :, :1]), c(rw[:, :1]), c(sh[:, :1]),
            c(s5[0, :, 1:]), c(s5[1, :, 1:]), c(rw[:, 1:]), c(sh[:, 1:]))


def kernel(**inputs):
    import concourse.bacc as bacc
    from concourse.bass_utils import run_bass_kernel_spmd

    nc = bacc.Bacc("TRN2", target_bir_lowering=False, num_devices=1)
    arrays = {f"{k}_dram": v for k, v in layout(inputs).items()}
    a = {k[:-5]: nc.dram_tensor(k, v.shape, F32, kind="ExternalInput").ap() for k, v in arrays.items()}
    for k, shape in OUTS.items():
        a[k] = nc.dram_tensor(f"{k}_dram", shape, F32, kind="ExternalOutput").ap()
    build(nc, a)
    r = run_bass_kernel_spmd(nc, [arrays], core_ids=[0]).results[0]
    return results({k: np.asarray(r[f"{k}_dram"]) for k in OUTS})
```
